# Optimizing a Trainium2 kernel written in Bass

```python
import math
import jax, jax.numpy as jnp
from jax import lax
import numpy as np

D_MODEL = 1024
BATCH = 1
SEQ = 256
DEPTH = 4

N_MIXERS = 3
N_A = (DEPTH + 2) // 3
N_B = (DEPTH + 1) // 3
N_C = DEPTH // 3

CONV_WIDTH = 3

RET_HEADS = 4
RET_DK = D_MODEL // RET_HEADS
RET_DV = 2 * RET_DK
RET_VDIM = RET_HEADS * RET_DV
RET_CHUNK = 128
ROPE_BASE = 10000.0

SGU_HALF = 3 * D_MODEL
SGU_GROUPS = 4
SGU_GD = SGU_HALF // SGU_GROUPS
SGU_CHUNK = 128

N_EXPERTS = 16
N_GROUPS = 4
EXPERTS_PER_GROUP = N_EXPERTS // N_GROUPS
TOP_K = 2
D_EXPERT = D_MODEL // 2

PLE_DIM = 256
ALPHA = (2 * DEPTH) ** 0.25
BETA = (8 * DEPTH) ** -0.25
LN_EPS = 1e-5

kernel_name = "hybrid_conv_retention_sgu_moe_deepnorm"

def _layer_norm(x, g, b):
    xf = x.astype(jnp.float32)
    mu = jnp.mean(xf, axis=-1, keepdims=True)
    xc = xf - mu
    var = jnp.mean(xc * xc, axis=-1, keepdims=True)
    return (xc * lax.rsqrt(var + LN_EPS) * g + b).astype(x.dtype)

def _short_conv_mixer(x, w_in, conv_w, w_out):
    bch = x @ w_in
    b_gate, c_gate, h = jnp.split(bch, 3, axis=-1)
    z = c_gate * h
    zc = lax.conv_general_dilated(
        z, conv_w[:, None, :].astype(z.dtype),
        window_strides=(1,), padding=[(CONV_WIDTH - 1, 0)],
        dimension_numbers=("NWC", "WIO", "NWC"),
        feature_group_count=D_MODEL)
    return (b_gate * zc) @ w_out

def _rotary(t, cos, sin):
    t1, t2 = jnp.split(t, 2, axis=-1)
    return jnp.concatenate([t1 * cos - t2 * sin, t2 * cos + t1 * sin], axis=-1)

def _retention_mixer(x, w_in, w_out):
    bsz, seq, _ = x.shape
    n_chunks = seq // RET_CHUNK
    proj = x @ w_in
    q, k, v, g = jnp.split(proj, [D_MODEL, 2 * D_MODEL, 2 * D_MODEL + RET_VDIM], axis=-1)
    q = q.astype(jnp.float32).reshape(bsz, seq, RET_HEADS, RET_DK)
    k = k.astype(jnp.float32).reshape(bsz, seq, RET_HEADS, RET_DK) * (RET_DK ** -0.5)
    v = v.astype(jnp.float32).reshape(bsz, seq, RET_HEADS, RET_DV)

    pos = jnp.arange(seq, dtype=jnp.float32)
    inv_freq = 1.0 / (ROPE_BASE ** jnp.linspace(0.0, 1.0, RET_DK // 2, dtype=jnp.float32))
    ang = pos[:, None] * inv_freq[None, :]
    cos = jnp.cos(ang)[:, None, :]
    sin = jnp.sin(ang)[:, None, :]
    q = _rotary(q, cos, sin)
    k = _rotary(k, cos, sin)

    def to_chunks(t):
        return t.reshape(bsz, n_chunks, RET_CHUNK, RET_HEADS, -1).transpose(1, 0, 3, 2, 4)
    qc, kc, vc = to_chunks(q), to_chunks(k), to_chunks(v)

    log_gamma = jnp.log(1.0 - 2.0 ** (-5.0 - jnp.arange(RET_HEADS, dtype=jnp.float32)))
    idx = jnp.arange(RET_CHUNK, dtype=jnp.float32)
    diff = idx[:, None] - idx[None, :]
    decay_mask = jnp.where(diff >= 0,
                           jnp.exp(log_gamma[:, None, None] * jnp.maximum(diff, 0.0)), 0.0)
    q_decay = jnp.exp(log_gamma[:, None] * (idx[None, :] + 1.0))
    k_decay = jnp.exp(log_gamma[:, None] * (RET_CHUNK - 1.0 - idx[None, :]))
    chunk_decay = jnp.exp(log_gamma * RET_CHUNK)

    scores = jnp.einsum("nbhcd,nbhsd->nbhcs", qc, kc) * decay_mask[None, None]
    inner = jnp.einsum("nbhcs,nbhse->nbhce", scores, vc)

    def step(state, inp):
        q_i, k_i, v_i = inp
        cross = jnp.einsum("bhcd,bhde->bhce", q_i, state) * q_decay[None, :, :, None]
        state = state * chunk_decay[None, :, None, None] + jnp.einsum(
            "bhcd,bhce->bhde", k_i * k_decay[None, :, :, None], v_i)
        return state, cross
    state0 = jnp.zeros((bsz, RET_HEADS, RET_DK, RET_DV), jnp.float32)
    _, cross = lax.scan(step, state0, (qc, kc, vc))

    o = (inner + cross).transpose(1, 0, 3, 2, 4).reshape(bsz, seq, RET_HEADS, RET_DV)
    mu = jnp.mean(o, axis=-1, keepdims=True)
    oc = o - mu
    o = oc * lax.rsqrt(jnp.mean(oc * oc, axis=-1, keepdims=True) + LN_EPS)
    o = o.reshape(bsz, seq, RET_VDIM).astype(x.dtype)
    return (jax.nn.silu(g) * o) @ w_out

def _sgu_mixer(x, w_in, ln_g, ln_b, w_s, b_s, w_out):
    bsz, seq, _ = x.shape
    n_chunks = seq // SGU_CHUNK
    z = jax.nn.gelu(x @ w_in, approximate=False)
    u, v = jnp.split(z, 2, axis=-1)
    v = _layer_norm(v, ln_g, ln_b).reshape(bsz, n_chunks, SGU_CHUNK, SGU_GROUPS, SGU_GD)
    causal = jnp.tril(jnp.ones((SGU_CHUNK, SGU_CHUNK), w_s.dtype))
    ws = w_s * causal[None]
    vs = jnp.einsum("gts,bnsgd->bntgd", ws, v) + b_s.T[None, None, :, :, None]
    return (u * vs.reshape(bsz, seq, SGU_HALF)) @ w_out

def _moe(h, router_w, router_b, w_gate, w_up, w_down):
    bsz, seq, d = h.shape
    hf = h.reshape(bsz * seq, d)
    scores = jax.nn.sigmoid((hf @ router_w).astype(jnp.float32))
    sel = scores + router_b.astype(jnp.float32)
    grp = lax.top_k(sel.reshape(-1, N_GROUPS, EXPERTS_PER_GROUP), 2)[0].sum(-1)
    g_idx = jnp.argmax(grp, axis=-1)
    in_group = (jnp.arange(N_EXPERTS) // EXPERTS_PER_GROUP)[None, :] == g_idx[:, None]
    _, e_idx = lax.top_k(jnp.where(in_group, sel, -jnp.inf), TOP_K)
    w = jnp.take_along_axis(scores, e_idx, axis=-1)
    w = w / jnp.sum(w, axis=-1, keepdims=True)
    combine = jnp.sum(jax.nn.one_hot(e_idx, N_EXPERTS, dtype=jnp.float32) * w[..., None],
                      axis=1).astype(h.dtype)
    y = jnp.zeros_like(hf)
    for e in range(N_EXPERTS):
        he = jax.nn.silu(hf @ w_gate[e]) * (hf @ w_up[e])
        y = y + combine[:, e:e + 1] * (he @ w_down[e])
    return y.reshape(bsz, seq, d)

def setup_inputs(seed: int = 0) -> dict:
    key = jax.random.key(seed)
    ks = jax.random.split(key, 24)

    def nrm(k, shape, scale):
        return jax.random.normal(k, shape, jnp.float32) * scale

    return {
        "x": nrm(ks[0], (BATCH, SEQ, D_MODEL), 1.0),
        "p": nrm(ks[1], (DEPTH, BATCH, SEQ, PLE_DIM), 1.0),
        "a_w_in": nrm(ks[2], (N_A, D_MODEL, 3 * D_MODEL), D_MODEL ** -0.5),
        "a_conv_w": nrm(ks[3], (N_A, CONV_WIDTH, D_MODEL), CONV_WIDTH ** -0.5),
        "a_w_out": nrm(ks[4], (N_A, D_MODEL, D_MODEL), D_MODEL ** -0.5 * BETA),
        "b_w_in": nrm(ks[5], (N_B, D_MODEL, 2 * D_MODEL + 2 * RET_VDIM), D_MODEL ** -0.5),
        "b_w_out": nrm(ks[6], (N_B, RET_VDIM, D_MODEL), RET_VDIM ** -0.5 * BETA),
        "c_w_in": nrm(ks[7], (N_C, D_MODEL, 2 * SGU_HALF), D_MODEL ** -0.5),
        "c_ln_g": 1.0 + nrm(ks[8], (N_C, SGU_HALF), 0.02),
        "c_ln_b": nrm(ks[9], (N_C, SGU_HALF), 0.02),
        "c_w_s": nrm(ks[10], (N_C, SGU_GROUPS, SGU_CHUNK, SGU_CHUNK), 0.5 * SGU_CHUNK ** -0.5),
        "c_b_s": 1.0 + nrm(ks[11], (N_C, SGU_GROUPS, SGU_CHUNK), 0.1),
        "c_w_out": nrm(ks[12], (N_C, SGU_HALF, D_MODEL), SGU_HALF ** -0.5 * BETA),
        "router_w": nrm(ks[13], (D_MODEL, N_EXPERTS), D_MODEL ** -0.5),
        "router_b": nrm(ks[14], (N_EXPERTS,), 0.01),
        "moe_w_gate": nrm(ks[15], (DEPTH, N_EXPERTS, D_MODEL, D_EXPERT), D_MODEL ** -0.5),
        "moe_w_up": nrm(ks[16], (DEPTH, N_EXPERTS, D_MODEL, D_EXPERT), D_MODEL ** -0.5),
        "moe_w_down": nrm(ks[17], (DEPTH, N_EXPERTS, D_EXPERT, D_MODEL), D_EXPERT ** -0.5 * BETA),
        "ln_g": 1.0 + nrm(ks[18], (DEPTH, 2, D_MODEL), 0.02),
        "ln_b": nrm(ks[19], (DEPTH, 2, D_MODEL), 0.02),
        "ple_w_proj": nrm(ks[20], (DEPTH, PLE_DIM, D_MODEL), PLE_DIM ** -0.5),
        "ple_w_gate": nrm(ks[21], (DEPTH, D_MODEL, D_MODEL), D_MODEL ** -0.5),
        "ple_b_gate": nrm(ks[22], (DEPTH, D_MODEL), 0.02),
    }

def reference(x, p, a_w_in, a_conv_w, a_w_out, b_w_in, b_w_out, c_w_in, c_ln_g, c_ln_b,
              c_w_s, c_b_s, c_w_out, router_w, router_b, moe_w_gate, moe_w_up, moe_w_down,
              ln_g, ln_b, ple_w_proj, ple_w_gate, ple_b_gate):
    for i in range(DEPTH):
        mixer, slot = i % N_MIXERS, i // N_MIXERS
        if mixer == 0:
            mix = _short_conv_mixer(x, a_w_in[slot], a_conv_w[slot], a_w_out[slot])
        elif mixer == 1:
            mix = _retention_mixer(x, b_w_in[slot], b_w_out[slot])
        else:
            mix = _sgu_mixer(x, c_w_in[slot], c_ln_g[slot], c_ln_b[slot],
                             c_w_s[slot], c_b_s[slot], c_w_out[slot])
        x = _layer_norm(ALPHA * x + mix, ln_g[i, 0], ln_b[i, 0])
        ffn = _moe(x, router_w, router_b, moe_w_gate[i], moe_w_up[i], moe_w_down[i])
        x = _layer_norm(ALPHA * x + ffn, ln_g[i, 1], ln_b[i, 1])
        emb = p[i] @ ple_w_proj[i]
        gate = jax.nn.sigmoid(x @ ple_w_gate[i] + ple_b_gate[i])
        x = x + gate * emb
    return x


_drawn_inputs = setup_inputs


def setup_inputs(seed=0):
    import zlib

    import numpy as np

    out = dict(_drawn_inputs(seed))
    spreads = {}
    factors = {'c_ln_g': 26.394, 'c_ln_b': 22.346, 'ple_b_gate': 3.499}
    for name, (base, spread) in spreads.items():
        noise = np.random.default_rng([zlib.crc32(name.encode()), seed]).standard_normal(out[name].shape)
        drawn = base * np.exp(spread * noise) if base else spread * noise
        out[name] = __import__('jax').numpy.asarray(drawn.astype(out[name].dtype))
    for name, factor in factors.items():
        out[name] = (out[name] * factor).astype(out[name].dtype)
    return out
```

```python
import numpy as np
import concourse.bass as bass
from concourse import mybir
from contextlib import ExitStack

P = 128
D = 1024
SEQ = 256
T = SEQ // P
DEPTH = 4
KD = D // P
NB = 512
HEADS, DK, DV = 4, 256, 512
VD = HEADS * DV
SGU, SGROUPS = 3 * D, 4
SGD = SGU // SGROUPS
SVB = SGD // 2
NE, NG, EPG = 16, 4, 4
FE = D // 2
PLE = 256
NBLK = NG + 1
ALPHA = float((2 * DEPTH) ** 0.25)
LN_EPS = 1e-5
RING = 8
SLOT = 4 * NB
W_SLOTS_EXPERT = 6
W_SLOTS_GROUP = EPG * W_SLOTS_EXPERT
MIXER_SLOTS = {0: (2 * 3 * D // NB, 4), 1: (2 * (2 * D + 2 * VD) // NB, 2 * VD // NB),
               2: (2 * 2 * SGU // NB, 2 * SGU // NB)}


def slot_starts():
    at, out = 0, []
    for layer in range(DEPTH):
        mixer = at
        at += sum(MIXER_SLOTS[layer % 3])
        proj, experts = at, at + 1
        at = experts + NG * W_SLOTS_GROUP
        out.append((mixer, proj, experts, at))
        at += 4
    return out


def shape_constants():
    f = np.float32
    pos = np.arange(SEQ, dtype=f)
    inv = (1.0 / (f(10000.0) ** np.linspace(0.0, 1.0, DK // 2, dtype=f))).astype(f)
    ang = pos[:, None] * inv[None, :]
    rot = np.stack([np.cos(ang), np.sin(ang)], 1).astype(f)
    rot = rot.reshape(T, P, 2, DK // 2).transpose(1, 0, 2, 3).copy()
    lg = np.log(1.0 - 2.0 ** (-5.0 - np.arange(HEADS)))[:, None, None]
    s, c = np.arange(P)[:, None], np.arange(P)[None, :]
    diag = np.where(c >= s, np.exp(lg * np.maximum(c - s, 0)), 0.0)
    cross = np.exp(lg * (P + c - s))
    decay = (np.concatenate([diag, cross, diag], 2) * DK ** -0.5).astype(f).transpose(1, 0, 2).copy()
    lower = (np.arange(4)[None, :] < np.arange(4)[:, None]).astype(f).reshape(1, 16)
    small = np.concatenate([lower, P * np.arange(4, dtype=f)[None], 1 + np.arange(4, dtype=f)[None]], 1)
    return {
        "identity": np.eye(P, dtype=f),
        "before": (s < c).astype(f),
        "causal": (c <= s).astype(f),
        "slot_number": np.broadcast_to(np.arange(NBLK * P, dtype=f), (P, NBLK * P)).copy(),
        "rotary": rot,
        "decay": decay,
        "small": np.broadcast_to(small, (P, 24)).copy(),
    }


def build(nc, A, out):
    F = mybir.dt.float32
    I32 = mybir.dt.int32
    ALU = mybir.AluOpType
    ACT = mybir.ActivationFunctionType
    X = mybir.AxisListType.X
    starts = slot_starts()

    ctx = ExitStack()
    with ctx:
        def sb(name, *shape, dt=F):
            return ctx.enter_context(nc.sbuf_tensor(name, [P, *shape], dt))

        def sem(name):
            return ctx.enter_context(nc.semaphore(name))

        ring = sb("ring", RING, SLOT)
        x = sb("x", T, D)
        xT = sb("xT", KD, SEQ)
        emb = sb("emb", T, D)
        tmp = sb("tmp", T, D)
        ln_par = sb("ln_par", 2, D)
        bgate = sb("bgate", D)
        p_in = sb("p_in", T, PLE)
        pT = sb("pT", 2, SEQ)
        ident = sb("ident", P)
        before = sb("before", P)
        causal = sb("causal", P)
        ones = sb("ones", P)
        slot_no = sb("slot_no", NBLK * P)
        rot = sb("rot", T, 2, DK // 2)
        decay = sb("decay", HEADS, 3 * P)
        small = sb("small", 24)
        rw = sb("rw", KD, NE)
        rb = sb("rb", NE)
        conv_w = sb("conv_w", 2, 3, KD)
        sgu_b = sb("sgu_b", SGROUPS)
        stats = sb("stats", T, 6, 6)
        nstat = sb("nstat", 8, 6)
        nmv = sb("nmv", 2)
        nvar, nsq, nrstd, nbits = sb("nvar", 1), sb("nsq", 1), sb("nrstd", 1), sb("nbits", 1, dt=I32)
        score = sb("score", T, NE)
        sel = sb("sel", T, NE)
        cmp1 = sb("cmp1", T * NG, 4, 4)
        cmp2 = sb("cmp2", T * NG, 4, 4)
        cnt = sb("cnt", T * NG, 4)
        top2 = sb("top2", T * NG, 4)
        gscore = sb("gscore", T, NG)
        gcnt = sb("gcnt", T, NG)
        ghot = sb("ghot", T, NG)
        cw = sb("cw", T, NG, 4)
        den = sb("den", T)
        cwn = sb("cwn", T, NG, 4)
        comb = sb("comb", T, 4)
        gpos = sb("gpos", T, NG)
        pos = sb("pos", T)
        gbase = sb("gbase", T)
        over = sb("over", T)
        shift = sb("shift", T)
        key = sb("key", T)
        big = sb("big", 4)
        bigmax = sb("bigmax", 1)
        flag = sb("flag", 1, dt=I32)
        cg = sb("cg", 4 * NBLK)
        work = sb("work", 18432)
        psum = ctx.enter_context(nc.psum_tensor("psum", [P, 8, NB], F))

        def view(start, size, pattern, **dims):
            return work[:, start:start + size].rearrange(pattern, **dims)

        bch = view(0, T * 3 * D, "p (t n) -> p t n", t=T)
        zT = view(6144, KD * (SEQ + 2), "p (j n) -> p j n", j=KD)
        bT = view(8208, KD * SEQ, "p (j n) -> p j n", j=KD)
        qk = view(0, T * 2 * D, "p (t n) -> p t n", t=T)
        rv = view(4096, T * VD, "p (t n) -> p t n", t=T)
        rg = view(8192, T * VD, "p (t n) -> p t n", t=T)
        qkT = view(12288, 2 * KD * SEQ, "p (a j n) -> p a j n", a=2, j=KD)
        sT = view(16384, HEADS * 3 * P, "p (h n) -> p h n", h=HEADS)
        oT = view(0, VD // P * SEQ, "p (j n) -> p j n", j=VD // P)
        su = view(0, T * SGU, "p (t n) -> p t n", t=T)
        sv = view(6144, T * SGU, "p (t n) -> p t n", t=T)
        uvT = view(12288, SGU // P * SEQ, "p (j n) -> p j n", j=SGU // P)
        c_ln = view(12288, 2 * SGU, "p (a n) -> p a n", a=2)
        sgu_w = tmp[:, 0, 0:512].rearrange("p (g s) -> p g s", g=SGROUPS)
        sgu_wT = tmp[:, 0, 512:1024].rearrange("p (g s) -> p g s", g=SGROUPS)
        pick = view(0, T * NBLK * P, "p (t n) -> p t n", t=T)
        place = view(1280, NBLK * SEQ, "p (b n) -> p b n", b=NBLK)
        xg = view(2560, KD * P, "p (j n) -> p j n", j=KD)
        y = view(3584, NBLK * D, "p (b n) -> p b n", b=NBLK)
        sg = view(8704, 2 * FE, "p (a n) -> p a n", a=2)
        hid = view(9728, 2 * FE, "p (a n) -> p a n", a=2)
        hT = view(10752, 2 * FE, "p (a j n) -> p a j n", a=2, j=4)

        s_const = sem("constants_loaded")
        s_x = sem("x_loaded")
        s_ones = sem("ones_set")
        slot_full = [sem(f"slot_full{i}") for i in range(RING)]
        weights_used = sem("weights_used")
        xt_in_psum, xt_ready = sem("xt_in_psum"), sem("xt_ready")
        x_tile_ready = sem("x_tile_ready")
        mix_done = sem("mix_done")
        dve_step = sem("dve_step")
        p_loaded, lnp_loaded, bg_loaded = sem("p_loaded"), sem("lnp_loaded"), sem("bg_loaded")
        pt_in_psum, pt_ready = sem("pt_in_psum"), sem("pt_ready")
        logits_done, score_ready = sem("logits_done"), sem("score_ready")
        emb_in_psum, emb_ready = sem("emb_in_psum"), sem("emb_ready")
        ghot_ready, rank_in_psum = sem("ghot_ready"), sem("rank_in_psum")
        flag_ready, pick_ready = sem("flag_ready"), sem("pick_ready")
        xg_in_psum, xg_ready = sem("xg_in_psum"), sem("xg_ready")
        cg_in_psum, cg_ready = sem("cg_in_psum"), sem("cg_ready")
        place_in_psum, y_banks_free = sem("place_in_psum"), sem("y_banks_free")
        sig_ready, silu_ready, h_ready = sem("sig_ready"), sem("silu_ready"), sem("h_ready")
        ht_in_psum, ht_ready = sem("ht_in_psum"), sem("ht_ready")
        ffn_done, ffn_added = sem("ffn_done"), sem("ffn_added")
        ple_done, ple_arg, ple_sig = sem("ple_done"), sem("ple_arg"), sem("ple_sig")
        proj_in_psum = [sem(f"proj_in_psum{i}") for i in range(DEPTH)]
        proj_ready = [sem(f"proj_ready{i}") for i in range(DEPTH)]
        z_ready = [sem(f"z_ready{i}") for i in range(DEPTH)]
        mt_in_psum = [sem(f"mixT_in_psum{i}") for i in range(DEPTH)]
        mt_ready = [sem(f"mixT_ready{i}") for i in range(DEPTH)]
        conv_ready = [sem(f"conv_ready{i}") for i in range(DEPTH)]
        g_ready, qk_ready = sem("g_ready"), sem("qk_ready")
        score_in_psum, sT_ready = sem("scores_in_psum"), sem("sT_ready")
        o_in_psum, o_read, o_ready = sem("o_in_psum"), sem("o_read"), sem("o_ready")
        oT_in_psum, oT_ready = sem("oT_in_psum"), sem("oT_ready")
        c_loaded, sw_masked, sw_in_psum, sw_ready = (sem("c_loaded"), sem("sw_masked"),
                                                     sem("sw_in_psum"), sem("sw_ready"))
        v_ready, vs_in_psum, uv_ready = sem("v_ready"), sem("vs_in_psum"), sem("uv_ready")
        s_out = sem("out_stored")
        OV = ["full", "used", "gate", "up", "sig", "silu", "h", "ht_in_psum", "ht", "y_saved", "ffn"]
        ov = [{n: sem(f"over_{n}{i}") for n in OV} for i in range(DEPTH)]
        N_CONST = 12

        block = ctx.enter_context(nc.Block())

        def wait_block(eng, L, b, t, tile0):
            if t == 0:
                eng.wait_ge(tile0, b + 1)
            else:
                eng.wait_ge(weights_used, starts[L][0] + 2 * (b + 1))

        def wait_rows(eng, L, t, tile0, count, end):
            if t == 0:
                eng.wait_ge(tile0, count)
            else:
                eng.wait_ge(weights_used, end)

        def expert_slots(L, i):
            return starts[L][2] + 2 * (i + 1)

        GATE_AT, UP_AT, LAST_AT = (0, 2, 5, 8), (1, 3, 6, 9), 11

        @block.sync
        def _(sp):
            def load(n, src):
                if n >= RING:
                    sp.wait_ge(weights_used, n - RING + 1)
                sp.dma_start(ring[:, n % RING, :], src).then_inc(slot_full[n % RING], 16)

            def load_columns(n, w, order):
                v = w.rearrange("(p j) n -> p j n", j=KD)
                for b in order:
                    for half in range(2):
                        if n >= RING:
                            sp.wait_ge(weights_used, n - RING + 1)
                        sp.dma_start(ring[:, n % RING, :].rearrange("p (j n) -> p j n", j=4),
                                     v[:, 4 * half:4 * half + 4, b * NB:(b + 1) * NB]
                                     ).then_inc(slot_full[n % RING], 16)
                        n += 1
                return n

            sp.dma_start(x[:, :, :], A["x"][0].rearrange("(t p) d -> p t d", p=P)).then_inc(s_x, 16)
            for L in range(DEPTH):
                n, n_proj, n_exp, n_gate = starts[L]
                if L % 3 == 0:
                    n = load_columns(n, A["a_w_in"][L // 3], range(6))
                    v = A["a_w_out"][L // 3].rearrange("(p j) n -> p (j n)", j=KD)
                    for i in range(4):
                        load(n + i, v[:, i * SLOT:(i + 1) * SLOT])
                elif L % 3 == 1:
                    n = load_columns(n, A["b_w_in"][L // 3], range(12))
                    v = A["b_w_out"][L // 3].rearrange("(s p j) n -> s p (j n)", p=P, j=4)
                    for i in range(2 * VD // NB):
                        load(n + i, v[i // 2, :, i % 2 * SLOT:(i % 2 + 1) * SLOT])
                else:
                    n = load_columns(n, A["c_w_in"][L // 3], [*range(6, 12), *range(6)])
                    v = A["c_w_out"][L // 3].rearrange("(s p j) n -> s p (j n)", p=P, j=4)
                    for i in range(2 * SGU // NB):
                        load(n + i, v[i // 2, :, i % 2 * SLOT:(i % 2 + 1) * SLOT])
                load(n_proj, A["ple_w_proj"][L].rearrange("(p j) n -> p (j n)", j=2))
                wg = A["moe_w_gate"][L].rearrange("(g e) (p j) n -> g e p (j n)", g=NG, j=KD)
                wu = A["moe_w_up"][L].rearrange("(g e) (p j) n -> g e p (j n)", g=NG, j=KD)
                wd = A["moe_w_down"][L].rearrange("(g e) (p j) n -> g e p (j n)", g=NG, j=4)
                order = [(wg, 0), (wu, 0), (wg, 1), (wu, 1), (wd, 0), (wg, 2), (wu, 2), (wd, 1),
                         (wg, 3), (wu, 3), (wd, 2), (wd, 3)]
                with sp.Fori(0, NG) as g:
                    for i, (w, e) in enumerate(order):
                        for half in range(2):
                            k = n_exp + 2 * i + half
                            sp.wait_ge(weights_used, k - RING + 1 + W_SLOTS_GROUP * g)
                            sp.dma_start(ring[:, k % RING, :], w[g, e, :, half * SLOT:(half + 1) * SLOT]
                                         ).then_inc(slot_full[k % RING], 16)
                sp.wait_ge(flag_ready, L + 1)
                crowded = sp.value_load(flag[0:1, 0:1], min_val=0, max_val=NG)
                with sp.If(crowded > 0):
                    group = sp.value_load(flag[0:1, 0:1], min_val=1, max_val=NG)
                    sp.wait_ge(weights_used, n_gate)
                    for e in range(EPG):
                        if e:
                            sp.wait_ge(ov[L]["used"], W_SLOTS_EXPERT * e)
                        for i, w in enumerate((wg, wu, wd)):
                            for half in range(2):
                                sp.dma_start(ring[:, 2 * i + half, :],
                                             w[group - 1, e, :, half * SLOT:(half + 1) * SLOT]
                                             ).then_inc(ov[L]["full"], 16)
                    sp.wait_ge(ov[L]["used"], W_SLOTS_EXPERT * EPG)
                v = A["ple_w_gate"][L].rearrange("(p j) n -> p (j n)", j=KD)
                for i in range(4):
                    load(n_gate + i, v[:, i * SLOT:(i + 1) * SLOT])
            for t in range(T):
                sp.wait_ge(x_tile_ready, 2 * (3 * DEPTH - 1) + t + 1)
                sp.dma_start(out[0, t * P:(t + 1) * P, :], x[:, t, :]).then_inc(s_out, 16)
            sp.wait_ge(s_out, 16 * T)

        @block.gpsimd
        def _(pool):
            nc.gpsimd.memset(ones[:, :], 1.0).then_inc(s_ones, 1)
            loads = [(ident[:, :], A["identity"]), (before[:, :], A["before"]),
                     (causal[:, :], A["causal"]), (slot_no[:, :], A["slot_number"]),
                     (rot[:, :, :, :], A["rotary"]), (decay[:, :, :], A["decay"]),
                     (small[:, :], A["small"]),
                     (rw[:, :, :], A["router_w"].rearrange("(p j) e -> p j e", j=KD)),
                     (rb[:, :], A["router_b"].partition_broadcast(P)),
                     (sgu_b[:, :], A["c_b_s"][0].rearrange("g t -> t g"))]
            loads += [(conv_w[:, i, :, :], A["a_conv_w"][i].rearrange("w (p j) -> p w j", j=KD))
                      for i in range(2)]
            assert len(loads) == N_CONST
            for dst, src in loads:
                pool.dma_start(dst, src, allow_slow_non_contiguous=True).then_inc(s_const, 16)
            def load_norm(L, i):
                pool.dma_start(ln_par[:, 0, :], A["ln_g"][L, i].partition_broadcast(P)).then_inc(lnp_loaded, 16)
                pool.dma_start(ln_par[:, 1, :], A["ln_b"][L, i].partition_broadcast(P)).then_inc(lnp_loaded, 16)

            load_norm(0, 0)
            for L in range(DEPTH):
                if L:
                    pool.wait_ge(x_tile_ready, 6 * L)
                pool.dma_start(p_in[:, :, :], A["p"][L, 0].rearrange("(t p) d -> p t d", p=P)
                               ).then_inc(p_loaded, 16)
                pool.dma_start(bgate[:, :], A["ple_b_gate"][L].partition_broadcast(P)).then_inc(bg_loaded, 16)
                if L % 3 == 2:
                    for a, name in enumerate(("c_ln_g", "c_ln_b")):
                        pool.dma_start(c_ln[:, a, :], A[name][0].partition_broadcast(P)).then_inc(c_loaded, 16)
                    pool.dma_start(sgu_w, A["c_w_s"][0].rearrange("g t s -> t g s")).then_inc(c_loaded, 16)
                pool.wait_ge(x_tile_ready, 6 * L + 2)
                load_norm(L, 1)
                if L + 1 < DEPTH:
                    pool.wait_ge(x_tile_ready, 6 * L + 4)
                    load_norm(L + 1, 0)

        @block.tensor
        def _(pe):
            mm = nc.tensor.matmul

            def slot(n):
                pe.wait_ge(slot_full[n % RING], 16 * (n // RING + 1))
                return ring[:, n % RING, :].rearrange("p (j n) -> p j n", j=4)

            def transpose4(bank, chunks):
                for i, c in enumerate(chunks):
                    last = nc.tensor.transpose(psum[:, bank, i * P:(i + 1) * P], c, ident[:, :])
                return last

            def transpose_x(k):
                for t in range(T):
                    if k == 0:
                        pe.wait_ge(s_x, 16)
                    else:
                        pe.wait_ge(x_tile_ready, 2 * (k - 1) + t + 1)
                    v = x[:, t, :].rearrange("p (c j) -> p j c", j=KD)
                    for q in range(2):
                        transpose4(2 * t + q, [v[:, 4 * q + i, :] for i in range(4)]).then_inc(xt_in_psum, 1)
                pe.wait_ge(xt_ready, 4 * (k + 1))

            def project(n, jobs_of_block, wait_banks, done):
                for b in range(jobs_of_block):
                    for half in range(2):
                        w = slot(n)
                        for t in range(T):
                            job = 2 * b + t
                            if half == 0 and job >= 8:
                                wait_banks(job)
                            for i in range(4):
                                last = mm(psum[:, job % 8, :], xT[:, 4 * half + i, t * P:(t + 1) * P],
                                          w[:, i, :], start=half == 0 and i == 0, stop=half == 1 and i == 3)
                            if half == 1 and t == 0:
                                last.then_inc(done, 1)
                        last.then_inc(weights_used, 1)
                        n += 1
                return n

            def rows_out(n, count, lhs, bank0, done):
                for s in range(count):
                    w = slot(n + s)
                    for t in range(T):
                        for i in range(2):
                            for c in range(2):
                                last = mm(psum[:, bank0 + 2 * t + c, :], lhs[:, 2 * s + i, t * P:(t + 1) * P],
                                          w[:, 2 * i + c, :], start=s == 0 and i == 0,
                                          stop=s == count - 1 and i == 1)
                        if s == count - 1 and t == 0:
                            last.then_inc(done, 1)
                    last.then_inc(weights_used, 1)

            def conv_mixer(L, n):
                def banks(job):
                    pe.wait_ge(proj_ready[L], job - 7)
                n = project(n, 6, banks, proj_in_psum[L])
                pe.wait_ge(proj_ready[L], 12)
                for src in range(2):
                    for t in range(T):
                        if src:
                            pe.wait_ge(z_ready[L], t + 1)
                        v = bch[:, t, src * D:(src + 1) * D].rearrange("p (c j) -> p j c", j=KD)
                        for q in range(2):
                            transpose4(4 * src + 2 * t + q, [v[:, 4 * q + i, :] for i in range(4)]
                                       ).then_inc(mt_in_psum[L], 1)
                pe.wait_ge(mt_ready[L], 8)
                pe.wait_ge(conv_ready[L], KD)
                rows_out(n, 4, bT, 4, mix_done)

            def retention_mixer(L, n):
                def banks(job):
                    pe.wait_ge(proj_ready[L], job - 7)
                n = project(n, 12, banks, proj_in_psum[L])
                pe.wait_ge(g_ready, 8)
                for src in range(2):
                    for t in range(T):
                        pe.wait_ge(qk_ready, t + 1)
                        for q in range(2):
                            c0 = src * D + q * NB
                            transpose4(4 * src + 2 * t + q, [qk[:, t, c0 + i * P:c0 + (i + 1) * P] for i in range(4)]
                                       ).then_inc(mt_in_psum[L], 1)
                pe.wait_ge(mt_ready[L], 8)
                for h in range(HEADS):
                    for half in range(2):
                        mm(psum[:, h, 0:2 * P], qkT[:, 1, 2 * h + half, 0:P], qkT[:, 0, 2 * h + half, 0:2 * P],
                           start=half == 0, stop=half == 1)
                    for half in range(2):
                        last = mm(psum[:, h, 2 * P:3 * P], qkT[:, 1, 2 * h + half, P:2 * P],
                                  qkT[:, 0, 2 * h + half, P:2 * P], start=half == 0, stop=half == 1)
                    last.then_inc(score_in_psum, 1)

                def attend(k):
                    h, c = divmod(k, 2)
                    pe.wait_ge(sT_ready, h + 1)
                    if k >= 4:
                        pe.wait_ge(o_read, k - 3)
                    for s in range(c + 1):
                        last = mm(psum[:, 4 + k % 4, :], sT[:, h, (c + s) * P:(c + s + 1) * P],
                                  rv[:, s, h * DV:(h + 1) * DV], start=s == 0, stop=s == c)
                    last.then_inc(o_in_psum, 1)

                def turn(k):
                    h, c = divmod(k, 2)
                    pe.wait_ge(o_ready, k + 1)
                    if k == 0:
                        pe.wait_ge(sT_ready, HEADS)
                    if k >= 4:
                        pe.wait_ge(oT_ready, k - 3)
                    v = rg[:, c, h * DV:(h + 1) * DV].rearrange("p (c j) -> p j c", j=4)
                    transpose4(k % 4, [v[:, i, :] for i in range(4)]).then_inc(oT_in_psum, 1)

                for k in range(8):
                    attend(k)
                    if k >= 3:
                        turn(k - 3)
                for k in range(5, 8):
                    turn(k)
                pe.wait_ge(oT_ready, 8)
                rows_out(n, 8, oT, 4, mix_done)

            def sgu_mixer(L, n):
                pe.wait_ge(sw_masked, 1)
                transpose4(7, [sgu_w[:, g, :] for g in range(SGROUPS)]).then_inc(sw_in_psum, 1)
                pe.wait_ge(sw_ready, 1)

                def banks(job):
                    pe.wait_ge(proj_ready[L], job - 7)
                n = project(n, 12, banks, proj_in_psum[L])
                pe.wait_ge(proj_ready[L], 24)
                for k in range(16):
                    b, c = divmod(k, 2)
                    pe.wait_ge(v_ready, c + 1)
                    if k >= 4:
                        pe.wait_ge(uv_ready, k - 3)
                    mm(psum[:, k % 4, 0:SVB], sgu_wT[:, b // 2, :], sv[:, c, b * SVB:(b + 1) * SVB],
                       start=True, stop=True).then_inc(vs_in_psum, 1)
                for k in range(12):
                    s, t = divmod(k, 2)
                    pe.wait_ge(uv_ready, 16)
                    if k >= 4:
                        pe.wait_ge(mt_ready[L], k - 3)
                    v = su[:, t, s * NB:(s + 1) * NB].rearrange("p (c j) -> p j c", j=4)
                    transpose4(4 + k % 4, [v[:, i, :] for i in range(4)]).then_inc(mt_in_psum[L], 1)
                pe.wait_ge(mt_ready[L], 12)
                rows_out(n, 12, uvT, 4, mix_done)

            def route(L):
                for t in range(T):
                    for j in range(KD):
                        last = mm(psum[:, 0, t * NE:(t + 1) * NE], xT[:, j, t * P:(t + 1) * P], rw[:, j, :],
                                  start=j == 0, stop=j == KD - 1)
                last.then_inc(logits_done, 1)
                pe.wait_ge(p_loaded, 16 * (L + 1))
                for t in range(T):
                    v = p_in[:, t, :].rearrange("p (c j) -> p j c", j=2)
                    for j in range(2):
                        last = nc.tensor.transpose(psum[:, 1, j * SEQ + t * P:j * SEQ + (t + 1) * P],
                                                   v[:, j, :], ident[:, :])
                last.then_inc(pt_in_psum, 1)
                pe.wait_ge(pt_ready, L + 1)
                rows_out(starts[L][1], 1, pT, 4, emb_in_psum)
                pe.wait_ge(ghot_ready, L + 1)
                mm(psum[:, 2, 0:4], before[:, :], ghot[:, 0, :], start=True, stop=True)
                mm(psum[:, 2, 4:8], ones[:, :], ghot[:, 0, :], start=True, stop=False)
                mm(psum[:, 2, 4:8], before[:, :], ghot[:, 1, :], start=False, stop=True)
                mm(psum[:, 2, 8:12], ones[:, :], ghot[:, 0, :], start=True, stop=False)
                mm(psum[:, 2, 8:12], ones[:, :], ghot[:, 1, :], start=False, stop=True
                   ).then_inc(rank_in_psum, 1)

            def gather(block):
                for q in range(2):
                    for i in range(4):
                        for t in range(T):
                            v = x[:, t, :].rearrange("p (c j) -> p j c", j=KD)
                            last = mm(psum[:, q, i * P:(i + 1) * P], v[:, 4 * q + i, :],
                                      pick[:, t, bass.ts(block, P)], start=t == 0, stop=t == T - 1)
                    last.then_inc(xg_in_psum, 1)

            def wide(bank, w, half):
                for i in range(4):
                    last = mm(psum[:, bank, :], xg[:, 4 * half + i, :], w[:, i, :],
                              start=half == 0 and i == 0, stop=half == 1 and i == 3)
                return last

            def turn_hidden(e):
                v = hid[:, e % 2, :].rearrange("p (c j) -> p j c", j=4)
                return transpose4(4, [v[:, i, :] for i in range(4)])

            def down(e, w, half):
                for i in range(2):
                    for c in range(2):
                        last = mm(psum[:, 6 + c, :], hT[:, e % 2, 2 * half + i, :], w[:, 2 * i + c, :],
                                  start=e == 0 and half == 0 and i == 0,
                                  stop=e == EPG - 1 and half == 1 and i == 1)
                return last

            def experts(L):
                n0 = starts[L][2]
                pe.wait_ge(pick_ready, L + 1)
                pe.wait_ge(emb_ready, 4 * (L + 1))
                gather(0)
                for b in range(NBLK):
                    for t in range(T):
                        last = mm(psum[:, 3, 4 * b:4 * b + 4], pick[:, t, b * P:(b + 1) * P], comb[:, t, :],
                                  start=t == 0, stop=t == T - 1)
                last.then_inc(cg_in_psum, 1)
                for b in range(NBLK):
                    for t in range(T):
                        c = b % 2 * SEQ + t * P
                        last = nc.tensor.transpose(psum[:, 4 + b // 2, c:c + P], pick[:, t, b * P:(b + 1) * P],
                                                   ident[:, :])
                    if b % 2 or b == NBLK - 1:
                        last.then_inc(place_in_psum, 1)
                pe.wait_ge(y_banks_free, 11 * L + 3)
                pe.wait_ge(cg_ready, L + 1)
                pe.wait_ge(flag_ready, L + 1)

                with pe.Fori(0, NG) as g:
                    def take(i, half):
                        k = n0 + 2 * i + half
                        pe.wait_ge(slot_full[k % RING], 16 * (k // RING + 1) + 16 * (W_SLOTS_GROUP // RING) * g)
                        return ring[:, k % RING, :].rearrange("p (j n) -> p j n", j=4)

                    def pass_wide(i, bank):
                        wide(bank, take(i, 0), 0).then_inc(weights_used, 1)
                        wide(bank, take(i, 1), 1).then_inc(weights_used, 1)

                    def pass_turn(e):
                        pe.wait_ge(h_ready, EPG * (NG * L) + e + 1 + EPG * g)
                        turn_hidden(e).then_inc(ht_in_psum, 1)

                    def pass_down(i, e, half):
                        if half == 0:
                            pe.wait_ge(ht_ready, EPG * NG * L + e + 1 + EPG * g)
                        if e == 0 and half == 0:
                            pe.wait_ge(y_banks_free, 11 * L + 3 + 2 * g)
                        down(e, take(i, half), half).then_inc(weights_used, 1)

                    pe.wait_ge(xg_ready, 10 * L + 2 + 2 * g)
                    pass_wide(0, 0)
                    pass_wide(1, 1)
                    pass_wide(2, 2)
                    pass_turn(0)
                    pass_wide(3, 3)
                    pass_down(4, 0, 0)
                    pass_down(4, 0, 1)
                    pass_wide(5, 0)
                    pass_turn(1)
                    pass_wide(6, 1)
                    pass_down(7, 1, 0)
                    pass_down(7, 1, 1)
                    pass_wide(8, 2)
                    pass_turn(2)
                    pass_wide(9, 3)
                    gather(g + 1)
                    pass_down(10, 2, 0)
                    pass_turn(3)
                    pass_down(10, 2, 1)
                    pass_down(11, 3, 0)
                    pass_down(11, 3, 1)

                pe.wait_ge(xg_ready, 10 * (L + 1))
                pe.wait_ge(y_banks_free, 11 * (L + 1))
                for t in range(T):
                    for b in range(NG):
                        for c in range(2):
                            last = mm(psum[:, 2 * t + c, :], place[:, b, t * P:(t + 1) * P],
                                      y[:, b, c * NB:(c + 1) * NB], start=b == 0, stop=b == NG - 1)
                    last.then_inc(ffn_done, 1)

                crowded = pe.value_load(flag[0:1, 0:1], min_val=0, max_val=NG)
                with pe.If(crowded > 0):
                    o = ov[L]
                    pe.wait_ge(ffn_added, T * (L + 1))
                    for e in range(EPG):
                        pe.wait_ge(o["full"], 16 * W_SLOTS_EXPERT * (e + 1))
                        w = [ring[:, i, :].rearrange("p (j n) -> p j n", j=4) for i in range(6)]
                        if e:
                            pe.wait_ge(o["h"], e)
                        for i, name in enumerate(("gate", "up")):
                            wide(i, w[2 * i], 0)
                            wide(i, w[2 * i + 1], 1).then_inc(o[name], 1)
                        pe.wait_ge(o["h"], e + 1)
                        turn_hidden(e).then_inc(o["ht_in_psum"], 1)
                        pe.wait_ge(o["ht"], e + 1)
                        down(e, w[4], 0)
                        down(e, w[5], 1).then_inc(o["used"], W_SLOTS_EXPERT)
                    pe.wait_ge(o["y_saved"], 2)
                    for t in range(T):
                        for c in range(2):
                            last = mm(psum[:, 2 * t + c, :], place[:, NG, t * P:(t + 1) * P],
                                      y[:, NG, c * NB:(c + 1) * NB], start=True, stop=True)
                        last.then_inc(o["ffn"], 1)

            pe.wait_ge(s_const, 16 * N_CONST)
            pe.wait_ge(s_ones, 1)
            for L in range(DEPTH):
                transpose_x(3 * L)
                (conv_mixer, retention_mixer, sgu_mixer)[L % 3](L, starts[L][0])
                transpose_x(3 * L + 1)
                route(L)
                experts(L)
                transpose_x(3 * L + 2)
                rows_out(starts[L][3], 4, xT, 4, ple_done)

        @block.scalar
        def _(act):
            def copy(dst, src, func=ACT.Copy):
                return nc.scalar.activation(dst, src, func)

            def quad(bank):
                return psum[:, bank, :].rearrange("p (j n) -> p j n", j=4)

            def transpose_x(k):
                for t in range(T):
                    for q in range(2):
                        act.wait_ge(xt_in_psum, 4 * k + 2 * t + q + 1)
                        copy(xT[:, 4 * q:4 * q + 4, t * P:(t + 1) * P], quad(2 * t + q)).then_inc(xt_ready, 1)

            def conv_mixer(L):
                for job in range(12):
                    b, t = divmod(job, 2)
                    wait_block(act, L, b, t, proj_in_psum[L])
                    copy(bch[:, t, b * NB:(b + 1) * NB], psum[:, job % 8, :]).then_inc(proj_ready[L], 1)
                for k in range(8):
                    src, t, q = k // 4, k // 2 % 2, k % 2
                    act.wait_ge(mt_in_psum[L], k + 1)
                    if src == 0:
                        dst = bT[:, 4 * q:4 * q + 4, t * P:(t + 1) * P]
                    else:
                        dst = zT[:, 4 * q:4 * q + 4, 2 + t * P:2 + (t + 1) * P]
                    copy(dst, quad(k)).then_inc(mt_ready[L], 1)

            def retention_mixer(L):
                for job in range(24):
                    b, t = divmod(job, 2)
                    wait_block(act, L, b, t, proj_in_psum[L])
                    if b < 4:
                        dst = qk[:, t, b * NB:(b + 1) * NB]
                    elif b < 8:
                        dst = rv[:, t, (b - 4) * NB:(b - 3) * NB]
                    else:
                        dst = rg[:, t, (b - 8) * NB:(b - 7) * NB]
                    copy(dst, psum[:, job % 8, :], ACT.Copy if b < 8 else ACT.Sigmoid
                         ).then_inc(proj_ready[L], 1)
                for k in range(8):
                    src, t, q = k // 4, k // 2 % 2, k % 2
                    act.wait_ge(mt_in_psum[L], k + 1)
                    copy(qkT[:, src, 4 * q:4 * q + 4, t * P:(t + 1) * P], quad(k)).then_inc(mt_ready[L], 1)
                for k in range(8):
                    h, c = divmod(k, 2)
                    act.wait_ge(oT_in_psum, k + 1)
                    copy(oT[:, 4 * h:4 * h + 4, c * P:(c + 1) * P], quad(k % 4)).then_inc(oT_ready, 1)

            def sgu_mixer(L):
                act.wait_ge(sw_in_psum, 1)
                copy(sgu_wT, quad(7)).then_inc(sw_ready, 1)
                for job in range(24):
                    b, t = divmod(job, 2)
                    wait_block(act, L, b, t, proj_in_psum[L])
                    dst = sv if b < 6 else su
                    b %= 6
                    copy(dst[:, t, b * NB:(b + 1) * NB], psum[:, job % 8, :], ACT.Gelu
                         ).then_inc(proj_ready[L], 1)
                for k in range(12):
                    s, t = divmod(k, 2)
                    act.wait_ge(mt_in_psum[L], k + 1)
                    copy(uvT[:, 4 * s:4 * s + 4, t * P:(t + 1) * P], quad(4 + k % 4)).then_inc(mt_ready[L], 1)

            def experts(L):
                act.wait_ge(logits_done, L + 1)
                copy(score[:, :, :], psum[:, 0, 0:T * NE].rearrange("p (t e) -> p t e", t=T), ACT.Sigmoid
                     ).then_inc(score_ready, 1)
                act.wait_ge(pt_in_psum, L + 1)
                copy(pT[:, :, :], psum[:, 1, :].rearrange("p (j n) -> p j n", j=2)).then_inc(pt_ready, 1)
                for k in range(4):
                    wait_rows(act, L, k // 2, emb_in_psum, L + 1, starts[L][2])
                    copy(emb[:, k // 2, k % 2 * NB:(k % 2 + 1) * NB], psum[:, 4 + k, :]).then_inc(emb_ready, 1)

                def save_gather(first):
                    for q in range(2):
                        act.wait_ge(xg_in_psum, first + q)
                        copy(xg[:, 4 * q:4 * q + 4, :], quad(q)).then_inc(xg_ready, 1)

                save_gather(10 * L + 1)
                act.wait_ge(cg_in_psum, L + 1)
                copy(cg[:, :], psum[:, 3, 0:4 * NBLK]).then_inc(cg_ready, 1)
                for k in range(3):
                    act.wait_ge(place_in_psum, 3 * L + k + 1)
                    n = 2 if k < 2 else 1
                    copy(place[:, 2 * k:2 * k + n, :], psum[:, 4 + k, 0:n * SEQ].rearrange("p (b n) -> p b n", b=n)
                         ).then_inc(y_banks_free, 1)

                n0 = EPG * NG * L
                with act.Fori(0, NG) as g:
                    def sigmoid(e):
                        act.wait_ge(weights_used, expert_slots(L, GATE_AT[e]) + W_SLOTS_GROUP * g)
                        copy(sg[:, e % 2, :], psum[:, e % 2 * 2, :], ACT.Sigmoid).then_inc(sig_ready, 1)

                    def save_hT(e):
                        act.wait_ge(ht_in_psum, n0 + e + 1 + EPG * g)
                        copy(hT[:, e % 2, :, :], quad(4)).then_inc(ht_ready, 1)

                    sigmoid(0)
                    sigmoid(1)
                    save_hT(0)
                    sigmoid(2)
                    save_hT(1)
                    sigmoid(3)
                    save_hT(2)
                    save_gather(10 * L + 3 + 2 * g)
                    save_hT(3)
                    act.wait_ge(weights_used, expert_slots(L, LAST_AT) + W_SLOTS_GROUP * g)
                    for c in range(2):
                        copy(y[:, g, c * NB:(c + 1) * NB], psum[:, 6 + c, :]).then_inc(y_banks_free, 1)

                act.wait_ge(flag_ready, L + 1)
                crowded = act.value_load(flag[0:1, 0:1], min_val=0, max_val=NG)
                with act.If(crowded > 0):
                    o = ov[L]
                    for e in range(EPG):
                        act.wait_ge(o["gate"], e + 1)
                        copy(sg[:, 0, :], psum[:, 0, :], ACT.Sigmoid).then_inc(o["sig"], 1)
                        act.wait_ge(o["ht_in_psum"], e + 1)
                        copy(hT[:, e % 2, :, :], quad(4)).then_inc(o["ht"], 1)
                    act.wait_ge(o["used"], W_SLOTS_EXPERT * EPG)
                    for c in range(2):
                        copy(y[:, NG, c * NB:(c + 1) * NB], psum[:, 6 + c, :]).then_inc(o["y_saved"], 1)

            for L in range(DEPTH):
                transpose_x(3 * L)
                (conv_mixer, retention_mixer, sgu_mixer)[L % 3](L)
                transpose_x(3 * L + 1)
                experts(L)
                transpose_x(3 * L + 2)
                for t in range(T):
                    act.wait_ge(ple_arg, 2 * L + t + 1)
                    copy(tmp[:, t, :], tmp[:, t, :], ACT.Sigmoid).then_inc(ple_sig, 1)

        @block.vector
        def _(dve):
            steps = [0]

            def link(ins):
                steps[0] += 1
                ins.then_inc(dve_step, 1)
                dve.wait_ge(dve_step, steps[0])

            tt, ts, stt = nc.vector.tensor_tensor, nc.vector.tensor_scalar, nc.vector.scalar_tensor_tensor

            def residual(t, bank0, add_to=ALPHA):
                for c in range(2):
                    xs = x[:, t, c * NB:(c + 1) * NB]
                    link(stt(xs, xs, add_to, psum[:, bank0 + 2 * t + c, :], ALU.mult, ALU.add))

            def moments(parts):
                link(nc.vector.bn_aggr(nmv[:, :], parts))
                link(ts(nvar[:, :], nmv[:, 1:2], LN_EPS, None, ALU.add))
                link(ts(nbits[:, :], nvar[:, :].bitcast(I32), 1, None, ALU.logical_shift_right))
                link(ts(nrstd[:, :].bitcast(I32), nbits[:, :], -1.0, float(0x5F3759DF), ALU.mult, ALU.add))
                for _ in range(3):
                    link(stt(nsq[:, :], nrstd[:, :], nvar[:, :], nrstd[:, :], ALU.mult, ALU.mult))
                    link(ts(nsq[:, :], nsq[:, :], -0.5, 1.5, ALU.mult, ALU.add))
                    link(tt(nrstd[:, :], nrstd[:, :], nsq[:, :], ALU.mult))
                return nmv[:, 0:1], nrstd[:, :]

            def layer_norm(t, k):
                for c in range(2):
                    link(nc.vector.bn_stats(stats[:, t, c, :], x[:, t, c * NB:(c + 1) * NB]))
                mean, rstd = moments(stats[:, t, 0:2, :])
                dve.wait_ge(lnp_loaded, 32 * (k + 1))
                link(stt(x[:, t, :], x[:, t, :], mean, ln_par[:, 0, :], ALU.subtract, ALU.mult))
                stt(x[:, t, :], x[:, t, :], rstd, ln_par[:, 1, :], ALU.mult, ALU.add
                    ).then_inc(x_tile_ready, 1)

            def conv_mixer(L):
                link(nc.vector.memset(zT[:, :, 0:2], 0.0))
                dve.wait_ge(proj_ready[L], 12)
                for t in range(T):
                    tt(bch[:, t, D:2 * D], bch[:, t, D:2 * D], bch[:, t, 2 * D:3 * D], ALU.mult
                       ).then_inc(z_ready[L], 1)
                dve.wait_ge(mt_ready[L], 8)
                base = steps[0]
                acc = tmp[:, :, :].rearrange("p t d -> p (t d)").rearrange("p (j n) -> p j n", j=KD)
                for w in range(3):
                    for j in range(KD):
                        s = conv_w[:, L // 3, w, j:j + 1]
                        src = zT[:, j, w:w + SEQ]
                        if w == 0:
                            ins = ts(acc[:, j, :], src, s, None, ALU.mult)
                        else:
                            dve.wait_ge(dve_step, base + (w - 1) * KD + j + 1)
                            ins = stt(acc[:, j, :], src, s, acc[:, j, :], ALU.mult, ALU.add)
                        ins.then_inc(dve_step, 1)
                steps[0] += 3 * KD
                for j in range(KD):
                    dve.wait_ge(dve_step, base + 2 * KD + j + 1)
                    tt(bT[:, j, :], bT[:, j, :], acc[:, j, :], ALU.mult).then_inc(conv_ready[L], 1)

            def retention_mixer(L):
                H8 = 2 * HEADS
                for t in range(T):
                    dve.wait_ge(proj_ready[L], 7 + t)
                    v = qk[:, t, :].rearrange("p (h a n) -> p h a n", h=H8, a=2)
                    t1, t2 = v[:, :, 0, :], v[:, :, 1, :]
                    cos = rot[:, t, 0:1, :].broadcast_to([P, H8, DK // 2])
                    sin = rot[:, t, 1:2, :].broadcast_to([P, H8, DK // 2])
                    a = tmp[:, 0, :].rearrange("p (h n) -> p h n", h=H8)
                    b = tmp[:, 1, :].rearrange("p (h n) -> p h n", h=H8)
                    c = emb[:, 0, :].rearrange("p (h n) -> p h n", h=H8)
                    link(tt(a, t2, sin, ALU.mult))
                    link(tt(b, t1, sin, ALU.mult))
                    link(tt(c, t1, cos, ALU.mult))
                    link(tt(t1, c, a, ALU.subtract))
                    link(tt(c, t2, cos, ALU.mult))
                    steps[0] += 1
                    tt(t2, c, b, ALU.add).then_inc(dve_step, 1)
                    dve.wait_ge(dve_step, steps[0])
                    dve.sem_inc(qk_ready, 1)
                for k in range(8):
                    b, t = divmod(k, 2)
                    dve.wait_ge(proj_ready[L], 17 + k)
                    gs = rg[:, t, b * NB:(b + 1) * NB]
                    tt(gs, gs, psum[:, k, :], ALU.mult).then_inc(g_ready, 1)
                for h in range(HEADS):
                    dve.wait_ge(score_in_psum, h + 1)
                    tt(sT[:, h, :], psum[:, h, 0:3 * P], decay[:, h, :], ALU.mult).then_inc(sT_ready, 1)
                dve.wait_ge(g_ready, 8)
                for k in range(8):
                    h, c = divmod(k, 2)
                    bank = psum[:, 4 + k % 4, :]
                    dve.wait_ge(o_in_psum, k + 1)
                    link(nc.vector.bn_stats(nstat[:, k, :], bank))
                    mean, rstd = moments(nstat[:, k, :])
                    gs = rg[:, c, h * DV:(h + 1) * DV]
                    stt(gs, bank, mean, gs, ALU.subtract, ALU.mult).then_inc(o_read, 1)
                    dve.wait_ge(o_read, k + 1)
                    ts(gs, gs, rstd, None, ALU.mult).then_inc(o_ready, 1)

            def sgu_mixer(L):
                dve.wait_ge(c_loaded, 48)
                tt(sgu_w, sgu_w, causal[:, :].unsqueeze(1).broadcast_to([P, SGROUPS, P]), ALU.mult
                   ).then_inc(sw_masked, 1)
                for t in range(T):
                    dve.wait_ge(proj_ready[L], 11 + t)
                    for b in range(6):
                        link(nc.vector.bn_stats(stats[:, t, b, :], sv[:, t, b * NB:(b + 1) * NB]))
                    mean, rstd = moments(stats[:, t, :, :])
                    link(stt(sv[:, t, :], sv[:, t, :], mean, c_ln[:, 0, :], ALU.subtract, ALU.mult))
                    stt(sv[:, t, :], sv[:, t, :], rstd, c_ln[:, 1, :], ALU.mult, ALU.add
                        ).then_inc(v_ready, 1)
                dve.wait_ge(proj_ready[L], 24)
                for k in range(16):
                    b, c = divmod(k, 2)
                    us = su[:, c, b * SVB:(b + 1) * SVB]
                    dve.wait_ge(vs_in_psum, k + 1)
                    stt(us, psum[:, k % 4, 0:SVB], sgu_b[:, b // 2:b // 2 + 1], us, ALU.add, ALU.mult
                        ).then_inc(uv_ready, 1)

            def route(L):
                TG = T * NG
                lower = small[:, 0:16].rearrange("p (i j) -> p i j", i=4)
                group_base, group_number = small[:, 16:20], small[:, 20:24]
                dve.wait_ge(score_ready, L + 1)
                link(tt(sel[:, :, :], score[:, :, :], rb[:, :].unsqueeze(1).broadcast_to([P, T, NE]), ALU.add))

                def ahead(v, n):
                    other = v.unsqueeze(2).broadcast_to([P, n, 4, 4])
                    own = v.unsqueeze(3).broadcast_to([P, n, 4, 4])
                    low = lower.unsqueeze(1).broadcast_to([P, n, 4, 4])
                    link(tt(cmp1[:, 0:n], other, own, ALU.is_gt))
                    link(tt(cmp2[:, 0:n], other, own, ALU.is_equal))
                    link(tt(cmp2[:, 0:n], cmp2[:, 0:n], low, ALU.mult))
                    link(tt(cmp1[:, 0:n], cmp1[:, 0:n], cmp2[:, 0:n], ALU.add))
                    link(nc.vector.tensor_reduce(cnt[:, 0:n], cmp1[:, 0:n], X, ALU.add))

                s8 = sel[:, :, :].rearrange("p t (g e) -> p (t g) e", g=NG)
                ahead(s8, TG)
                link(ts(top2[:, :, :], cnt[:, :, :], 1.5, None, ALU.is_lt))
                link(tt(cw[:, :, :, :].rearrange("p t g e -> p (t g) e"), top2[:, :, :], s8, ALU.mult))
                link(nc.vector.tensor_reduce(gscore[:, :, :], cw[:, :, :, :], X, ALU.add))
                ahead(gscore[:, :, :], T)
                ts(ghot[:, :, :], cnt[:, 0:T], 0.5, None, ALU.is_lt).then_inc(ghot_ready, 1)
                dve.wait_ge(ghot_ready, L + 1)
                link(tt(cw[:, :, :, :].rearrange("p t g e -> p (t g) e"), top2[:, :, :],
                        score[:, :, :].rearrange("p t (g e) -> p (t g) e", g=NG), ALU.mult))
                link(tt(cw[:, :, :, :], cw[:, :, :, :],
                        ghot[:, :, :].unsqueeze(3).broadcast_to([P, T, NG, 4]), ALU.mult))
                link(nc.vector.tensor_reduce(comb[:, :, :], cw[:, :, :, :].rearrange("p t g e -> p t e g"),
                                             X, ALU.add))
                link(nc.vector.tensor_reduce(den[:, :], comb[:, :, :], X, ALU.add))
                link(nc.vector.reciprocal(den[:, :], den[:, :]))
                link(tt(comb[:, :, :], comb[:, :, :], den[:, :].unsqueeze(2).broadcast_to([P, T, 4]), ALU.mult))
                link(tt(gpos[:, :, :], ghot[:, :, :], group_base.unsqueeze(1).broadcast_to([P, T, NG]), ALU.mult))
                link(nc.vector.tensor_reduce(gbase[:, :], gpos[:, :, :], X, ALU.add))
                link(ts(shift[:, :], gbase[:, :], -1.0, float((NG - 1) * P), ALU.mult, ALU.add))
                dve.wait_ge(rank_in_psum, L + 1)
                link(tt(gpos[:, :, :], ghot[:, :, :], psum[:, 2, 0:8].rearrange("p (t g) -> p t g", t=T), ALU.mult))
                link(nc.vector.tensor_reduce(pos[:, :], gpos[:, :, :], X, ALU.add))
                link(ts(over[:, :], pos[:, :], P - 0.5, None, ALU.is_gt))
                link(tt(over[:, :], over[:, :], shift[:, :], ALU.mult))
                link(tt(key[:, :], pos[:, :], gbase[:, :], ALU.add))
                link(tt(key[:, :], key[:, :], over[:, :], ALU.add))
                for t in range(T):
                    link(ts(pick[:, t, :], slot_no[:, :], key[:, t:t + 1], None, ALU.is_equal))
                dve.sem_inc(pick_ready, 1)
                link(ts(big[:, :], psum[:, 2, 8:12], P + 0.5, None, ALU.is_gt))
                link(tt(big[:, :], big[:, :], group_number, ALU.mult))
                link(nc.vector.tensor_reduce(bigmax[:, :], big[:, :], X, ALU.max))
                nc.vector.tensor_copy(flag[:, :], bigmax[:, :]).then_inc(flag_ready, 1)

            def experts(L):
                n0 = EPG * NG * L
                dve.wait_ge(cg_ready, L + 1)
                with dve.Fori(0, NG) as g:
                    for e in range(EPG):
                        k = n0 + e + 1 + EPG * g
                        s = sg[:, e % 2, :]
                        dve.wait_ge(sig_ready, k)
                        tt(s, s, psum[:, e % 2 * 2, :], ALU.mult).then_inc(silu_ready, 1)
                        dve.wait_ge(silu_ready, k)
                        dve.wait_ge(weights_used, expert_slots(L, UP_AT[e]) + W_SLOTS_GROUP * g)
                        stt(hid[:, e % 2, :], psum[:, e % 2 * 2 + 1, :], cg[:, bass.ds(4 * g + e, 1)], s,
                            ALU.mult, ALU.mult).then_inc(h_ready, 1)
                for t in range(T):
                    dve.wait_ge(ffn_done, T * L + t + 1)
                    residual(t, 0)
                    dve.sem_inc(ffn_added, 1)
                dve.wait_ge(flag_ready, L + 1)
                crowded = dve.value_load(flag[0:1, 0:1], min_val=0, max_val=NG)
                with dve.If(crowded > 0):
                    o = ov[L]
                    for e in range(EPG):
                        s = sg[:, 0, :]
                        dve.wait_ge(o["sig"], e + 1)
                        tt(s, s, psum[:, 0, :], ALU.mult).then_inc(o["silu"], 1)
                        dve.wait_ge(o["silu"], e + 1)
                        dve.wait_ge(o["up"], e + 1)
                        stt(hid[:, e % 2, :], psum[:, 1, :], cg[:, 4 * NG + e:4 * NG + e + 1], s,
                            ALU.mult, ALU.mult).then_inc(o["h"], 1)
                    for t in range(T):
                        dve.wait_ge(o["ffn"], t + 1)
                        for c in range(2):
                            xs = x[:, t, c * NB:(c + 1) * NB]
                            tt(xs, xs, psum[:, 2 * t + c, :], ALU.add).then_inc(o["silu"], 1)
                    dve.wait_ge(o["silu"], EPG + 2 * T)

            dve.wait_ge(s_const, 16 * N_CONST)
            for L in range(DEPTH):
                (conv_mixer, retention_mixer, sgu_mixer)[L % 3](L)
                for t in range(T):
                    wait_rows(dve, L, t, mix_done, L + 1, starts[L][1])
                    residual(t, 4)
                    layer_norm(t, 2 * L)
                route(L)
                experts(L)
                for t in range(T):
                    layer_norm(t, 2 * L + 1)
                dve.wait_ge(bg_loaded, 16 * (L + 1))
                for t in range(T):
                    wait_rows(dve, L, t, ple_done, L + 1, starts[L][3] + 4)
                    for c in range(2):
                        cols = slice(c * NB, (c + 1) * NB)
                        link(tt(tmp[:, t, cols], psum[:, 4 + 2 * t + c, :], bgate[:, cols], ALU.add))
                    dve.sem_inc(ple_arg, 1)
                for t in range(T):
                    dve.wait_ge(ple_sig, 2 * L + t + 1)
                    link(tt(tmp[:, t, :], tmp[:, t, :], emb[:, t, :], ALU.mult))
                    tt(x[:, t, :], x[:, t, :], tmp[:, t, :], ALU.add).then_inc(x_tile_ready, 1)


def kernel(**inputs):
    import concourse.bacc as bacc
    from concourse.bass_utils import run_bass_kernel_spmd

    nc = bacc.Bacc("TRN2", target_bir_lowering=False, num_devices=1)
    arrays = {n: np.ascontiguousarray(a) for n, a in inputs.items()}
    arrays.update(shape_constants())
    aps, feed = {}, {}
    for name, a in arrays.items():
        feed[f"in_{name}"] = a
        aps[name] = nc.dram_tensor(f"in_{name}", a.shape, mybir.dt.from_np(a.dtype), kind="ExternalInput").ap()
    out = nc.dram_tensor("out", (1, SEQ, D), mybir.dt.float32, kind="ExternalOutput").ap()
    build(nc, aps, out)
    r = run_bass_kernel_spmd(nc, [feed], core_ids=[0])
    return r.results[0]["out"]
```

```python
import numpy as np
import concourse.bass as bass
from concourse import mybir
from contextlib import ExitStack

P = 128
D = 1024
SEQ = 256
T = SEQ // P
DEPTH = 4
KD = D // P
NB = 512
HEADS, DK, DV = 4, 256, 512
VD = HEADS * DV
SGU, SGROUPS = 3 * D, 4
SGD = SGU // SGROUPS
SVB = SGD // 2
NE, NG, EPG = 16, 4, 4
FE = D // 2
PLE = 256
NBLK = NG + 1
ALPHA = float((2 * DEPTH) ** 0.25)
LN_EPS = 1e-5
RING = 6
HIGH = 4
SLOT = 4 * NB
W_SLOTS_EXPERT = 6
W_SLOTS_GROUP = EPG * W_SLOTS_EXPERT
MIXER_SLOTS = {0: (2 * 3 * D // NB, 4), 1: (2 * (2 * D + 2 * VD) // NB, 2 * VD // NB),
               2: (2 * 2 * SGU // NB, 2 * SGU // NB)}


def slot_starts():
    at, out = 0, []
    for layer in range(DEPTH):
        mixer = at
        at += sum(MIXER_SLOTS[layer % 3])
        proj, experts = at, at + 1
        at = experts + NG * W_SLOTS_GROUP
        out.append((mixer, proj, experts, at))
        at += 4
    return out


def shape_constants():
    f = np.float32
    pos = np.arange(SEQ, dtype=f)
    inv = (1.0 / (f(10000.0) ** np.linspace(0.0, 1.0, DK // 2, dtype=f))).astype(f)
    ang = pos[:, None] * inv[None, :]
    rot = np.stack([np.cos(ang), np.sin(ang)], 1).astype(f)
    rot = rot.reshape(T, P, 2, DK // 2).transpose(1, 0, 2, 3).copy()
    lg = np.log(1.0 - 2.0 ** (-5.0 - np.arange(HEADS)))[:, None, None]
    s, c = np.arange(P)[:, None], np.arange(P)[None, :]
    diag = np.where(c >= s, np.exp(lg * np.maximum(c - s, 0)), 0.0)
    cross = np.exp(lg * (P + c - s))
    decay = (np.concatenate([diag, cross], 2) * DK ** -0.5).astype(f).transpose(1, 0, 2).copy()
    lower = (np.arange(4)[None, :] < np.arange(4)[:, None]).astype(f).reshape(1, 16)
    small = np.concatenate([lower, P * np.arange(4, dtype=f)[None], 1 + np.arange(4, dtype=f)[None]], 1)
    return {
        "identity": np.eye(P, dtype=f),
        "before": (s < c).astype(f),
        "causal": (c <= s).astype(f),
        "slot_number": np.broadcast_to(np.arange(NBLK * P, dtype=f), (P, NBLK * P)).copy(),
        "rotary": rot,
        "decay": decay,
        "small": np.broadcast_to(small, (P, 24)).copy(),
    }


def build(nc, A, out):
    F = mybir.dt.float32
    FR = mybir.dt.float32r
    I32 = mybir.dt.int32
    ALU = mybir.AluOpType
    ACT = mybir.ActivationFunctionType
    X = mybir.AxisListType.X
    starts = slot_starts()

    ctx = ExitStack()
    with ctx:
        def sb(name, *shape, dt=F):
            return ctx.enter_context(nc.sbuf_tensor(name, [P, *shape], dt))

        def sem(name):
            return ctx.enter_context(nc.semaphore(name))

        WORK = 18432
        sb("arena", WORK + RING * SLOT)
        arena_at = nc.sbuf_base - 4 * (WORK + RING * SLOT)

        def arena(name, offset, *shape, dt=F):
            return nc.alloc_sbuf_tensor_at(name, [P, *shape], dt, offset=arena_at + 4 * offset)

        work, work_r = arena("work", 0, WORK), arena("work_r", 0, WORK, dt=FR)
        raw, w_lo = arena("raw", WORK, RING, SLOT), arena("w_lo", WORK, RING, SLOT, dt=FR)
        w_hi = sb("w_hi", HIGH, SLOT, dt=FR)
        x = sb("x", T, D)
        xT = [sb("xT_hi", KD, SEQ, dt=FR), sb("xT_lo", KD, SEQ, dt=FR)]
        emb = sb("emb", T, D)
        ln_par = sb("ln_par", 2, D)
        bgate = sb("bgate", D)
        ident = sb("ident", P)
        before = sb("before", P)
        causal = sb("causal", P)
        ones = sb("ones", P)
        slot_no = sb("slot_no", NBLK * P)
        small = sb("small", 24)
        rw = sb("rw", KD, NE)
        rwr = [sb("rw_hi", KD, NE, dt=FR), sb("rw_lo", KD, NE, dt=FR)]
        rb = sb("rb", NE)
        conv_w = sb("conv_w", 2, 3, KD)
        sgu_b = sb("sgu_b", SGROUPS)
        stats = sb("stats", T, 6, 6)
        nstat = sb("nstat", 8, 6)
        nmv = sb("nmv", 2)
        nvar, nsq, nrstd, nbits = sb("nvar", 1), sb("nsq", 1), sb("nrstd", 1), sb("nbits", 1, dt=I32)
        score = sb("score", T, NE)
        sel = sb("sel", T, NE)
        cmp1 = sb("cmp1", T * NG, 4, 4)
        cmp2 = sb("cmp2", T * NG, 4, 4)
        cnt = sb("cnt", T * NG, 4)
        top2 = sb("top2", T * NG, 4)
        gscore = sb("gscore", T, NG)
        gcnt = sb("gcnt", T, NG)
        ghot = sb("ghot", T, NG)
        cw = sb("cw", T, NG, 4)
        den = sb("den", T)
        cwn = sb("cwn", T, NG, 4)
        comb = sb("comb", T, 4)
        gpos = sb("gpos", T, NG)
        pos = sb("pos", T)
        gbase = sb("gbase", T)
        over = sb("over", T)
        shift = sb("shift", T)
        key = sb("key", T)
        big = sb("big", 4)
        bigmax = sb("bigmax", 1)
        flag = sb("flag", 1, dt=I32)
        cg = sb("cg", 4 * NBLK)
        psum = ctx.enter_context(nc.psum_tensor("psum", [P, 8, NB], F))

        def view(start, size, pattern, of=work, **dims):
            return of[:, start:start + size].rearrange(pattern, **dims)

        def pair(hi, lo, size, pattern, **dims):
            return [view(a, size, pattern, of=work_r, **dims) for a in (hi, lo)]

        bch = view(0, T * 3 * D, "p (t n) -> p t n", t=T)
        zT = view(6144, KD * (SEQ + 2), "p (j n) -> p j n", j=KD)
        bT = view(8208, KD * SEQ, "p (j n) -> p j n", j=KD)
        conv = view(10256, KD * SEQ, "p (j n) -> p j n", j=KD)
        gT = pair(0, 2048, KD * SEQ, "p (j n) -> p j n", j=KD)
        qk = view(0, T * 2 * D, "p (t n) -> p t n", t=T)
        rv = view(4096, T * VD, "p (t n) -> p t n", t=T)
        rg = view(8192, T * VD, "p (t n) -> p t n", t=T)
        turned = [view(12288 + D * i, D, "p (h n) -> p h n", h=2 * HEADS) for i in range(3)]
        qkT = view(12288, 2 * KD * SEQ, "p (a j n) -> p a j n", a=2, j=KD)
        sT = view(16384, HEADS * 3 * P, "p (h n) -> p h n", h=HEADS)
        rot = view(17920, T * DK, "p (t a n) -> p t a n", t=T, a=2)
        oT = pair(0, 12288, VD // P * SEQ, "p (j n) -> p j n", j=VD // P)
        su = view(0, T * SGU, "p (t n) -> p t n", t=T)
        sv = view(6144, T * SGU, "p (t n) -> p t n", t=T)
        c_ln = view(12288, 2 * SGU, "p (a n) -> p a n", a=2)
        uvT = pair(12288, 6144, SGU // P * SEQ, "p (j n) -> p j n", j=SGU // P)
        pick = view(0, T * NBLK * P, "p (t n) -> p t n", t=T)
        place = view(1280, NBLK * SEQ, "p (b n) -> p b n", of=work_r, b=NBLK)
        xg = pair(2560, 3584, KD * P, "p (j n) -> p j n", j=KD)
        y = pair(4608, 9728, NBLK * D, "p (b n) -> p b n", b=NBLK)
        pT = pair(4608, 5120, 2 * SEQ, "p (j n) -> p j n", j=2)
        hid = view(14848, 2 * FE, "p (a n) -> p a n", a=2)
        hT = pair(15872, 16896, 2 * FE, "p (a j n) -> p a j n", a=2, j=4)
        ple = view(0, T * D, "p (t n) -> p t n", t=T)
        sgu_w = emb[:, 0, 0:512].rearrange("p (g s) -> p g s", g=SGROUPS)
        sgu_wT = emb[:, 0, 512:1024].rearrange("p (g s) -> p g s", g=SGROUPS)
        decay = emb[:, 0, :].rearrange("p (h n) -> p h n", h=HEADS)
        p_in = emb[:, 1, 0:T * PLE].rearrange("p (t n) -> p t n", t=T)

        s_const = sem("constants_loaded")
        s_x = sem("x_loaded")
        s_ident = sem("identity_loaded")
        hi_ready, lo_ready = sem("hi_ready"), sem("lo_ready")
        rw_hi_ready, rw_ready = sem("rw_hi_ready"), sem("rw_ready")
        xt_hi = sem("xt_hi")
        pt_hi, xg_hi, ht_hi, y_hi = sem("pt_hi"), sem("xg_hi"), sem("ht_hi"), sem("y_hi")
        oT_hi = sem("oT_hi")
        s_ones = sem("ones_set")
        slot_full = [sem(f"slot_full{i}") for i in range(RING)]
        weights_used = sem("weights_used")
        xt_in_psum, xt_ready = sem("xt_in_psum"), sem("xt_ready")
        x_tile_ready = sem("x_tile_ready")
        mix_done = sem("mix_done")
        dve_step = sem("dve_step")
        p_loaded, lnp_loaded, bg_loaded = sem("p_loaded"), sem("lnp_loaded"), sem("bg_loaded")
        pt_in_psum, pt_ready = sem("pt_in_psum"), sem("pt_ready")
        logits_done, score_ready = sem("logits_done"), sem("score_ready")
        emb_in_psum, emb_ready = sem("emb_in_psum"), sem("emb_ready")
        ghot_ready, rank_in_psum = sem("ghot_ready"), sem("rank_in_psum")
        flag_ready, pick_ready = sem("flag_ready"), sem("pick_ready")
        xg_in_psum, xg_ready = sem("xg_in_psum"), sem("xg_ready")
        cg_in_psum, cg_ready = sem("cg_in_psum"), sem("cg_ready")
        place_in_psum, y_banks_free = sem("place_in_psum"), sem("y_banks_free")
        sig_ready, silu_ready, h_ready = sem("sig_ready"), sem("silu_ready"), sem("h_ready")
        ht_in_psum, ht_ready = sem("ht_in_psum"), sem("ht_ready")
        ffn_done, ffn_added = sem("ffn_done"), sem("ffn_added")
        ple_done, ple_arg, ple_sig = sem("ple_done"), sem("ple_arg"), sem("ple_sig")
        proj_in_psum = [sem(f"proj_in_psum{i}") for i in range(DEPTH)]
        proj_ready = [sem(f"proj_ready{i}") for i in range(DEPTH)]
        z_ready = {i: sem(f"z_ready{i}") for i in range(0, DEPTH, 3)}
        mt_in_psum = [sem(f"mixT_in_psum{i}") for i in range(DEPTH)]
        mt_ready = [sem(f"mixT_ready{i}") for i in range(DEPTH)]
        conv_ready = {i: sem(f"conv_ready{i}") for i in range(0, DEPTH, 3)}
        conv_hi = {i: sem(f"conv_hi{i}") for i in range(0, DEPTH, 3)}
        gT_ready = {i: sem(f"gT_ready{i}") for i in range(0, DEPTH, 3)}
        uv_hi, b_loaded = sem("uv_hi"), sem("b_loaded")
        g_ready, qk_ready = sem("g_ready"), sem("qk_ready")
        score_in_psum, sT_ready = sem("scores_in_psum"), sem("sT_ready")
        o_in_psum, o_read, o_ready = sem("o_in_psum"), sem("o_read"), sem("o_ready")
        oT_in_psum, oT_ready = sem("oT_in_psum"), sem("oT_ready")
        c_loaded, sw_masked, sw_in_psum, sw_ready = (sem("c_loaded"), sem("sw_masked"),
                                                     sem("sw_in_psum"), sem("sw_ready"))
        v_ready, vs_in_psum, uv_ready = sem("v_ready"), sem("vs_in_psum"), sem("uv_ready")
        s_out = sem("out_stored")
        OV = ["full", "split_hi", "split_lo", "ht_hi", "y_hi", "added", "used", "sig", "silu", "h", "ht_in_psum", "ht", "y_saved", "ffn"]
        ov = [{n: sem(f"over_{n}{i}") for n in OV} for i in range(DEPTH)]
        N_CONST = 9

        block = ctx.enter_context(nc.Block())

        def wait_block(eng, L, b, t, tile0):
            if t == 0:
                eng.wait_ge(tile0, b + 1)
            else:
                eng.wait_ge(weights_used, starts[L][0] + 2 * (b + 1))

        def wait_rows(eng, L, t, tile0, count, end):
            if t == 0:
                eng.wait_ge(tile0, count)
            else:
                eng.wait_ge(weights_used, end)

        def expert_slots(L, i):
            return starts[L][2] + 2 * (i + 1)

        GATE_AT, UP_AT, LAST_AT = (0, 2, 5, 8), (1, 3, 6, 9), 11

        @block.sync
        def _(sp):
            def load(n, src):
                if n >= RING:
                    sp.wait_ge(weights_used, n - RING + 1)
                sp.dma_start(raw[:, n % RING, :], src).then_inc(slot_full[n % RING], 16)

            def load_columns(n, w, order):
                v = w.rearrange("(p j) n -> p j n", j=KD)
                for b in order:
                    for half in range(2):
                        if n >= RING:
                            sp.wait_ge(weights_used, n - RING + 1)
                        sp.dma_start(raw[:, n % RING, :].rearrange("p (j n) -> p j n", j=4),
                                     v[:, 4 * half:4 * half + 4, b * NB:(b + 1) * NB]
                                     ).then_inc(slot_full[n % RING], 16)
                        n += 1
                return n

            sp.dma_start(ident[:, :], A["identity"]).then_inc(s_ident, 16)
            sp.dma_start(x[:, :, :], A["x"][0].rearrange("(t p) d -> p t d", p=P)).then_inc(s_x, 16)
            for L in range(DEPTH):
                n, n_proj, n_exp, n_gate = starts[L]
                if L % 3 == 0:
                    n = load_columns(n, A["a_w_in"][L // 3], range(6))
                    v = A["a_w_out"][L // 3].rearrange("(p j) n -> p (j n)", j=KD)
                    for i in range(4):
                        load(n + i, v[:, i * SLOT:(i + 1) * SLOT])
                elif L % 3 == 1:
                    n = load_columns(n, A["b_w_in"][L // 3], range(12))
                    v = A["b_w_out"][L // 3].rearrange("(s p j) n -> s p (j n)", p=P, j=4)
                    for i in range(2 * VD // NB):
                        load(n + i, v[i // 2, :, i % 2 * SLOT:(i % 2 + 1) * SLOT])
                else:
                    n = load_columns(n, A["c_w_in"][L // 3], [*range(6, 12), *range(6)])
                    v = A["c_w_out"][L // 3].rearrange("(s p j) n -> s p (j n)", p=P, j=4)
                    for i in range(2 * SGU // NB):
                        load(n + i, v[i // 2, :, i % 2 * SLOT:(i % 2 + 1) * SLOT])
                load(n_proj, A["ple_w_proj"][L].rearrange("(p j) n -> p (j n)", j=2))
                wg = A["moe_w_gate"][L].rearrange("(g e) (p j) n -> g e p (j n)", g=NG, j=KD)
                wu = A["moe_w_up"][L].rearrange("(g e) (p j) n -> g e p (j n)", g=NG, j=KD)
                wd = A["moe_w_down"][L].rearrange("(g e) (p j) n -> g e p (j n)", g=NG, j=4)
                order = [(wg, 0), (wu, 0), (wg, 1), (wu, 1), (wd, 0), (wg, 2), (wu, 2), (wd, 1),
                         (wg, 3), (wu, 3), (wd, 2), (wd, 3)]
                with sp.Fori(0, NG) as g:
                    for i, (w, e) in enumerate(order):
                        for half in range(2):
                            k = n_exp + 2 * i + half
                            sp.wait_ge(weights_used, k - RING + 1 + W_SLOTS_GROUP * g)
                            sp.dma_start(raw[:, k % RING, :], w[g, e, :, half * SLOT:(half + 1) * SLOT]
                                         ).then_inc(slot_full[k % RING], 16)
                v = A["ple_w_gate"][L].rearrange("(p j) n -> p (j n)", j=KD)
                for i in range(4):
                    load(n_gate + i, v[:, i * SLOT:(i + 1) * SLOT])
                sp.wait_ge(flag_ready, L + 1)
                crowded = sp.value_load(flag[0:1, 0:1], min_val=0, max_val=NG)
                with sp.If(crowded > 0):
                    group = sp.value_load(flag[0:1, 0:1], min_val=1, max_val=NG)
                    sp.wait_ge(weights_used, n_gate)
                    sp.wait_ge(lo_ready, n_gate + 4)
                    for e in range(EPG):
                        if e:
                            sp.wait_ge(ov[L]["used"], W_SLOTS_EXPERT * e)
                        for i, w in enumerate((wg, wu, wd)):
                            for half in range(2):
                                sp.dma_start(raw[:, 2 * i + half, :],
                                             w[group - 1, e, :, half * SLOT:(half + 1) * SLOT]
                                             ).then_inc(ov[L]["full"], 16)
                    sp.wait_ge(ov[L]["used"], W_SLOTS_GROUP)
                    for i in range(4):
                        sp.dma_start(raw[:, (n_gate + i) % RING, :], v[:, i * SLOT:(i + 1) * SLOT]
                                     ).then_inc(ov[L]["full"], 16)
            for t in range(T):
                sp.wait_ge(x_tile_ready, 2 * (3 * DEPTH - 1) + t + 1)
                sp.dma_start(out[0, t * P:(t + 1) * P, :], x[:, t, :]).then_inc(s_out, 16)
            sp.wait_ge(s_out, 16 * T)

        @block.gpsimd
        def _(pool):
            nc.gpsimd.memset(ones[:, :], 1.0).then_inc(s_ones, 1)
            loads = [(before[:, :], A["before"]),
                     (causal[:, :], A["causal"]), (slot_no[:, :], A["slot_number"]),
                     (small[:, :], A["small"]),
                     (rw[:, :, :], A["router_w"].rearrange("(p j) e -> p j e", j=KD)),
                     (rb[:, :], A["router_b"].partition_broadcast(P)),
                     (sgu_b[:, :], A["c_b_s"][0].rearrange("g t -> t g"))]
            loads += [(conv_w[:, i, :, :], A["a_conv_w"][i].rearrange("w (p j) -> p w j", j=KD))
                      for i in range(2)]
            assert len(loads) == N_CONST
            for dst, src in loads:
                pool.dma_start(dst, src, allow_slow_non_contiguous=True).then_inc(s_const, 16)
            def load_norm(L, i):
                pool.dma_start(ln_par[:, 0, :], A["ln_g"][L, i].partition_broadcast(P)).then_inc(lnp_loaded, 16)
                pool.dma_start(ln_par[:, 1, :], A["ln_b"][L, i].partition_broadcast(P)).then_inc(lnp_loaded, 16)

            load_norm(0, 0)
            for L in range(DEPTH):
                if L:
                    pool.wait_ge(x_tile_ready, 6 * L)
                pool.dma_start(p_in[:, :, :], A["p"][L, 0].rearrange("(t p) d -> p t d", p=P)
                               ).then_inc(p_loaded, 16)
                pool.dma_start(bgate[:, :], A["ple_b_gate"][L].partition_broadcast(P)).then_inc(bg_loaded, 16)
                if L % 3 == 1:
                    pool.dma_start(rot, A["rotary"]).then_inc(b_loaded, 16)
                    pool.dma_start(decay, A["decay"]).then_inc(b_loaded, 16)
                if L % 3 == 2:
                    for a, name in enumerate(("c_ln_g", "c_ln_b")):
                        pool.dma_start(c_ln[:, a, :], A[name][0].partition_broadcast(P)).then_inc(c_loaded, 16)
                    pool.dma_start(sgu_w, A["c_w_s"][0].rearrange("g t s -> t g s")).then_inc(c_loaded, 16)
                pool.wait_ge(x_tile_ready, 6 * L + 2)
                load_norm(L, 1)
                if L + 1 < DEPTH:
                    pool.wait_ge(x_tile_ready, 6 * L + 4)
                    load_norm(L + 1, 0)

        @block.tensor
        def _(pe):
            mm = nc.tensor.matmul

            def quarters(n):
                return (w_hi[:, n % HIGH, :].rearrange("p (j n) -> p j n", j=4),
                        w_lo[:, n % RING, :].rearrange("p (j n) -> p j n", j=4))

            def slot(n):
                pe.wait_ge(lo_ready, n + 1)
                return quarters(n)

            def product(out, lhs, rhs, start, stop):
                mm(out, lhs[0], rhs[0], start=start, stop=False)
                mm(out, lhs[0], rhs[1], start=False, stop=False)
                return mm(out, lhs[1], rhs[0], start=False, stop=stop)

            def part(v, *at):
                return [a[at] for a in v]

            ALL = slice(None)

            def transpose4(bank, chunks):
                for i, c in enumerate(chunks):
                    last = nc.tensor.transpose(psum[:, bank, i * P:(i + 1) * P], c, ident[:, :])
                return last

            def transpose_x(k):
                for t in range(T):
                    if k == 0:
                        pe.wait_ge(s_x, 16)
                    else:
                        pe.wait_ge(x_tile_ready, 2 * (k - 1) + t + 1)
                    v = x[:, t, :].rearrange("p (c j) -> p j c", j=KD)
                    for q in range(2):
                        transpose4(2 * t + q, [v[:, 4 * q + i, :] for i in range(4)]).then_inc(xt_in_psum, 1)
                pe.wait_ge(xt_ready, 4 * (k + 1))

            def project(n, jobs_of_block, wait_banks, done):
                for b in range(jobs_of_block):
                    for half in range(2):
                        w = slot(n)
                        for t in range(T):
                            job = 2 * b + t
                            if half == 0 and job >= 8:
                                wait_banks(job)
                            for i in range(4):
                                last = product(psum[:, job % 8, :], part(xT, ALL, 4 * half + i, bass.ts(t, P)),
                                               part(w, ALL, i), half == 0 and i == 0, half == 1 and i == 3)
                            if half == 1 and t == 0:
                                last.then_inc(done, 1)
                        last.then_inc(weights_used, 1)
                        n += 1
                return n

            def rows_out(n, count, lhs, bank0, done):
                for s in range(count):
                    w = slot(n + s)
                    for t in range(T):
                        for i in range(2):
                            for c in range(2):
                                last = product(psum[:, bank0 + 2 * t + c, :],
                                               part(lhs, ALL, 2 * s + i, bass.ts(t, P)),
                                               part(w, ALL, 2 * i + c), s == 0 and i == 0,
                                               s == count - 1 and i == 1)
                        if s == count - 1 and t == 0:
                            last.then_inc(done, 1)
                    last.then_inc(weights_used, 1)

            def conv_mixer(L, n):
                def banks(job):
                    pe.wait_ge(proj_ready[L], job - 7)
                n = project(n, 6, banks, proj_in_psum[L])
                pe.wait_ge(proj_ready[L], 12)
                for src in range(2):
                    for t in range(T):
                        if src:
                            pe.wait_ge(z_ready[L], t + 1)
                        v = bch[:, t, src * D:(src + 1) * D].rearrange("p (c j) -> p j c", j=KD)
                        for q in range(2):
                            transpose4(4 * src + 2 * t + q, [v[:, 4 * q + i, :] for i in range(4)]
                                       ).then_inc(mt_in_psum[L], 1)
                pe.wait_ge(mt_ready[L], 8)
                pe.wait_ge(gT_ready[L], KD)
                rows_out(n, 4, gT, 4, mix_done)

            def retention_mixer(L, n):
                def banks(job):
                    pe.wait_ge(proj_ready[L], job - 7)
                n = project(n, 12, banks, proj_in_psum[L])
                pe.wait_ge(g_ready, 8)
                for src in range(2):
                    for t in range(T):
                        pe.wait_ge(qk_ready, t + 1)
                        for q in range(2):
                            c0 = src * D + q * NB
                            transpose4(4 * src + 2 * t + q, [qk[:, t, c0 + i * P:c0 + (i + 1) * P] for i in range(4)]
                                       ).then_inc(mt_in_psum[L], 1)
                pe.wait_ge(mt_ready[L], 8)
                for h in range(HEADS):
                    for half in range(2):
                        mm(psum[:, h, 0:2 * P], qkT[:, 1, 2 * h + half, 0:P], qkT[:, 0, 2 * h + half, 0:2 * P],
                           start=half == 0, stop=half == 1)
                    for half in range(2):
                        last = mm(psum[:, h, 2 * P:3 * P], qkT[:, 1, 2 * h + half, P:2 * P],
                                  qkT[:, 0, 2 * h + half, P:2 * P], start=half == 0, stop=half == 1)
                    last.then_inc(score_in_psum, 1)

                def attend(k):
                    h, c = divmod(k, 2)
                    pe.wait_ge(sT_ready, h + 1)
                    if k >= 4:
                        pe.wait_ge(o_read, k - 3)
                    for s in range(c + 1):
                        last = mm(psum[:, 4 + k % 4, :], sT[:, h, (c + s) * P:(c + s + 1) * P],
                                  rv[:, s, h * DV:(h + 1) * DV], start=s == 0, stop=s == c)
                    last.then_inc(o_in_psum, 1)

                def turn(k):
                    h, c = divmod(k, 2)
                    pe.wait_ge(o_ready, k + 1)
                    if k == 0:
                        pe.wait_ge(sT_ready, HEADS)
                    if k >= 4:
                        pe.wait_ge(oT_ready, k - 3)
                    v = rg[:, c, h * DV:(h + 1) * DV].rearrange("p (c j) -> p j c", j=4)
                    transpose4(k % 4, [v[:, i, :] for i in range(4)]).then_inc(oT_in_psum, 1)

                for k in range(8):
                    attend(k)
                    if k >= 3:
                        turn(k - 3)
                for k in range(5, 8):
                    turn(k)
                pe.wait_ge(oT_ready, 8)
                rows_out(n, 8, oT, 4, mix_done)

            def sgu_mixer(L, n):
                pe.wait_ge(sw_masked, 1)
                transpose4(7, [sgu_w[:, g, :] for g in range(SGROUPS)]).then_inc(sw_in_psum, 1)
                pe.wait_ge(sw_ready, 1)

                def banks(job):
                    pe.wait_ge(proj_ready[L], job - 7)
                n = project(n, 12, banks, proj_in_psum[L])
                pe.wait_ge(proj_ready[L], 24)
                for k in range(16):
                    b, c = divmod(k, 2)
                    pe.wait_ge(v_ready, 12)
                    if k >= 4:
                        pe.wait_ge(uv_ready, k - 3)
                    mm(psum[:, k % 4, 0:SVB], sgu_wT[:, b // 2, :], sv[:, c, b * SVB:(b + 1) * SVB],
                       start=True, stop=True).then_inc(vs_in_psum, 1)
                for k in range(12):
                    s, t = divmod(k, 2)
                    pe.wait_ge(uv_ready, 16)
                    if k >= 4:
                        pe.wait_ge(mt_ready[L], k - 3)
                    v = su[:, t, s * NB:(s + 1) * NB].rearrange("p (c j) -> p j c", j=4)
                    transpose4(4 + k % 4, [v[:, i, :] for i in range(4)]).then_inc(mt_in_psum[L], 1)
                pe.wait_ge(mt_ready[L], 12)
                rows_out(n, 12, uvT, 4, mix_done)

            def route(L):
                pe.wait_ge(rw_ready, 1)
                for t in range(T):
                    for j in range(KD):
                        last = product(psum[:, 0, t * NE:(t + 1) * NE], part(xT, ALL, j, bass.ts(t, P)),
                                       part(rwr, ALL, j), j == 0, j == KD - 1)
                last.then_inc(logits_done, 1)
                pe.wait_ge(p_loaded, 16 * (L + 1))
                for t in range(T):
                    v = p_in[:, t, :].rearrange("p (c j) -> p j c", j=2)
                    for j in range(2):
                        last = nc.tensor.transpose(psum[:, 1, j * SEQ + t * P:j * SEQ + (t + 1) * P],
                                                   v[:, j, :], ident[:, :])
                last.then_inc(pt_in_psum, 1)
                pe.wait_ge(pt_ready, L + 1)
                rows_out(starts[L][1], 1, pT, 4, emb_in_psum)
                pe.wait_ge(ghot_ready, L + 1)
                mm(psum[:, 2, 0:4], before[:, :], ghot[:, 0, :], start=True, stop=True)
                mm(psum[:, 2, 4:8], ones[:, :], ghot[:, 0, :], start=True, stop=False)
                mm(psum[:, 2, 4:8], before[:, :], ghot[:, 1, :], start=False, stop=True)
                mm(psum[:, 2, 8:12], ones[:, :], ghot[:, 0, :], start=True, stop=False)
                mm(psum[:, 2, 8:12], ones[:, :], ghot[:, 1, :], start=False, stop=True
                   ).then_inc(rank_in_psum, 1)

            def gather(block):
                for q in range(2):
                    for i in range(4):
                        for t in range(T):
                            v = x[:, t, :].rearrange("p (c j) -> p j c", j=KD)
                            last = mm(psum[:, q, i * P:(i + 1) * P], v[:, 4 * q + i, :],
                                      pick[:, t, bass.ts(block, P)], start=t == 0, stop=t == T - 1)
                    last.then_inc(xg_in_psum, 1)

            def wide(bank, w, half):
                for i in range(4):
                    last = product(psum[:, bank, :], part(xg, ALL, 4 * half + i), part(w, ALL, i),
                                   half == 0 and i == 0, half == 1 and i == 3)
                return last

            def turn_hidden(e):
                v = hid[:, e % 2, :].rearrange("p (c j) -> p j c", j=4)
                return transpose4(4, [v[:, i, :] for i in range(4)])

            def down(e, w, half):
                for i in range(2):
                    for c in range(2):
                        last = product(psum[:, 6 + c, :], part(hT, ALL, e % 2, 2 * half + i),
                                       part(w, ALL, 2 * i + c), e == 0 and half == 0 and i == 0,
                                       e == EPG - 1 and half == 1 and i == 1)
                return last

            def put_back(b, t, c, start, stop):
                for i in range(2):
                    last = mm(psum[:, 2 * t + c, :], place[:, b, t * P:(t + 1) * P],
                              y[i][:, b, c * NB:(c + 1) * NB], start=start and i == 0, stop=stop and i == 1)
                return last

            def experts(L):
                n0 = starts[L][2]
                pe.wait_ge(pick_ready, L + 1)
                pe.wait_ge(emb_ready, 4 * (L + 1))
                gather(0)
                for b in range(NBLK):
                    for t in range(T):
                        last = mm(psum[:, 3, 4 * b:4 * b + 4], pick[:, t, b * P:(b + 1) * P], comb[:, t, :],
                                  start=t == 0, stop=t == T - 1)
                last.then_inc(cg_in_psum, 1)
                for b in range(NBLK):
                    for t in range(T):
                        c = b % 2 * SEQ + t * P
                        last = nc.tensor.transpose(psum[:, 4 + b // 2, c:c + P], pick[:, t, b * P:(b + 1) * P],
                                                   ident[:, :])
                    if b % 2 or b == NBLK - 1:
                        last.then_inc(place_in_psum, 1)
                pe.wait_ge(y_banks_free, 11 * L + 3)
                pe.wait_ge(cg_ready, L + 1)
                pe.wait_ge(flag_ready, L + 1)

                with pe.Fori(0, NG) as g:
                    def take(i, half):
                        k = n0 + 2 * i + half
                        pe.wait_ge(lo_ready, k + 1 + W_SLOTS_GROUP * g)
                        return quarters(k)

                    def pass_wide(i, bank):
                        wide(bank, take(i, 0), 0).then_inc(weights_used, 1)
                        wide(bank, take(i, 1), 1).then_inc(weights_used, 1)

                    def pass_turn(e):
                        pe.wait_ge(h_ready, EPG * (NG * L) + e + 1 + EPG * g)
                        turn_hidden(e).then_inc(ht_in_psum, 1)

                    def pass_down(i, e, half):
                        if half == 0:
                            pe.wait_ge(ht_ready, EPG * NG * L + e + 1 + EPG * g)
                        if e == 0 and half == 0:
                            pe.wait_ge(y_banks_free, 11 * L + 3 + 2 * g)
                        down(e, take(i, half), half).then_inc(weights_used, 1)

                    pe.wait_ge(xg_ready, 10 * L + 2 + 2 * g)
                    pass_wide(0, 0)
                    pass_wide(1, 1)
                    pass_wide(2, 2)
                    pass_turn(0)
                    pass_wide(3, 3)
                    pass_down(4, 0, 0)
                    pass_down(4, 0, 1)
                    pass_wide(5, 0)
                    pass_turn(1)
                    pass_wide(6, 1)
                    pass_down(7, 1, 0)
                    pass_down(7, 1, 1)
                    pass_wide(8, 2)
                    pass_turn(2)
                    pass_wide(9, 3)
                    gather(g + 1)
                    pass_down(10, 2, 0)
                    pass_turn(3)
                    pass_down(10, 2, 1)
                    pass_down(11, 3, 0)
                    pass_down(11, 3, 1)

                pe.wait_ge(xg_ready, 10 * (L + 1))
                pe.wait_ge(y_banks_free, 11 * (L + 1))
                for t in range(T):
                    for b in range(NG):
                        for c in range(2):
                            last = put_back(b, t, c, b == 0, b == NG - 1)
                    last.then_inc(ffn_done, 1)

                crowded = pe.value_load(flag[0:1, 0:1], min_val=0, max_val=NG)
                with pe.If(crowded > 0):
                    o = ov[L]
                    pe.wait_ge(ffn_added, T * (L + 1))
                    for e in range(EPG):
                        def take(i):
                            k = W_SLOTS_EXPERT * e + i
                            pe.wait_ge(o["split_lo"], k + 1)
                            return (w_hi[:, k % HIGH, :].rearrange("p (j n) -> p j n", j=4),
                                    w_lo[:, k % RING, :].rearrange("p (j n) -> p j n", j=4))

                        if e:
                            pe.wait_ge(o["h"], e)
                        for i in range(2):
                            wide(i, take(2 * i), 0).then_inc(o["used"], 1)
                            wide(i, take(2 * i + 1), 1).then_inc(o["used"], 1)
                        pe.wait_ge(o["h"], e + 1)
                        turn_hidden(e).then_inc(o["ht_in_psum"], 1)
                        pe.wait_ge(o["ht"], e + 1)
                        down(e, take(4), 0).then_inc(o["used"], 1)
                        down(e, take(5), 1).then_inc(o["used"], 1)
                    pe.wait_ge(o["y_saved"], 2)
                    for t in range(T):
                        for c in range(2):
                            last = put_back(NG, t, c, True, True)
                        last.then_inc(o["ffn"], 1)
                    pe.wait_ge(o["split_lo"], W_SLOTS_GROUP + 4)

            pe.wait_ge(s_ident, 16)
            for L in range(DEPTH):
                transpose_x(3 * L)
                if L == 0:
                    pe.wait_ge(s_ones, 1)
                (conv_mixer, retention_mixer, sgu_mixer)[L % 3](L, starts[L][0])
                transpose_x(3 * L + 1)
                route(L)
                experts(L)
                transpose_x(3 * L + 2)
                rows_out(starts[L][3], 4, xT, 4, ple_done)

        @block.scalar
        def _(act):
            split = [0]

            def copy(dst, src, func=ACT.Copy):
                return nc.scalar.activation(dst, src, func)

            def quad(bank):
                return psum[:, bank, :].rearrange("p (j n) -> p j n", j=4)

            def split_slot(n, later=0, arrivals=0):
                act.wait_ge(slot_full[n % RING], 16 * (n // RING + 1) + arrivals)
                if n >= HIGH:
                    act.wait_ge(weights_used, n - HIGH + 1 + later)
                copy(w_hi[:, n % HIGH, :], raw[:, n % RING, :]).then_inc(hi_ready, 1)

            def split_behind(used):
                while split[0] < min(used + HIGH, starts[-1][3] + 4):
                    split_slot(split[0])
                    split[0] += 1

            def transpose_x(k):
                for t in range(T):
                    for q in range(2):
                        act.wait_ge(xt_in_psum, 4 * k + 2 * t + q + 1)
                        copy(xT[0][:, 4 * q:4 * q + 4, t * P:(t + 1) * P], quad(2 * t + q)).then_inc(xt_hi, 1)

            def conv_mixer(L):
                n = starts[L][0]
                for job in range(12):
                    b, t = divmod(job, 2)
                    split_behind(n + job)
                    wait_block(act, L, b, t, proj_in_psum[L])
                    copy(bch[:, t, b * NB:(b + 1) * NB], psum[:, job % 8, :]).then_inc(proj_ready[L], 1)
                split_behind(n + 12)
                if L == 0:
                    act.wait_ge(s_const, 16 * N_CONST)
                    copy(rwr[0][:, :, :], rw[:, :, :]).then_inc(rw_hi_ready, 1)
                for k in range(8):
                    src, t, q = k // 4, k // 2 % 2, k % 2
                    act.wait_ge(mt_in_psum[L], k + 1)
                    if src == 0:
                        dst = bT[:, 4 * q:4 * q + 4, t * P:(t + 1) * P]
                    else:
                        dst = zT[:, 4 * q:4 * q + 4, 2 + t * P:2 + (t + 1) * P]
                    copy(dst, quad(k)).then_inc(mt_ready[L], 1)
                for j in range(KD):
                    act.wait_ge(conv_ready[L], j + 1)
                    copy(gT[0][:, j, :], bT[:, j, :]).then_inc(conv_hi[L], 1)
                split_behind(starts[L][1] - 1)

            def retention_mixer(L):
                n = starts[L][0]
                for job in range(24):
                    b, t = divmod(job, 2)
                    split_behind(n + job)
                    wait_block(act, L, b, t, proj_in_psum[L])
                    if b < 4:
                        dst = qk[:, t, b * NB:(b + 1) * NB]
                    elif b < 8:
                        dst = rv[:, t, (b - 4) * NB:(b - 3) * NB]
                    else:
                        dst = rg[:, t, (b - 8) * NB:(b - 7) * NB]
                    copy(dst, psum[:, job % 8, :], ACT.Copy if b < 8 else ACT.Sigmoid
                         ).then_inc(proj_ready[L], 1)
                split_behind(n + 24)
                for k in range(8):
                    src, t, q = k // 4, k // 2 % 2, k % 2
                    act.wait_ge(mt_in_psum[L], k + 1)
                    copy(qkT[:, src, 4 * q:4 * q + 4, t * P:(t + 1) * P], quad(k)).then_inc(mt_ready[L], 1)
                for k in range(8):
                    h, c = divmod(k, 2)
                    act.wait_ge(oT_in_psum, k + 1)
                    copy(oT[0][:, 4 * h:4 * h + 4, c * P:(c + 1) * P], quad(k % 4)).then_inc(oT_hi, 1)
                split_behind(starts[L][1] - 1)

            def sgu_mixer(L):
                n = starts[L][0]
                act.wait_ge(sw_in_psum, 1)
                copy(sgu_wT, quad(7)).then_inc(sw_ready, 1)
                for job in range(24):
                    b, t = divmod(job, 2)
                    split_behind(n + job)
                    wait_block(act, L, b, t, proj_in_psum[L])
                    dst = sv if b < 6 else su
                    b %= 6
                    copy(dst[:, t, b * NB:(b + 1) * NB], psum[:, job % 8, :], ACT.Gelu
                         ).then_inc(proj_ready[L], 1)
                split_behind(n + 24)
                for k in range(12):
                    s, t = divmod(k, 2)
                    act.wait_ge(mt_in_psum[L], k + 1)
                    copy(uvT[0][:, 4 * s:4 * s + 4, t * P:(t + 1) * P], quad(4 + k % 4)).then_inc(uv_hi, 1)
                split_behind(starts[L][1] - 1)

            def save_gather(first):
                for q in range(2):
                    act.wait_ge(xg_in_psum, first + q)
                    copy(xg[0][:, 4 * q:4 * q + 4, :], quad(q)).then_inc(xg_hi, 1)

            def route(L):
                act.wait_ge(logits_done, L + 1)
                copy(score[:, :, :], psum[:, 0, 0:T * NE].rearrange("p (t e) -> p t e", t=T), ACT.Sigmoid
                     ).then_inc(score_ready, 1)
                act.wait_ge(pt_in_psum, L + 1)
                copy(pT[0][:, :, :], psum[:, 1, :].rearrange("p (j n) -> p j n", j=2)).then_inc(pt_hi, 1)
                for k in range(4):
                    wait_rows(act, L, k // 2, emb_in_psum, L + 1, starts[L][2])
                    copy(emb[:, k // 2, k % 2 * NB:(k % 2 + 1) * NB], psum[:, 4 + k, :]).then_inc(emb_ready, 1)
                split_behind(starts[L][2])
                save_gather(10 * L + 1)
                act.wait_ge(cg_in_psum, L + 1)
                copy(cg[:, :], psum[:, 3, 0:4 * NBLK]).then_inc(cg_ready, 1)

            def experts(L):
                n0, s0 = EPG * NG * L, starts[L][2]
                with act.Fori(0, NG) as g:
                    def sigmoid(e):
                        act.wait_ge(weights_used, expert_slots(L, GATE_AT[e]) + W_SLOTS_GROUP * g)
                        copy(hid[:, e % 2, :], psum[:, e % 2 * 2, :], ACT.Sigmoid).then_inc(sig_ready, 1)

                    def save_hT(e):
                        act.wait_ge(ht_in_psum, n0 + e + 1 + EPG * g)
                        copy(hT[0][:, e % 2, :, :], quad(4)).then_inc(ht_hi, 1)

                    for m in range(W_SLOTS_GROUP):
                        if m in (1, 5, 11, 17):
                            sigmoid((1, 5, 11, 17).index(m))
                        if m in (5, 11, 17, 20):
                            save_hT((5, 11, 17, 20).index(m))
                        if m == 23:
                            act.wait_ge(weights_used, expert_slots(L, LAST_AT) + W_SLOTS_GROUP * g)
                            for c in range(2):
                                copy(y[0][:, g, c * NB:(c + 1) * NB], psum[:, 6 + c, :]).then_inc(y_hi, 1)
                        split_slot(s0 + m + HIGH, W_SLOTS_GROUP * g, 16 * (W_SLOTS_GROUP // RING) * g)
                        if m == 19:
                            save_gather(10 * L + 3 + 2 * g)
                split[0] = starts[L][3] + HIGH

                act.wait_ge(flag_ready, L + 1)
                crowded = act.value_load(flag[0:1, 0:1], min_val=0, max_val=NG)
                with act.If(crowded > 0):
                    o = ov[L]
                    for e in range(EPG):
                        act.wait_ge(o["full"], 16 * W_SLOTS_EXPERT * (e + 1))
                        if e == 0:
                            act.wait_ge(lo_ready, starts[L][3] + 4)
                        for k in range(W_SLOTS_EXPERT * e, W_SLOTS_EXPERT * (e + 1)):
                            if k >= HIGH:
                                act.wait_ge(o["used"], k - HIGH + 1)
                            copy(w_hi[:, k % HIGH, :], raw[:, k % RING, :]).then_inc(o["split_hi"], 1)
                        act.wait_ge(o["used"], W_SLOTS_EXPERT * e + 2)
                        copy(hid[:, e % 2, :], psum[:, 0, :], ACT.Sigmoid).then_inc(o["sig"], 1)
                        act.wait_ge(o["ht_in_psum"], e + 1)
                        copy(hT[0][:, e % 2, :, :], quad(4)).then_inc(o["ht_hi"], 1)
                    act.wait_ge(o["used"], W_SLOTS_GROUP)
                    for c in range(2):
                        copy(y[0][:, NG, c * NB:(c + 1) * NB], psum[:, 6 + c, :]).then_inc(o["y_hi"], 1)
                    act.wait_ge(o["full"], 16 * (W_SLOTS_GROUP + 4))
                    for k in range(starts[L][3], starts[L][3] + 4):
                        copy(w_hi[:, k % HIGH, :], raw[:, k % RING, :]).then_inc(o["split_hi"], 1)

            split_behind(0)
            for L in range(DEPTH):
                transpose_x(3 * L)
                (conv_mixer, retention_mixer, sgu_mixer)[L % 3](L)
                split_behind(starts[L][1])
                transpose_x(3 * L + 1)
                route(L)
                experts(L)
                transpose_x(3 * L + 2)
                split_behind(starts[L][3] + 3)
                for t in range(T):
                    act.wait_ge(ple_arg, 2 * L + t + 1)
                    copy(ple[:, t, :], ple[:, t, :], ACT.Sigmoid).then_inc(ple_sig, 1)
                split_behind(starts[L][3] + 4)

        @block.vector
        def _(dve):
            steps = [0]

            def link(ins):
                steps[0] += 1
                ins.then_inc(dve_step, 1)
                dve.wait_ge(dve_step, steps[0])

            tt, ts, stt = nc.vector.tensor_tensor, nc.vector.tensor_scalar, nc.vector.scalar_tensor_tensor
            split = [0]

            def rest(lo, whole, hi):
                return tt(lo, whole, hi.bitcast(F), ALU.subtract)

            def quad(bank):
                return psum[:, bank, :].rearrange("p (j n) -> p j n", j=4)

            def split_slot(n, later=0):
                dve.wait_ge(hi_ready, n + 1 + later)
                rest(w_lo[:, n % RING, :], raw[:, n % RING, :], w_hi[:, n % HIGH, :]).then_inc(lo_ready, 1)

            def split_behind(used):
                while split[0] < min(used + HIGH, starts[-1][3] + 4):
                    split_slot(split[0])
                    split[0] += 1

            def transpose_x(k):
                for t in range(T):
                    for q in range(2):
                        dve.wait_ge(xt_hi, 4 * k + 2 * t + q + 1)
                        at = (slice(None), slice(4 * q, 4 * q + 4), bass.ts(t, P))
                        rest(xT[1][at], quad(2 * t + q), xT[0][at]).then_inc(xt_ready, 1)

            def residual(t, bank0, add_to=ALPHA):
                for c in range(2):
                    xs = x[:, t, c * NB:(c + 1) * NB]
                    link(stt(xs, xs, add_to, psum[:, bank0 + 2 * t + c, :], ALU.mult, ALU.add))

            def moments(parts):
                link(nc.vector.bn_aggr(nmv[:, :], parts))
                link(ts(nvar[:, :], nmv[:, 1:2], LN_EPS, None, ALU.add))
                link(ts(nbits[:, :], nvar[:, :].bitcast(I32), 1, None, ALU.logical_shift_right))
                link(ts(nrstd[:, :].bitcast(I32), nbits[:, :], -1.0, float(0x5F3759DF), ALU.mult, ALU.add))
                for _ in range(3):
                    link(stt(nsq[:, :], nrstd[:, :], nvar[:, :], nrstd[:, :], ALU.mult, ALU.mult))
                    link(ts(nsq[:, :], nsq[:, :], -0.5, 1.5, ALU.mult, ALU.add))
                    link(tt(nrstd[:, :], nrstd[:, :], nsq[:, :], ALU.mult))
                return nmv[:, 0:1], nrstd[:, :]

            def layer_norm(t, k):
                for c in range(2):
                    link(nc.vector.bn_stats(stats[:, t, c, :], x[:, t, c * NB:(c + 1) * NB]))
                mean, rstd = moments(stats[:, t, 0:2, :])
                dve.wait_ge(lnp_loaded, 32 * (k + 1))
                link(stt(x[:, t, :], x[:, t, :], mean, ln_par[:, 0, :], ALU.subtract, ALU.mult))
                stt(x[:, t, :], x[:, t, :], rstd, ln_par[:, 1, :], ALU.mult, ALU.add
                    ).then_inc(x_tile_ready, 1)

            def conv_mixer(L):
                n = starts[L][0]
                link(nc.vector.memset(zT[:, :, 0:2], 0.0))
                split_behind(n + 11)
                dve.wait_ge(proj_ready[L], 12)
                for t in range(T):
                    tt(bch[:, t, D:2 * D], bch[:, t, D:2 * D], bch[:, t, 2 * D:3 * D], ALU.mult
                       ).then_inc(z_ready[L], 1)
                split_behind(n + 12)
                if L == 0:
                    dve.wait_ge(s_const, 16 * N_CONST)
                    dve.wait_ge(rw_hi_ready, 1)
                    rest(rwr[1][:, :, :], rw[:, :, :], rwr[0][:, :, :]).then_inc(rw_ready, 1)
                dve.wait_ge(mt_ready[L], 8)
                base = steps[0]
                for w in range(3):
                    for j in range(KD):
                        s = conv_w[:, L // 3, w, j:j + 1]
                        src = zT[:, j, w:w + SEQ]
                        if w == 0:
                            ins = ts(conv[:, j, :], src, s, None, ALU.mult)
                        else:
                            dve.wait_ge(dve_step, base + (w - 1) * KD + j + 1)
                            ins = stt(conv[:, j, :], src, s, conv[:, j, :], ALU.mult, ALU.add)
                        ins.then_inc(dve_step, 1)
                steps[0] += 3 * KD
                for j in range(KD):
                    dve.wait_ge(dve_step, base + 2 * KD + j + 1)
                    tt(bT[:, j, :], bT[:, j, :], conv[:, j, :], ALU.mult).then_inc(conv_ready[L], 1)
                for j in range(KD):
                    dve.wait_ge(conv_hi[L], j + 1)
                    rest(gT[1][:, j, :], bT[:, j, :], gT[0][:, j, :]).then_inc(gT_ready[L], 1)
                split_behind(starts[L][1] - 1)

            def rotary(L, t, step):
                v = qk[:, t, :].rearrange("p (h a n) -> p h a n", h=2 * HEADS, a=2)
                t1, t2 = v[:, :, 0, :], v[:, :, 1, :]
                cos = rot[:, t, 0:1, :].broadcast_to([P, 2 * HEADS, DK // 2])
                sin = rot[:, t, 1:2, :].broadcast_to([P, 2 * HEADS, DK // 2])
                a, b, c = turned
                link((lambda: tt(a, t2, sin, ALU.mult), lambda: tt(b, t1, sin, ALU.mult),
                      lambda: tt(c, t1, cos, ALU.mult), lambda: tt(t1, c, a, ALU.subtract),
                      lambda: tt(c, t2, cos, ALU.mult), lambda: tt(t2, c, b, ALU.add))[step]())
                if step == 5:
                    dve.sem_inc(qk_ready, 1)

            def retention_mixer(L):
                n = starts[L][0]
                split_behind(n + 7)
                dve.wait_ge(b_loaded, 32)
                dve.wait_ge(proj_ready[L], 8)
                for i in range(12):
                    rotary(L, i // 6, i % 6)
                    split_behind(n + 8 + i // 2)
                for k in range(8):
                    b, t = divmod(k, 2)
                    split_behind(n + 16 + k)
                    dve.wait_ge(proj_ready[L], 17 + k)
                    gs = rg[:, t, b * NB:(b + 1) * NB]
                    tt(gs, gs, psum[:, k, :], ALU.mult).then_inc(g_ready, 1)
                split_behind(n + 24)
                for h in range(HEADS):
                    dve.wait_ge(score_in_psum, h + 1)
                    tt(sT[:, h, 0:2 * P], psum[:, h, 0:2 * P], decay[:, h, :], ALU.mult)
                    tt(sT[:, h, 2 * P:3 * P], psum[:, h, 2 * P:3 * P], decay[:, h, 0:P], ALU.mult
                       ).then_inc(sT_ready, 1)
                dve.wait_ge(g_ready, 8)

                def save_rest(k):
                    h, c = divmod(k, 2)
                    dve.wait_ge(oT_hi, k + 1)
                    at = (slice(None), slice(4 * h, 4 * h + 4), bass.ts(c, P))
                    rest(oT[1][at], quad(k % 4), oT[0][at]).then_inc(oT_ready, 1)

                for k in range(8):
                    h, c = divmod(k, 2)
                    bank = psum[:, 4 + k % 4, :]
                    dve.wait_ge(o_in_psum, k + 1)
                    link(nc.vector.bn_stats(nstat[:, k, :], bank))
                    mean, rstd = moments(nstat[:, k, :])
                    gs = rg[:, c, h * DV:(h + 1) * DV]
                    stt(gs, bank, mean, gs, ALU.subtract, ALU.mult).then_inc(o_read, 1)
                    dve.wait_ge(o_read, k + 1)
                    ts(gs, gs, rstd, None, ALU.mult).then_inc(o_ready, 1)
                    if k >= 4:
                        save_rest(k - 4)
                for k in range(4, 8):
                    save_rest(k)
                split_behind(starts[L][1] - 1)

            def sgu_mixer(L):
                n = starts[L][0]
                dve.wait_ge(c_loaded, 48)
                tt(sgu_w, sgu_w, causal[:, :].unsqueeze(1).broadcast_to([P, SGROUPS, P]), ALU.mult
                   ).then_inc(sw_masked, 1)
                for b in range(6):
                    for t in range(T):
                        split_behind(n + 2 * b + t)
                        dve.wait_ge(proj_ready[L], 2 * b + t + 1)
                        link(nc.vector.bn_stats(stats[:, t, b, :], sv[:, t, b * NB:(b + 1) * NB]))
                for t in range(T):
                    mean, rstd = moments(stats[:, t, :, :])
                    for b in range(6):
                        cols = slice(b * NB, (b + 1) * NB)
                        link(stt(sv[:, t, cols], sv[:, t, cols], mean, c_ln[:, 0, cols], ALU.subtract, ALU.mult))
                        ins = stt(sv[:, t, cols], sv[:, t, cols], rstd, c_ln[:, 1, cols], ALU.mult, ALU.add)
                        ins.then_inc(v_ready, 1)
                        split_behind(n + 12 + 6 * t + b)
                split_behind(n + 23)
                dve.wait_ge(v_ready, 12)
                dve.wait_ge(proj_ready[L], 24)
                split_behind(n + 24)
                for k in range(16):
                    b, c = divmod(k, 2)
                    us = su[:, c, b * SVB:(b + 1) * SVB]
                    dve.wait_ge(vs_in_psum, k + 1)
                    stt(us, psum[:, k % 4, 0:SVB], sgu_b[:, b // 2:b // 2 + 1], us, ALU.add, ALU.mult
                        ).then_inc(uv_ready, 1)
                for k in range(12):
                    s, t = divmod(k, 2)
                    dve.wait_ge(uv_hi, k + 1)
                    at = (slice(None), slice(4 * s, 4 * s + 4), bass.ts(t, P))
                    rest(uvT[1][at], quad(4 + k % 4), uvT[0][at]).then_inc(mt_ready[L], 1)
                split_behind(starts[L][1] - 1)

            def route(L):
                TG = T * NG
                lower = small[:, 0:16].rearrange("p (i j) -> p i j", i=4)
                group_base, group_number = small[:, 16:20], small[:, 20:24]
                dve.wait_ge(pt_hi, L + 1)
                rest(pT[1][:, :, :], psum[:, 1, :].rearrange("p (j n) -> p j n", j=2), pT[0][:, :, :]
                     ).then_inc(pt_ready, 1)
                dve.wait_ge(score_ready, L + 1)
                link(tt(sel[:, :, :], score[:, :, :], rb[:, :].unsqueeze(1).broadcast_to([P, T, NE]), ALU.add))

                def ahead(v, n):
                    other = v.unsqueeze(2).broadcast_to([P, n, 4, 4])
                    own = v.unsqueeze(3).broadcast_to([P, n, 4, 4])
                    low = lower.unsqueeze(1).broadcast_to([P, n, 4, 4])
                    link(tt(cmp1[:, 0:n], other, own, ALU.is_gt))
                    link(tt(cmp2[:, 0:n], other, own, ALU.is_equal))
                    link(tt(cmp2[:, 0:n], cmp2[:, 0:n], low, ALU.mult))
                    link(tt(cmp1[:, 0:n], cmp1[:, 0:n], cmp2[:, 0:n], ALU.add))
                    link(nc.vector.tensor_reduce(cnt[:, 0:n], cmp1[:, 0:n], X, ALU.add))

                s8 = sel[:, :, :].rearrange("p t (g e) -> p (t g) e", g=NG)
                ahead(s8, TG)
                link(ts(top2[:, :, :], cnt[:, :, :], 1.5, None, ALU.is_lt))
                link(tt(cw[:, :, :, :].rearrange("p t g e -> p (t g) e"), top2[:, :, :], s8, ALU.mult))
                link(nc.vector.tensor_reduce(gscore[:, :, :], cw[:, :, :, :], X, ALU.add))
                ahead(gscore[:, :, :], T)
                ts(ghot[:, :, :], cnt[:, 0:T], 0.5, None, ALU.is_lt).then_inc(ghot_ready, 1)
                dve.wait_ge(ghot_ready, L + 1)
                link(tt(cw[:, :, :, :].rearrange("p t g e -> p (t g) e"), top2[:, :, :],
                        score[:, :, :].rearrange("p t (g e) -> p (t g) e", g=NG), ALU.mult))
                link(tt(cw[:, :, :, :], cw[:, :, :, :],
                        ghot[:, :, :].unsqueeze(3).broadcast_to([P, T, NG, 4]), ALU.mult))
                link(nc.vector.tensor_reduce(comb[:, :, :], cw[:, :, :, :].rearrange("p t g e -> p t e g"),
                                             X, ALU.add))
                link(nc.vector.tensor_reduce(den[:, :], comb[:, :, :], X, ALU.add))
                link(nc.vector.reciprocal(den[:, :], den[:, :]))
                link(tt(comb[:, :, :], comb[:, :, :], den[:, :].unsqueeze(2).broadcast_to([P, T, 4]), ALU.mult))
                link(tt(gpos[:, :, :], ghot[:, :, :], group_base.unsqueeze(1).broadcast_to([P, T, NG]), ALU.mult))
                link(nc.vector.tensor_reduce(gbase[:, :], gpos[:, :, :], X, ALU.add))
                link(ts(shift[:, :], gbase[:, :], -1.0, float((NG - 1) * P), ALU.mult, ALU.add))
                dve.wait_ge(rank_in_psum, L + 1)
                link(tt(gpos[:, :, :], ghot[:, :, :], psum[:, 2, 0:8].rearrange("p (t g) -> p t g", t=T), ALU.mult))
                link(nc.vector.tensor_reduce(pos[:, :], gpos[:, :, :], X, ALU.add))
                link(ts(over[:, :], pos[:, :], P - 0.5, None, ALU.is_gt))
                link(tt(over[:, :], over[:, :], shift[:, :], ALU.mult))
                link(tt(key[:, :], pos[:, :], gbase[:, :], ALU.add))
                link(tt(key[:, :], key[:, :], over[:, :], ALU.add))
                for t in range(T):
                    link(ts(pick[:, t, :], slot_no[:, :], key[:, t:t + 1], None, ALU.is_equal))
                dve.sem_inc(pick_ready, 1)
                link(ts(big[:, :], psum[:, 2, 8:12], P + 0.5, None, ALU.is_gt))
                link(tt(big[:, :], big[:, :], group_number, ALU.mult))
                link(nc.vector.tensor_reduce(bigmax[:, :], big[:, :], X, ALU.max))
                nc.vector.tensor_copy(flag[:, :], bigmax[:, :]).then_inc(flag_ready, 1)

            def save_gather(first):
                for q in range(2):
                    dve.wait_ge(xg_hi, first + q)
                    at = (slice(None), slice(4 * q, 4 * q + 4))
                    rest(xg[1][at], quad(q), xg[0][at]).then_inc(xg_ready, 1)

            def experts(L):
                n0, s0 = EPG * NG * L, starts[L][2]
                split_behind(starts[L][2])
                save_gather(10 * L + 1)
                for k in range(3):
                    dve.wait_ge(place_in_psum, 3 * L + k + 1)
                    n = 2 if k < 2 else 1
                    nc.vector.tensor_copy(place[:, 2 * k:2 * k + n, :],
                                          psum[:, 4 + k, 0:n * SEQ].rearrange("p (b n) -> p b n", b=n)
                                          ).then_inc(y_banks_free, 1)
                dve.wait_ge(cg_ready, L + 1)
                with dve.Fori(0, NG) as g:
                    def hidden(e):
                        k = n0 + e + 1 + EPG * g
                        s = hid[:, e % 2, :]
                        dve.wait_ge(sig_ready, k)
                        tt(s, s, psum[:, e % 2 * 2, :], ALU.mult).then_inc(silu_ready, 1)
                        dve.wait_ge(silu_ready, k)
                        dve.wait_ge(weights_used, expert_slots(L, UP_AT[e]) + W_SLOTS_GROUP * g)
                        stt(s, psum[:, e % 2 * 2 + 1, :], cg[:, bass.ds(4 * g + e, 1)], s,
                            ALU.mult, ALU.mult).then_inc(h_ready, 1)

                    def save_hT(e):
                        dve.wait_ge(ht_hi, n0 + e + 1 + EPG * g)
                        rest(hT[1][:, e % 2, :, :], quad(4), hT[0][:, e % 2, :, :]).then_inc(ht_ready, 1)

                    for m in range(W_SLOTS_GROUP):
                        if m in (3, 7, 13, 19):
                            hidden((3, 7, 13, 19).index(m))
                        if m in (5, 11, 17, 20):
                            save_hT((5, 11, 17, 20).index(m))
                        if m == 23:
                            for c in range(2):
                                cols = slice(c * NB, (c + 1) * NB)
                                dve.wait_ge(y_hi, 2 * NG * L + c + 1 + 2 * g)
                                rest(y[1][:, g, cols], psum[:, 6 + c, :], y[0][:, g, cols]
                                     ).then_inc(y_banks_free, 1)
                        split_slot(s0 + m + HIGH, W_SLOTS_GROUP * g)
                        if m == 19:
                            save_gather(10 * L + 3 + 2 * g)
                split[0] = starts[L][3] + HIGH
                for t in range(T):
                    dve.wait_ge(ffn_done, T * L + t + 1)
                    residual(t, 0)
                    dve.sem_inc(ffn_added, 1)
                dve.wait_ge(flag_ready, L + 1)
                crowded = dve.value_load(flag[0:1, 0:1], min_val=0, max_val=NG)
                with dve.If(crowded > 0):
                    o = ov[L]
                    for e in range(EPG):
                        for k in range(W_SLOTS_EXPERT * e, W_SLOTS_EXPERT * (e + 1)):
                            dve.wait_ge(o["split_hi"], k + 1)
                            rest(w_lo[:, k % RING, :], raw[:, k % RING, :], w_hi[:, k % HIGH, :]
                                 ).then_inc(o["split_lo"], 1)
                        s = hid[:, e % 2, :]
                        dve.wait_ge(o["sig"], e + 1)
                        tt(s, s, psum[:, 0, :], ALU.mult).then_inc(o["silu"], 1)
                        dve.wait_ge(o["silu"], e + 1)
                        dve.wait_ge(o["used"], W_SLOTS_EXPERT * e + 4)
                        stt(s, psum[:, 1, :], cg[:, 4 * NG + e:4 * NG + e + 1], s,
                            ALU.mult, ALU.mult).then_inc(o["h"], 1)
                        dve.wait_ge(o["ht_hi"], e + 1)
                        rest(hT[1][:, e % 2, :, :], quad(4), hT[0][:, e % 2, :, :]).then_inc(o["ht"], 1)
                    for c in range(2):
                        cols = slice(c * NB, (c + 1) * NB)
                        dve.wait_ge(o["y_hi"], c + 1)
                        rest(y[1][:, NG, cols], psum[:, 6 + c, :], y[0][:, NG, cols]).then_inc(o["y_saved"], 1)
                    for t in range(T):
                        dve.wait_ge(o["ffn"], t + 1)
                        for c in range(2):
                            xs = x[:, t, c * NB:(c + 1) * NB]
                            tt(xs, xs, psum[:, 2 * t + c, :], ALU.add).then_inc(o["added"], 1)
                    dve.wait_ge(o["added"], 2 * T)
                    for i, k in enumerate(range(starts[L][3], starts[L][3] + 4)):
                        dve.wait_ge(o["split_hi"], W_SLOTS_GROUP + i + 1)
                        rest(w_lo[:, k % RING, :], raw[:, k % RING, :], w_hi[:, k % HIGH, :]
                             ).then_inc(o["split_lo"], 1)

            split_behind(0)
            for L in range(DEPTH):
                transpose_x(3 * L)
                (conv_mixer, retention_mixer, sgu_mixer)[L % 3](L)
                for t in range(T):
                    wait_rows(dve, L, t, mix_done, L + 1, starts[L][1])
                    residual(t, 4)
                    layer_norm(t, 2 * L)
                transpose_x(3 * L + 1)
                split_behind(starts[L][1])
                route(L)
                experts(L)
                for t in range(T):
                    layer_norm(t, 2 * L + 1)
                transpose_x(3 * L + 2)
                split_behind(starts[L][3] + 3)
                dve.wait_ge(bg_loaded, 16 * (L + 1))
                for t in range(T):
                    wait_rows(dve, L, t, ple_done, L + 1, starts[L][3] + 4)
                    for c in range(2):
                        cols = slice(c * NB, (c + 1) * NB)
                        link(tt(ple[:, t, cols], psum[:, 4 + 2 * t + c, :], bgate[:, cols], ALU.add))
                    dve.sem_inc(ple_arg, 1)
                for t in range(T):
                    dve.wait_ge(ple_sig, 2 * L + t + 1)
                    link(tt(ple[:, t, :], ple[:, t, :], emb[:, t, :], ALU.mult))
                    tt(x[:, t, :], x[:, t, :], ple[:, t, :], ALU.add).then_inc(x_tile_ready, 1)
                split_behind(starts[L][3] + 4)


def kernel(**inputs):
    import concourse.bacc as bacc
    from concourse.bass_utils import run_bass_kernel_spmd

    nc = bacc.Bacc("TRN2", target_bir_lowering=False, num_devices=1)
    arrays = {n: np.ascontiguousarray(a) for n, a in inputs.items()}
    arrays.update(shape_constants())
    aps, feed = {}, {}
    for name, a in arrays.items():
        feed[f"in_{name}"] = a
        aps[name] = nc.dram_tensor(f"in_{name}", a.shape, mybir.dt.from_np(a.dtype), kind="ExternalInput").ap()
    out = nc.dram_tensor("out", (1, SEQ, D), mybir.dt.float32, kind="ExternalOutput").ap()
    build(nc, aps, out)
    r = run_bass_kernel_spmd(nc, [feed], core_ids=[0])
    return r.results[0]["out"]
```

```python
import numpy as np
import concourse.bass as bass
from concourse import mybir
from contextlib import ExitStack

P = 128
D = 1024
SEQ = 256
T = SEQ // P
DEPTH = 4
KD = D // P
NB = 512
HEADS, DK, DV = 4, 256, 512
VD = HEADS * DV
SGU, SGROUPS = 3 * D, 4
SGD = SGU // SGROUPS
SVB = SGD // 2
NE, NG, EPG = 16, 4, 4
FE = D // 2
PLE = 256
NBLK = NG + 1
ALPHA = float((2 * DEPTH) ** 0.25)
LN_EPS = 1e-5
RING = 6
HIGH = 4
SLOT = 4 * NB
W_SLOTS_EXPERT = 6
W_SLOTS_GROUP = EPG * W_SLOTS_EXPERT
MIXER_SLOTS = {0: (2 * 3 * D // NB, 4), 1: (2 * (2 * D + 2 * VD) // NB, 2 * VD // NB),
               2: (2 * 2 * SGU // NB, 2 * SGU // NB)}


def slot_starts():
    at, out = 0, []
    for layer in range(DEPTH):
        mixer = at
        at += sum(MIXER_SLOTS[layer % 3])
        proj, experts = at, at + 1
        at = experts + NG * W_SLOTS_GROUP
        out.append((mixer, proj, experts, at))
        at += 4
    return out


def shape_constants():
    f = np.float32
    pos = np.arange(SEQ, dtype=f)
    inv = (1.0 / (f(10000.0) ** np.linspace(0.0, 1.0, DK // 2, dtype=f))).astype(f)
    ang = pos[:, None] * inv[None, :]
    rot = np.stack([np.cos(ang), np.sin(ang)], 1).astype(f)
    rot = rot.reshape(T, P, 2, DK // 2).transpose(1, 0, 2, 3).copy()
    lg = np.log(1.0 - 2.0 ** (-5.0 - np.arange(HEADS)))[:, None, None]
    s, c = np.arange(P)[:, None], np.arange(P)[None, :]
    diag = np.where(c >= s, np.exp(lg * np.maximum(c - s, 0)), 0.0)
    cross = np.exp(lg * (P + c - s))
    decay = (np.concatenate([diag, cross], 2) * DK ** -0.5).astype(f).transpose(1, 0, 2).copy()
    lower = (np.arange(4)[None, :] < np.arange(4)[:, None]).astype(f).reshape(1, 16)
    number = np.arange(4, dtype=f)[None]
    small = np.concatenate([lower, P * number, 1 + number, number, number], 1)
    return {
        "identity": np.eye(P, dtype=f),
        "before": (s < c).astype(f),
        "causal": (c <= s).astype(f),
        "slot_number": np.broadcast_to(np.arange(NBLK * P, dtype=f), (P, NBLK * P)).copy(),
        "rotary": rot,
        "decay": decay,
        "small": np.broadcast_to(small, (P, 32)).copy(),
    }


def build(nc, A, out):
    F = mybir.dt.float32
    FR = mybir.dt.float32r
    I32 = mybir.dt.int32
    ALU = mybir.AluOpType
    ACT = mybir.ActivationFunctionType
    X = mybir.AxisListType.X
    starts = slot_starts()

    ctx = ExitStack()
    with ctx:
        def sb(name, *shape, dt=F):
            return ctx.enter_context(nc.sbuf_tensor(name, [P, *shape], dt))

        def sem(name):
            return ctx.enter_context(nc.semaphore(name))

        WORK = 18432
        sb("arena", WORK + RING * SLOT + T * D)
        arena_at = nc.sbuf_base - 4 * (WORK + RING * SLOT + T * D)

        def arena(name, offset, *shape, dt=F):
            return nc.alloc_sbuf_tensor_at(name, [P, *shape], dt, offset=arena_at + 4 * offset)

        work, work_r = arena("work", 0, WORK), arena("work_r", 0, WORK, dt=FR)
        raw, w_lo = arena("raw", WORK, RING, SLOT), arena("w_lo", WORK, RING, SLOT, dt=FR)
        w_hi = sb("w_hi", HIGH, SLOT, dt=FR)
        x = sb("x", T, D)
        xT = [sb("xT_hi", KD, SEQ, dt=FR), sb("xT_lo", KD, SEQ, dt=FR)]
        emb, emb_r = arena("emb", WORK + RING * SLOT, T, D), arena("emb_r", WORK + RING * SLOT, T * D, dt=FR)
        ln_par = sb("ln_par", 2, D)
        bgate = sb("bgate", D)
        ident = sb("ident", P)
        before = sb("before", P)
        causal = sb("causal", P)
        ones = sb("ones", P)
        slot_no = sb("slot_no", NBLK * P)
        small = sb("small", 32)
        rw = sb("rw", KD, NE)
        rw_pad = sb("rw_pad", KD, P, dt=FR)
        fold = sb("fold", NE)
        rb = sb("rb", NE)
        conv_w = sb("conv_w", 2, 3, KD)
        sgu_b = sb("sgu_b", SGROUPS)
        stats = sb("stats", T, 6, 6)
        nstat = sb("nstat", 8, 6)
        nmv = sb("nmv", 4, 2)
        nvar, nsq, nrstd = sb("nvar", 4), sb("nsq", 4), sb("nrstd", 4)
        score = sb("score", T, NE)
        sel = sb("sel", T, NE)
        cnt = sb("cnt", T * NG, 4)
        gscore = sb("gscore", T, NG)
        gcnt = sb("gcnt", T, NG)
        ghot = sb("ghot", T, NG)
        cw = sb("cw", T, NG, 4)
        den = sb("den", T)
        comb = sb("comb", T, 4)
        gpos = sb("gpos", T, NG)
        full = sb("full", T)
        gbase = sb("gbase", T)
        over = sb("over", T)
        shift = sb("shift", T)
        key = sb("key", T)
        big = sb("big", 4)
        table = sb("table", 1)
        bigmax = sb("bigmax", 1)
        flag = sb("flag", 1, dt=I32)
        cg = sb("cg", 4 * NBLK)
        psum = ctx.enter_context(nc.psum_tensor("psum", [P, 8, NB], F))

        def view(start, size, pattern, of=work, **dims):
            return of[:, start:start + size].rearrange(pattern, **dims)

        def pair(hi, lo, size, pattern, **dims):
            return [view(a, size, pattern, of=work_r, **dims) for a in (hi, lo)]

        bch = view(0, T * 3 * D, "p (t n) -> p t n", t=T)
        zT = view(6144, KD * (SEQ + 2), "p (j n) -> p j n", j=KD)
        bT = view(8208, KD * SEQ, "p (j n) -> p j n", j=KD)
        conv = view(10256, KD * SEQ, "p (j n) -> p j n", j=KD)
        gT = pair(12304, 14352, KD * SEQ, "p (j n) -> p j n", j=KD)
        qk = view(0, T * 2 * D, "p (t n) -> p t n", t=T)
        rv = view(4096, T * VD, "p (t n) -> p t n", t=T)
        rg = view(8192, T * VD, "p (t n) -> p t n", t=T)
        turned = [view(12288 + D * i, D, "p (h n) -> p h n", h=2 * HEADS) for i in range(3)]
        qkT = view(12288, 2 * KD * SEQ, "p (a j n) -> p a j n", a=2, j=KD)
        sT = view(16384, HEADS * 3 * P, "p (h n) -> p h n", h=HEADS)
        rot = view(17920, T * DK, "p (t a n) -> p t a n", t=T, a=2)
        oT = pair(0, 12288, VD // P * SEQ, "p (j n) -> p j n", j=VD // P)
        su = view(0, T * SGU, "p (t n) -> p t n", t=T)
        sv = view(6144, T * SGU, "p (t n) -> p t n", t=T)
        c_ln = view(12288, 2 * SGU, "p (a n) -> p a n", a=2)
        uvT = [view(12288, T * SGU, "p (j t n) -> p j t n", of=work_r, t=T, n=P),
               view(6144, T * SGU, "p (t j n) -> p j t n", of=work_r, t=T, n=P)]
        pick = view(0, T * NBLK * P, "p (t n) -> p t n", t=T)
        place = view(1280, NBLK * SEQ, "p (b n) -> p b n", of=work_r, b=NBLK)
        xg = pair(2560, 3584, KD * P, "p (j n) -> p j n", j=KD)
        y = pair(4608, 9728, NBLK * D, "p (b n) -> p b n", b=NBLK)
        hid = view(14848, 2 * FE, "p (a n) -> p a n", a=2)
        hT = pair(15872, 16896, 2 * FE, "p (a j n) -> p a j n", a=2, j=4)
        logitsT = view(2560, SEQ, "p n -> p n")
        cmp1, cmp2 = [view(a, T * NG * 16, "p (r i j) -> p r i j", i=4, j=4) for a in (2816, 2944)]
        ple = view(0, T * D, "p (t n) -> p t n", t=T)
        sgu_w = emb[:, 0, 0:512].rearrange("p (g s) -> p g s", g=SGROUPS)
        sgu_wT = emb[:, 0, 512:1024].rearrange("p (g s) -> p g s", g=SGROUPS)
        decay = emb[:, 0, :].rearrange("p (h n) -> p h n", h=HEADS)
        p_in = emb[:, 1, 0:T * PLE].rearrange("p (t n) -> p t n", t=T)
        pT = [emb_r[:, D + 512 * i:D + 512 * (i + 1)].rearrange("p (j n) -> p j n", j=2) for i in (1, 0)]

        s_const = sem("constants_loaded")
        s_x = [sem(f"x_loaded{t}") for t in range(T)]
        s_ident = sem("identity_loaded")
        hi_ready, lo_ready = sem("hi_ready"), sem("lo_ready")
        rw_zeroed, logitsT_in_psum, logitsT_ready = (sem("rw_zeroed"), sem("logitsT_in_psum"),
                                                     sem("logitsT_ready"))
        rw_hi_ready, rw_ready = sem("rw_hi_ready"), sem("rw_ready")
        xt_hi = sem("xt_hi")
        pt_hi, xg_hi, ht_hi, y_hi = sem("pt_hi"), sem("xg_hi"), sem("ht_hi"), sem("y_hi")
        oT_hi = sem("oT_hi")
        s_ones, comb_ready = sem("ones_set"), sem("comb_ready")
        slot_full = [sem(f"slot_full{i}") for i in range(RING)]
        weights_used = sem("weights_used")
        xt_in_psum, xt_ready = sem("xt_in_psum"), sem("xt_ready")
        x_tile_ready = sem("x_tile_ready")
        mix_done, mix_read = sem("mix_done"), sem("mix_read")
        dve_step = sem("dve_step")
        p_loaded, lnp_loaded, bg_loaded = sem("p_loaded"), sem("lnp_loaded"), sem("bg_loaded")
        pt_in_psum, pt_ready = sem("pt_in_psum"), sem("pt_ready")
        logits_done, score_ready = sem("logits_done"), sem("score_ready")
        emb_in_psum, emb_ready = sem("emb_in_psum"), sem("emb_ready")
        ghot_ready, rank_in_psum = sem("ghot_ready"), sem("rank_in_psum")
        flag_ready, pick_ready = sem("flag_ready"), sem("pick_ready")
        xg_in_psum, xg_ready = sem("xg_in_psum"), sem("xg_ready")
        cg_in_psum, cg_ready = sem("cg_in_psum"), sem("cg_ready")
        place_in_psum, y_banks_free = sem("place_in_psum"), sem("y_banks_free")
        sig_ready, silu_ready, h_ready = sem("sig_ready"), sem("silu_ready"), sem("h_ready")
        ht_in_psum, ht_ready = sem("ht_in_psum"), sem("ht_ready")
        ffn_done = sem("ffn_done")
        ple_done, ple_arg, ple_sig = sem("ple_done"), sem("ple_arg"), sem("ple_sig")
        proj_in_psum = [sem(f"proj_in_psum{i}") for i in range(DEPTH)]
        proj_ready = [sem(f"proj_ready{i}") for i in range(DEPTH)]
        z_ready = {i: sem(f"z_ready{i}") for i in range(0, DEPTH, 3)}
        mt_in_psum = [sem(f"mixT_in_psum{i}") for i in range(DEPTH)]
        mt_ready = [sem(f"mixT_ready{i}") for i in range(DEPTH)]
        conv_ready = {i: sem(f"conv_ready{i}") for i in range(0, DEPTH, 3)}
        conv_hi = {i: sem(f"conv_hi{i}") for i in range(0, DEPTH, 3)}
        gT_ready = {i: sem(f"gT_ready{i}") for i in range(0, DEPTH, 3)}
        tap_ready = {i: sem(f"tap_ready{i}") for i in range(0, DEPTH, 3)}
        pad_ready = {i: sem(f"pad_ready{i}") for i in range(0, DEPTH, 3)}
        uv_hi, b_loaded, sw_loaded = sem("uv_hi"), sem("b_loaded"), sem("sw_loaded")
        g_ready, qk_ready = sem("g_ready"), sem("qk_ready")
        score_in_psum, sT_ready = sem("scores_in_psum"), sem("sT_ready")
        o_in_psum, o_ready = sem("o_in_psum"), sem("o_ready")
        oT_in_psum, oT_ready = sem("oT_in_psum"), sem("oT_ready")
        c_loaded, sw_masked, sw_in_psum, sw_ready = (sem("c_loaded"), sem("sw_masked"),
                                                     sem("sw_in_psum"), sem("sw_ready"))
        v_ready, vs_in_psum, uv_ready = sem("v_ready"), sem("vs_in_psum"), sem("uv_ready")
        s_out = sem("out_stored")
        OV = ["full", "split_hi", "split_lo", "ht_hi", "y_hi", "used", "sig", "silu", "h", "ht_in_psum", "ht", "y_saved"]
        ov = [{n: sem(f"over_{n}{i}") for n in OV} for i in range(DEPTH)]
        N_CONST = 9

        block = ctx.enter_context(nc.Block())

        def wait_block(eng, L, b, t, tile0):
            if t == 0:
                eng.wait_ge(tile0, b + 1)
            else:
                eng.wait_ge(weights_used, starts[L][0] + 2 * (b + 1))

        def wait_rows(eng, L, t, tile0, count, end):
            if t == 0:
                eng.wait_ge(tile0, count)
            else:
                eng.wait_ge(weights_used, end)

        def group_jobs(q):
            return [(2 * q + i, t) for t in range(T) for i in range(2)]

        def expert_slots(L, i):
            return starts[L][2] + 2 * (i + 1)

        GATE_AT, UP_AT, LAST_AT = (0, 2, 5, 8), (1, 3, 6, 9), 11

        @block.sync
        def _(sp):
            def load(n, src):
                if n >= RING:
                    sp.wait_ge(weights_used, n - RING + 1)
                sp.dma_start(raw[:, n % RING, :], src).then_inc(slot_full[n % RING], 16)

            def load_columns(n, w, order):
                v = w.rearrange("(p j) n -> p j n", j=KD)
                for b in order:
                    for half in range(2):
                        if n >= RING:
                            sp.wait_ge(weights_used, n - RING + 1)
                        sp.dma_start(raw[:, n % RING, :].rearrange("p (j n) -> p j n", j=4),
                                     v[:, 4 * half:4 * half + 4, b * NB:(b + 1) * NB]
                                     ).then_inc(slot_full[n % RING], 16)
                        n += 1
                        if n == 2:
                            load_x(1)
                return n

            def load_x(t):
                sp.dma_start(x[:, t, :], A["x"][0, t * P:(t + 1) * P, :]).then_inc(s_x[t], 16)

            sp.dma_start(ident[:, :], A["identity"]).then_inc(s_ident, 16)
            load_x(0)
            for L in range(DEPTH):
                n, n_proj, n_exp, n_gate = starts[L]
                if L % 3 == 0:
                    n = load_columns(n, A["a_w_in"][L // 3], [2, 3, 4, 5, 0, 1])
                    v = A["a_w_out"][L // 3].rearrange("(p j) n -> p (j n)", j=KD)
                    for i in range(4):
                        load(n + i, v[:, i * SLOT:(i + 1) * SLOT])
                elif L % 3 == 1:
                    n = load_columns(n, A["b_w_in"][L // 3], range(12))
                    v = A["b_w_out"][L // 3].rearrange("(s p j) n -> s p (j n)", p=P, j=4)
                    for i in range(2 * VD // NB):
                        load(n + i, v[i // 2, :, i % 2 * SLOT:(i % 2 + 1) * SLOT])
                else:
                    n = load_columns(n, A["c_w_in"][L // 3], [*range(6, 12), *range(6)])
                    v = A["c_w_out"][L // 3].rearrange("(s p j) n -> s p (j n)", p=P, j=4)
                    for i in range(2 * SGU // NB):
                        load(n + i, v[i // 2, :, i % 2 * SLOT:(i % 2 + 1) * SLOT])
                load(n_proj, A["ple_w_proj"][L].rearrange("(p j) n -> p (j n)", j=2))
                wg = A["moe_w_gate"][L].rearrange("(g e) (p j) n -> g e p (j n)", g=NG, j=KD)
                wu = A["moe_w_up"][L].rearrange("(g e) (p j) n -> g e p (j n)", g=NG, j=KD)
                wd = A["moe_w_down"][L].rearrange("(g e) (p j) n -> g e p (j n)", g=NG, j=4)
                order = [(wg, 0), (wu, 0), (wg, 1), (wu, 1), (wd, 0), (wg, 2), (wu, 2), (wd, 1),
                         (wg, 3), (wu, 3), (wd, 2), (wd, 3)]
                with sp.Fori(0, NG) as g:
                    for i, (w, e) in enumerate(order):
                        for half in range(2):
                            k = n_exp + 2 * i + half
                            sp.wait_ge(weights_used, k - RING + 1 + W_SLOTS_GROUP * g)
                            sp.dma_start(raw[:, k % RING, :], w[g, e, :, half * SLOT:(half + 1) * SLOT]
                                         ).then_inc(slot_full[k % RING], 16)
                v = A["ple_w_gate"][L].rearrange("(p j) n -> p (j n)", j=KD)
                for i in range(4):
                    load(n_gate + i, v[:, i * SLOT:(i + 1) * SLOT])
                sp.wait_ge(flag_ready, L + 1)
                crowded = sp.value_load(flag[0:1, 0:1], min_val=0, max_val=NG)
                with sp.If(crowded > 0):
                    group = sp.value_load(flag[0:1, 0:1], min_val=1, max_val=NG)
                    sp.wait_ge(weights_used, n_gate)
                    sp.wait_ge(lo_ready, n_gate + 4)
                    for e in range(EPG):
                        if e:
                            sp.wait_ge(ov[L]["used"], W_SLOTS_EXPERT * e)
                        for i, w in enumerate((wg, wu, wd)):
                            for half in range(2):
                                sp.dma_start(raw[:, 2 * i + half, :],
                                             w[group - 1, e, :, half * SLOT:(half + 1) * SLOT]
                                             ).then_inc(ov[L]["full"], 16)
                    sp.wait_ge(ov[L]["used"], W_SLOTS_GROUP)
                    for i in range(4):
                        sp.dma_start(raw[:, (n_gate + i) % RING, :], v[:, i * SLOT:(i + 1) * SLOT]
                                     ).then_inc(ov[L]["full"], 16)
            for t in range(T):
                sp.wait_ge(x_tile_ready, 2 * (3 * DEPTH - 1) + t + 1)
                sp.dma_start(out[0, t * P:(t + 1) * P, :], x[:, t, :]).then_inc(s_out, 16)
            sp.wait_ge(s_out, 16 * T)

        @block.gpsimd
        def _(pool):
            nc.gpsimd.memset(ones[:, :], 1.0).then_inc(s_ones, 1)
            loads = [(before[:, :], A["before"]),
                     (causal[:, :], A["causal"]), (slot_no[:, :], A["slot_number"]),
                     (small[:, :], A["small"]),
                     (rw[:, :, :], A["router_w"].rearrange("(p j) e -> p j e", j=KD)),
                     (rb[:, :], A["router_b"].partition_broadcast(P)),
                     (sgu_b[:, :], A["c_b_s"][0].rearrange("g t -> t g"))]
            loads += [(conv_w[:, i, :, :], A["a_conv_w"][i].rearrange("w (p j) -> p w j", j=KD))
                      for i in range(2)]
            assert len(loads) == N_CONST
            pool.dma_start(p_in, A["p"][0, 0].rearrange("(t p) d -> p t d", p=P)).then_inc(p_loaded, 16)
            for dst, src in loads:
                pool.dma_start(dst, src, allow_slow_non_contiguous=True).then_inc(s_const, 16)
            def load_norm(L, i):
                pool.dma_start(ln_par[:, 0, :], A["ln_g"][L, i].partition_broadcast(P)).then_inc(lnp_loaded, 16)
                pool.dma_start(ln_par[:, 1, :], A["ln_b"][L, i].partition_broadcast(P)).then_inc(lnp_loaded, 16)

            load_norm(0, 0)
            for L in range(DEPTH):
                if L % 3 == 2:
                    pool.wait_ge(x_tile_ready, 6 * L - 1)
                    pool.dma_start(sgu_w, A["c_w_s"][0].rearrange("g t s -> t g s")).then_inc(sw_loaded, 16)
                if L:
                    pool.wait_ge(x_tile_ready, 6 * L)
                    pool.dma_start(p_in, A["p"][L, 0].rearrange("(t p) d -> p t d", p=P)).then_inc(p_loaded, 16)
                pool.dma_start(bgate[:, :], A["ple_b_gate"][L].partition_broadcast(P)).then_inc(bg_loaded, 16)
                if L % 3 == 1:
                    pool.dma_start(rot, A["rotary"]).then_inc(b_loaded, 16)
                    pool.dma_start(decay, A["decay"]).then_inc(b_loaded, 16)
                if L % 3 == 2:
                    for a, name in enumerate(("c_ln_g", "c_ln_b")):
                        pool.dma_start(c_ln[:, a, :], A[name][0].partition_broadcast(P)).then_inc(c_loaded, 16)
                pool.wait_ge(x_tile_ready, 6 * L + 2)
                load_norm(L, 1)
                if L + 1 < DEPTH:
                    pool.wait_ge(x_tile_ready, 6 * L + 4)
                    load_norm(L + 1, 0)

        @block.tensor
        def _(pe):
            mm = nc.tensor.matmul

            def quarters(n):
                return (w_hi[:, n % HIGH, :].rearrange("p (j n) -> p j n", j=4),
                        w_lo[:, n % RING, :].rearrange("p (j n) -> p j n", j=4))

            def slot(n):
                pe.wait_ge(lo_ready, n + 1)
                return quarters(n)

            def product(out, lhs, rhs, start, stop):
                mm(out, lhs[0], rhs[0], start=start, stop=False)
                mm(out, lhs[0], rhs[1], start=False, stop=False)
                return mm(out, lhs[1], rhs[0], start=False, stop=stop)

            def part(v, *at):
                return [a[at] for a in v]

            ALL = slice(None)

            def transpose4(bank, chunks):
                for i, c in enumerate(chunks):
                    last = nc.tensor.transpose(psum[:, bank, i * P:(i + 1) * P], c, ident[:, :])
                return last

            def transpose_tile(k, t):
                if k == 0:
                    pe.wait_ge(s_x[t], 16)
                else:
                    pe.wait_ge(x_tile_ready, 2 * (k - 1) + t + 1)
                v = x[:, t, :].rearrange("p (c j) -> p j c", j=KD)
                for q in range(2):
                    transpose4(4 + 2 * t + q, [v[:, 4 * q + i, :] for i in range(4)]).then_inc(xt_in_psum, 1)

            def turned_tile(k, t):
                pe.wait_ge(xt_ready, 4 * k + 2 * (t + 1))

            def turn_p(L):
                pe.wait_ge(p_loaded, 16 * (L + 1))
                for t in range(T):
                    v = p_in[:, t, :].rearrange("p (c j) -> p j c", j=2)
                    for j in range(2):
                        last = nc.tensor.transpose(psum[:, 2, j * SEQ + t * P:j * SEQ + (t + 1) * P],
                                                   v[:, j, :], ident[:, :])
                last.then_inc(pt_in_psum, 1)


            def project_slot(L, q, t, i):
                n = starts[L][0] + 4 * q + i
                c, half = divmod(i, 2)
                if half == 0 and q:
                    pe.wait_ge(proj_ready[L], 4 * (q - 1) + 2 * t + c + 1)
                    if L % 3 == 1 and q == 5:
                        pe.wait_ge(g_ready, 2 * t + c + 1)
                w = slot(n)
                for j in range(4):
                    last = product(psum[:, 2 * t + c, :], part(xT, ALL, 4 * half + j, bass.ts(t, P)),
                                   part(w, ALL, j), half == 0 and j == 0, half == 1 and j == 3)
                if t == 1:
                    last.then_inc(weights_used, 1)
                elif half == 1:
                    last.then_inc(proj_in_psum[L], 1)

            def project_group(L, q):
                for t in range(T):
                    for i in range(4):
                        project_slot(L, q, t, i)

            def first_group(L):
                turned_tile(3 * L, 0)
                for i in range(4):
                    if i == 3:
                        transpose_tile(3 * L, 1)
                        turn_p(L)
                        if L % 3 == 2:
                            pe.wait_ge(sw_masked, 1)
                            transpose4(3, [sgu_w[:, g, :] for g in range(SGROUPS)]).then_inc(sw_in_psum, 1)
                    project_slot(L, 0, 0, i)
                turned_tile(3 * L, 1)
                pe.wait_ge(pt_ready, L + 1)
                if L % 3 == 2:
                    pe.wait_ge(sw_ready, 1)
                for i in range(4):
                    project_slot(L, 0, 1, i)

            def rows_slot(n, count, lhs, q, t, i, done):
                s = 4 * q + i
                w = slot(n + s)
                for j in range(2):
                    for c in range(2):
                        last = product(psum[:, 2 * t + c, :], part(lhs, ALL, 2 * s + j, t),
                                       part(w, ALL, 2 * j + c), s == 0 and j == 0, s == count - 1 and j == 1)
                if t == 1:
                    last.then_inc(weights_used, 1)
                elif s == count - 1:
                    last.then_inc(done, 1)

            xv = [a[:, :, :] for a in xT]

            def tiled(v):
                return [a.rearrange("p j (t n) -> p j t n", t=T) for a in v]

            def rows_group(n, count, lhs, q, t, done):
                for i in range(min(4, count)):
                    rows_slot(n, count, lhs, q, t, i, done)

            def last_group(L, n, count, lhs, q, first=0):
                for i in range(first, 4):
                    if i == 3:
                        transpose_tile(3 * L + 1, 0)
                    rows_slot(n, count, lhs, q, 1, i, mix_done)

            def conv_mixer(L):
                n = starts[L][0] + 12
                first_group(L)
                project_group(L, 1)
                for i in range(4):
                    if i == 2:
                        for t in range(T):
                            pe.wait_ge(z_ready[L], t + 1)
                            v = bch[:, t, D:2 * D].rearrange("p (c j) -> p j c", j=KD)
                            for q in range(2):
                                transpose4(4 + 2 * t + q, [v[:, 4 * q + k, :] for k in range(4)]
                                           ).then_inc(mt_in_psum[L], 1)
                    project_slot(L, 2, 0, i)
                for i in range(4):
                    project_slot(L, 2, 1, i)
                for t in range(T):
                    pe.wait_ge(proj_ready[L], 8 + 2 * (t + 1))
                    pe.wait_ge(mt_ready[L], 4)
                    v = bch[:, t, 0:D].rearrange("p (c j) -> p j c", j=KD)
                    for q in range(2):
                        transpose4(4 + 2 * t + q, [v[:, 4 * q + k, :] for k in range(4)]
                                   ).then_inc(mt_in_psum[L], 1)
                for t in range(T):
                    pe.wait_ge(gT_ready[L], 2 * (t + 1))
                    rows_slot(n, 4, tiled(gT), 0, t, 0, mix_done)
                for i in range(1, 4):
                    rows_slot(n, 4, tiled(gT), 0, 0, i, mix_done)
                last_group(L, n, 4, tiled(gT), 0, first=1)

            def retention_mixer(L):
                n = starts[L][0] + 24

                def turn_qk(src):
                    for k in range(4 * src, 4 * src + 4):
                        t, q = k // 2 % 2, k % 2
                        pe.wait_ge(qk_ready, t + 1)
                        if k >= 4:
                            pe.wait_ge(mt_ready[L], k - 3)
                        c0 = src * D + q * NB
                        transpose4(4 + k % 4, [qk[:, t, c0 + i * P:c0 + (i + 1) * P] for i in range(4)]
                                   ).then_inc(mt_in_psum[L], 1)

                def scores():
                    pe.wait_ge(mt_ready[L], 8)
                    for h in range(HEADS):
                        for half in range(2):
                            mm(psum[:, 4 + h, 0:2 * P], qkT[:, 1, 2 * h + half, 0:P],
                               qkT[:, 0, 2 * h + half, 0:2 * P], start=half == 0, stop=half == 1)
                        for half in range(2):
                            last = mm(psum[:, 4 + h, 2 * P:3 * P], qkT[:, 1, 2 * h + half, P:2 * P],
                                      qkT[:, 0, 2 * h + half, P:2 * P], start=half == 0, stop=half == 1)
                        last.then_inc(score_in_psum, 1)

                def attend(k):
                    h, c = divmod(k, 2)
                    if k < 4:
                        pe.wait_ge(sT_ready, HEADS)
                    else:
                        pe.wait_ge(oT_ready, k - 3)
                    for s in range(c + 1):
                        last = mm(psum[:, 4 + k % 4, :], sT[:, h, (c + s) * P:(c + s + 1) * P],
                                  rv[:, s, h * DV:(h + 1) * DV], start=s == 0, stop=s == c)
                    last.then_inc(o_in_psum, 1)

                def turn(k):
                    h, c = divmod(k, 2)
                    pe.wait_ge(o_ready, k + 1)
                    v = rg[:, c, h * DV:(h + 1) * DV].rearrange("p (c j) -> p j c", j=4)
                    transpose4(4 + k % 4, [v[:, i, :] for i in range(4)]).then_inc(oT_in_psum, 1)

                first_group(L)
                for q in range(1, 6):
                    for t in range(T):
                        for i in range(4):
                            project_slot(L, q, t, i)
                        if q == 3:
                            turn_qk(t)
                        elif (q, t) == (4, 0):
                            scores()
                        elif (q, t) == (4, 1):
                            for k in range(4):
                                attend(k)
                        elif (q, t) == (5, 0):
                            for k in range(4):
                                turn(k)
                for k in range(4, 8):
                    attend(k)
                pe.wait_ge(oT_ready, 4)
                pe.wait_ge(proj_ready[L], 24)
                pe.wait_ge(g_ready, 8)
                rows_group(n, 8, tiled(oT), 0, 0, mix_done)
                for i in range(4):
                    if i == 3:
                        for k in range(4, 8):
                            turn(k)
                    rows_slot(n, 8, tiled(oT), 0, 1, i, mix_done)
                pe.wait_ge(oT_ready, 8)
                rows_group(n, 8, tiled(oT), 1, 0, mix_done)
                last_group(L, n, 8, tiled(oT), 1)

            def sgu_mixer(L):
                n = starts[L][0] + 24

                def spatial(m):
                    for k in range(4 * m, 4 * m + 4):
                        b, c = divmod(k, 2)
                        pe.wait_ge(v_ready, 6 + -(-(b + 1) * SVB // NB))
                        if m == 2:
                            pe.wait_ge(mt_ready[L], k - 7)
                        elif m == 3:
                            pe.wait_ge(mt_ready[L], k - 7)
                        elif m:
                            pe.wait_ge(uv_ready, k - 3)
                        mm(psum[:, 4 + k % 4, 0:SVB], sgu_wT[:, b // 2, :], sv[:, c, b * SVB:(b + 1) * SVB],
                           start=True, stop=True).then_inc(vs_in_psum, 1)

                def turn(m):
                    pe.wait_ge(uv_ready, (8, 12, 16)[m])
                    for k in range(4 * m, 4 * m + 4):
                        s, t = divmod(k, 2)
                        v = su[:, t, s * NB:(s + 1) * NB].rearrange("p (c j) -> p j c", j=4)
                        transpose4(4 + k % 4, [v[:, i, :] for i in range(4)]).then_inc(mt_in_psum[L], 1)

                first_group(L)
                for q in range(1, 6):
                    for t in range(T):
                        for i in range(4):
                            project_slot(L, q, t, i)
                        if (q, t) == (4, 1):
                            spatial(0)
                        elif (q, t) == (5, 0):
                            spatial(1)
                pe.wait_ge(proj_ready[L], 24)
                turn(0)
                for q in range(2):
                    pe.wait_ge(mt_ready[L], 4 * (q + 1))
                    rows_group(n, 12, uvT, q, 0, mix_done)
                    spatial(q + 2)
                    for i in range(4):
                        if i == 3:
                            turn(q + 1)
                        rows_slot(n, 12, uvT, q, 1, i, mix_done)
                pe.wait_ge(mt_ready[L], 12)
                rows_group(n, 12, uvT, 2, 0, mix_done)
                last_group(L, n, 12, uvT, 2)

            def route(L):
                def logits(t):
                    for i in range(2):
                        for j in range(KD):
                            last = mm(psum[:, 4, t * P:(t + 1) * P], rw_pad[:, j, :],
                                      xT[i][:, j, t * P:(t + 1) * P],
                                      start=i == 0 and j == 0, stop=i == 1 and j == KD - 1)
                    return last

                pe.wait_ge(rw_ready, 1)
                turned_tile(3 * L + 1, 0)
                logits(0)
                rows_group(starts[L][1], 1, tiled(pT), 0, 0, emb_in_psum)
                pe.wait_ge(mix_read, L + 1)
                rows_group(starts[L][1], 1, tiled(pT), 0, 1, emb_in_psum)
                transpose_tile(3 * L + 1, 1)
                turned_tile(3 * L + 1, 1)
                logits(1).then_inc(logitsT_in_psum, 1)
                pe.wait_ge(logitsT_ready, L + 1)
                for t in range(T):
                    last = mm(psum[:, 6, t * NE:(t + 1) * NE], logitsT[:, t * P:(t + 1) * P], fold[:, :],
                              start=True, stop=True)
                last.then_inc(logits_done, 1)
                mm(psum[:, 5, 0:8], ones[:, :], small[:, 24:32], start=True, stop=False)
                pe.wait_ge(ghot_ready, L + 1)
                mm(psum[:, 5, 4:8], ones[:, :], ghot[:, 0, :], start=False, stop=False)
                mm(psum[:, 5, 0:8], before[:, :], ghot[:, :, :], start=False, stop=True
                   ).then_inc(rank_in_psum, 1)
                mm(psum[:, 7, 0:4], ones[:, :], ghot[:, 0, :], start=True, stop=False)
                mm(psum[:, 7, 0:4], ones[:, :], ghot[:, 1, :], start=False, stop=True
                   ).then_inc(rank_in_psum, 1)

            def gather(block):
                for q in range(2):
                    for i in range(4):
                        for t in range(T):
                            v = x[:, t, :].rearrange("p (c j) -> p j c", j=KD)
                            last = mm(psum[:, q, i * P:(i + 1) * P], v[:, 4 * q + i, :],
                                      pick[:, t, bass.ts(block, P)], start=t == 0, stop=t == T - 1)
                    last.then_inc(xg_in_psum, 1)

            def wide(bank, w, half):
                for i in range(4):
                    last = product(psum[:, bank, :], part(xg, ALL, 4 * half + i), part(w, ALL, i),
                                   half == 0 and i == 0, half == 1 and i == 3)
                return last

            def turn_hidden(e):
                v = hid[:, e % 2, :].rearrange("p (c j) -> p j c", j=4)
                return transpose4(4, [v[:, i, :] for i in range(4)])

            def down(e, w, half):
                for i in range(2):
                    for c in range(2):
                        last = product(psum[:, 6 + c, :], part(hT, ALL, e % 2, 2 * half + i),
                                       part(w, ALL, 2 * i + c), e == 0 and half == 0 and i == 0,
                                       e == EPG - 1 and half == 1 and i == 1)
                return last

            def put_back(b, t, c, start, stop):
                for i in range(2):
                    last = mm(psum[:, 2 * t + c, :], place[:, b, t * P:(t + 1) * P],
                              y[i][:, b, c * NB:(c + 1) * NB], start=start and i == 0, stop=stop and i == 1)
                return last

            def experts(L):
                n0 = starts[L][2]
                pe.wait_ge(pick_ready, 2 * T * L + T)
                pe.wait_ge(emb_ready, 4 * (L + 1))
                gather(0)
                pe.wait_ge(pick_ready, 2 * T * (L + 1))
                pe.wait_ge(comb_ready, L + 1)
                for b in range(NBLK):
                    for t in range(T):
                        last = mm(psum[:, 3, 4 * b:4 * b + 4], pick[:, t, b * P:(b + 1) * P], comb[:, t, :],
                                  start=t == 0, stop=t == T - 1)
                last.then_inc(cg_in_psum, 1)
                pe.wait_ge(flag_ready, L + 1)
                crowded = pe.value_load(flag[0:1, 0:1], min_val=0, max_val=NG)
                for b in range(NBLK):
                    for t in range(T):
                        c = b % 2 * SEQ + t * P
                        last = nc.tensor.transpose(psum[:, 4 + b // 2, c:c + P], pick[:, t, b * P:(b + 1) * P],
                                                   ident[:, :])
                    if b % 2 or b == NBLK - 1:
                        last.then_inc(place_in_psum, 1)
                pe.wait_ge(cg_ready, L + 1)

                with pe.Fori(0, NG) as g:
                    def take(i, half):
                        k = n0 + 2 * i + half
                        pe.wait_ge(lo_ready, k + 1 + W_SLOTS_GROUP * g)
                        return quarters(k)

                    def pass_wide(i, bank):
                        wide(bank, take(i, 0), 0).then_inc(weights_used, 1)
                        wide(bank, take(i, 1), 1).then_inc(weights_used, 1)

                    def pass_turn(e):
                        pe.wait_ge(h_ready, EPG * (NG * L) + e + 1 + EPG * g)
                        turn_hidden(e).then_inc(ht_in_psum, 1)

                    def pass_down(i, e, half):
                        if half == 0:
                            pe.wait_ge(ht_ready, EPG * NG * L + e + 1 + EPG * g)
                        if e == 0 and half == 0:
                            pe.wait_ge(y_banks_free, 11 * L + 3 + 2 * g)
                        down(e, take(i, half), half).then_inc(weights_used, 1)

                    pe.wait_ge(xg_ready, 10 * L + 2 + 2 * g)
                    pass_wide(0, 0)
                    pass_wide(1, 1)
                    pass_wide(2, 2)
                    pass_turn(0)
                    pass_wide(3, 3)
                    pass_down(4, 0, 0)
                    pass_down(4, 0, 1)
                    pass_wide(5, 0)
                    pass_turn(1)
                    pass_wide(6, 1)
                    pass_down(7, 1, 0)
                    pass_down(7, 1, 1)
                    pass_wide(8, 2)
                    pass_turn(2)
                    pass_wide(9, 3)
                    gather(g + 1)
                    pass_down(10, 2, 0)
                    pass_turn(3)
                    pass_down(10, 2, 1)
                    pass_down(11, 3, 0)
                    pass_down(11, 3, 1)

                pe.wait_ge(xg_ready, 10 * (L + 1))
                def put_back_all(blocks):
                    for t in range(T):
                        for b in range(blocks):
                            if b == NG - 1:
                                pe.wait_ge(y_banks_free, 11 * (L + 1))
                            for c in range(2):
                                last = put_back(b, t, c, b == 0, b == blocks - 1)
                        last.then_inc(ffn_done, 1)

                with pe.If(crowded > 0):
                    o = ov[L]
                    for e in range(EPG):
                        def take(i):
                            k = W_SLOTS_EXPERT * e + i
                            pe.wait_ge(o["split_lo"], k + 1)
                            return (w_hi[:, k % HIGH, :].rearrange("p (j n) -> p j n", j=4),
                                    w_lo[:, k % RING, :].rearrange("p (j n) -> p j n", j=4))

                        if e:
                            pe.wait_ge(o["h"], e)
                        for i in range(2):
                            wide(i, take(2 * i), 0).then_inc(o["used"], 1)
                            wide(i, take(2 * i + 1), 1).then_inc(o["used"], 1)
                        pe.wait_ge(o["h"], e + 1)
                        turn_hidden(e).then_inc(o["ht_in_psum"], 1)
                        pe.wait_ge(o["ht"], e + 1)
                        down(e, take(4), 0).then_inc(o["used"], 1)
                        down(e, take(5), 1).then_inc(o["used"], 1)
                    pe.wait_ge(o["y_saved"], 2)
                    put_back_all(NBLK)
                    pe.wait_ge(o["split_lo"], W_SLOTS_GROUP + 4)
                with pe.Else():
                    put_back_all(NG)

            pe.wait_ge(s_ident, 16)
            transpose_tile(0, 0)
            for L in range(DEPTH):
                (conv_mixer, retention_mixer, sgu_mixer)[L % 3](L)
                if L == 0:
                    pe.wait_ge(s_const, 16 * N_CONST)
                    pe.wait_ge(s_ones, 1)
                route(L)
                experts(L)
                transpose_tile(3 * L + 2, 0)
                turned_tile(3 * L + 2, 0)
                for i in range(4):
                    if i == 3:
                        transpose_tile(3 * L + 2, 1)
                    rows_slot(starts[L][3], 4, tiled(xv), 0, 0, i, ple_done)
                turned_tile(3 * L + 2, 1)
                for i in range(4):
                    if i == 3 and L + 1 < DEPTH:
                        transpose_tile(3 * L + 3, 0)
                    rows_slot(starts[L][3], 4, tiled(xv), 0, 1, i, ple_done)

        @block.scalar
        def _(act):
            split = [0]

            def copy(dst, src, func=ACT.Copy):
                return nc.scalar.activation(dst, src, func)

            def quad(bank):
                return psum[:, bank, :].rearrange("p (j n) -> p j n", j=4)

            def split_slot(n, later=0, arrivals=0):
                act.wait_ge(slot_full[n % RING], 16 * (n // RING + 1) + arrivals)
                if n >= HIGH:
                    act.wait_ge(weights_used, n - HIGH + 1 + later)
                copy(w_hi[:, n % HIGH, :], raw[:, n % RING, :]).then_inc(hi_ready, 1)

            def split_behind(used):
                while split[0] < min(used + HIGH, starts[-1][3] + 4):
                    split_slot(split[0])
                    split[0] += 1

            def save_tile(k, t):
                for q in range(2):
                    act.wait_ge(xt_in_psum, 4 * k + 2 * t + q + 1)
                    copy(xT[0][:, 4 * q:4 * q + 4, t * P:(t + 1) * P], quad(4 + 2 * t + q)).then_inc(xt_hi, 1)

            def save_group(L, q, save):
                n = starts[L][0] + 4 * q
                split_behind(n)
                for b, t in group_jobs(q):
                    wait_block(act, L, b, t, proj_in_psum[L])
                    save(b, t, psum[:, 2 * t + b % 2, :]).then_inc(proj_ready[L], 1)
                    if t:
                        split_behind(n + 2 * (b % 2 + 1))

            def first_group(L, save):
                n = starts[L][0]
                split_behind(n)
                save_tile(3 * L, 1)
                act.wait_ge(pt_in_psum, L + 1)
                copy(pT[0], psum[:, 2, :].rearrange("p (j n) -> p j n", j=2)).then_inc(pt_hi, 1)
                if L % 3 == 2:
                    act.wait_ge(sw_in_psum, 1)
                    copy(sgu_wT, quad(3)).then_inc(sw_ready, 1)
                save_group(L, 0, save)

            def conv_mixer(L):
                n = starts[L][0]

                def save(b, t, bank):
                    b = (b + 2) % 6
                    return copy(bch[:, t, b * NB:(b + 1) * NB], bank)

                first_group(L, save)
                save_group(L, 1, save)
                split_behind(n + 8)
                for k in range(4):
                    act.wait_ge(mt_in_psum[L], k + 1)
                    t, q = divmod(k, 2)
                    copy(zT[:, 4 * q:4 * q + 4, 2 + t * P:2 + (t + 1) * P], quad(4 + k)).then_inc(mt_ready[L], 1)
                act.wait_ge(mt_ready[L], 4)
                act.wait_ge(pad_ready[L], 1)
                if L == 0:
                    act.wait_ge(s_const, 16 * N_CONST)
                for j in range(KD):
                    nc.scalar.activation(conv[:, j, :], zT[:, j, 0:SEQ], ACT.Copy,
                                         scale=conv_w[:, L // 3, 0, j:j + 1]).then_inc(tap_ready[L], 1)
                split_behind(n + 8)
                for b, t in group_jobs(2):
                    wait_block(act, L, b, t, proj_in_psum[L])
                    save(b, t, psum[:, 2 * t + b % 2, :]).then_inc(proj_ready[L], 1)
                    if t:
                        split_behind(n + 10 + b % 2)
                if L == 0:
                    act.wait_ge(s_const, 16 * N_CONST)
                    act.wait_ge(rw_zeroed, 1)
                    copy(rw_pad[:, :, 0:NE], rw[:, :, :]).then_inc(rw_hi_ready, 1)
                for k in range(4):
                    t, q = divmod(k, 2)
                    act.wait_ge(conv_ready[L], k + 1)
                    at = (slice(None), slice(4 * q, 4 * q + 4), bass.ts(t, P))
                    copy(gT[0][at], bT[at]).then_inc(conv_hi[L], 1)

            def retention_mixer(L):
                def save(b, t, bank):
                    if b < 4:
                        dst = qk[:, t, b * NB:(b + 1) * NB]
                    elif b < 8:
                        dst = rv[:, t, (b - 4) * NB:(b - 3) * NB]
                    else:
                        dst = rg[:, t, (b - 8) * NB:(b - 7) * NB]
                    return copy(dst, bank, ACT.Copy if b < 8 else ACT.Sigmoid)

                def save_qkT(src):
                    for k in range(4 * src, 4 * src + 4):
                        t, q = k // 2 % 2, k % 2
                        act.wait_ge(mt_in_psum[L], k + 1)
                        copy(qkT[:, src, 4 * q:4 * q + 4, t * P:(t + 1) * P], quad(4 + k % 4)
                             ).then_inc(mt_ready[L], 1)

                def save_oT(first):
                    for k in range(first, first + 4):
                        h, c = divmod(k, 2)
                        act.wait_ge(oT_in_psum, k + 1)
                        copy(oT[0][:, 4 * h:4 * h + 4, c * P:(c + 1) * P], quad(4 + k % 4)).then_inc(oT_hi, 1)

                n = starts[L][0]
                first_group(L, save)
                save_group(L, 1, save)
                save_group(L, 2, save)
                for b, t in group_jobs(3):
                    split_behind(n + 12)
                    wait_block(act, L, b, t, proj_in_psum[L])
                    save(b, t, psum[:, 2 * t + b % 2, :]).then_inc(proj_ready[L], 1)
                    if (b % 2, t) == (1, 0):
                        save_qkT(0)
                    elif t:
                        split_behind(n + 12 + 2 * (b % 2 + 1))
                save_qkT(1)
                save_group(L, 4, save)
                for b, t in group_jobs(5):
                    split_behind(n + 20)
                    wait_block(act, L, b, t, proj_in_psum[L])
                    save(b, t, psum[:, 2 * t + b % 2, :]).then_inc(proj_ready[L], 1)
                    if (b % 2, t) == (1, 0):
                        save_oT(0)
                    elif t:
                        split_behind(n + 20 + 2 * (b % 2 + 1))
                split_behind(n + 27)
                save_oT(4)
                split_behind(n + 28)

            def sgu_mixer(L):
                def save(b, t, bank):
                    dst = sv if b < 6 else su
                    return copy(dst[:, t, b % 6 * NB:(b % 6 + 1) * NB], bank, ACT.Gelu)

                def save_uvT(m):
                    for k in range(4 * m, 4 * m + 4):
                        s, t = divmod(k, 2)
                        act.wait_ge(mt_in_psum[L], k + 1)
                        copy(uvT[0][:, 4 * s:4 * s + 4, t, :], quad(4 + k % 4)).then_inc(uv_hi, 1)

                n = starts[L][0]
                first_group(L, save)
                for q in range(1, 5):
                    save_group(L, q, save)
                split_behind(n + 20)
                for b, t in group_jobs(5):
                    wait_block(act, L, b, t, proj_in_psum[L])
                    save(b, t, psum[:, 2 * t + b % 2, :]).then_inc(proj_ready[L], 1)
                    if t and b % 2 == 0:
                        split_behind(n + 22)
                save_uvT(0)
                split_behind(n + 24)
                for q in range(2):
                    split_behind(n + 24 + 4 * q + 3)
                    save_uvT(q + 1)
                split_behind(n + 32)

            def save_gather(first):
                for q in range(2):
                    act.wait_ge(xg_in_psum, first + q)
                    copy(xg[0][:, 4 * q:4 * q + 4, :], quad(q)).then_inc(xg_hi, 1)

            def save_embedding(L, t):
                wait_rows(act, L, t, emb_in_psum, L + 1, starts[L][2])
                for c in range(2):
                    copy(emb[:, t, c * NB:(c + 1) * NB], psum[:, 2 * t + c, :]).then_inc(emb_ready, 1)

            def route(L):
                act.wait_ge(logitsT_in_psum, L + 1)
                copy(logitsT, psum[:, 4, 0:SEQ]).then_inc(logitsT_ready, 1)
                act.wait_ge(logits_done, L + 1)
                copy(score[:, :, :], psum[:, 6, 0:T * NE].rearrange("p (t e) -> p t e", t=T), ACT.Sigmoid
                     ).then_inc(score_ready, 1)
                save_embedding(L, 1)
                split_behind(starts[L][2])
                save_gather(10 * L + 1)
                act.wait_ge(cg_in_psum, L + 1)
                copy(cg[:, :], psum[:, 3, 0:4 * NBLK]).then_inc(cg_ready, 1)

            def experts(L):
                n0, s0 = EPG * NG * L, starts[L][2]
                with act.Fori(0, NG) as g:
                    def sigmoid(e):
                        act.wait_ge(weights_used, expert_slots(L, GATE_AT[e]) + W_SLOTS_GROUP * g)
                        copy(hid[:, e % 2, :], psum[:, e % 2 * 2, :], ACT.Sigmoid).then_inc(sig_ready, 1)

                    def save_hT(e):
                        act.wait_ge(ht_in_psum, n0 + e + 1 + EPG * g)
                        copy(hT[0][:, e % 2, :, :], quad(4)).then_inc(ht_hi, 1)

                    for m in range(W_SLOTS_GROUP):
                        if m in (1, 5, 11, 17):
                            sigmoid((1, 5, 11, 17).index(m))
                        if m in (5, 11, 17, 20):
                            save_hT((5, 11, 17, 20).index(m))
                        if m == 23:
                            act.wait_ge(weights_used, expert_slots(L, LAST_AT) + W_SLOTS_GROUP * g)
                            for c in range(2):
                                copy(y[0][:, g, c * NB:(c + 1) * NB], psum[:, 6 + c, :]).then_inc(y_hi, 1)
                        split_slot(s0 + m + HIGH, W_SLOTS_GROUP * g, 16 * (W_SLOTS_GROUP // RING) * g)
                        if m == 19:
                            save_gather(10 * L + 3 + 2 * g)
                split[0] = starts[L][3] + HIGH

                act.wait_ge(flag_ready, L + 1)
                crowded = act.value_load(flag[0:1, 0:1], min_val=0, max_val=NG)
                with act.If(crowded > 0):
                    o = ov[L]
                    for e in range(EPG):
                        act.wait_ge(o["full"], 16 * W_SLOTS_EXPERT * (e + 1))
                        if e == 0:
                            act.wait_ge(lo_ready, starts[L][3] + 4)
                        for k in range(W_SLOTS_EXPERT * e, W_SLOTS_EXPERT * (e + 1)):
                            if k >= HIGH:
                                act.wait_ge(o["used"], k - HIGH + 1)
                            copy(w_hi[:, k % HIGH, :], raw[:, k % RING, :]).then_inc(o["split_hi"], 1)
                        act.wait_ge(o["used"], W_SLOTS_EXPERT * e + 2)
                        copy(hid[:, e % 2, :], psum[:, 0, :], ACT.Sigmoid).then_inc(o["sig"], 1)
                        act.wait_ge(o["ht_in_psum"], e + 1)
                        copy(hT[0][:, e % 2, :, :], quad(4)).then_inc(o["ht_hi"], 1)
                    act.wait_ge(o["used"], W_SLOTS_GROUP)
                    for c in range(2):
                        copy(y[0][:, NG, c * NB:(c + 1) * NB], psum[:, 6 + c, :]).then_inc(o["y_hi"], 1)
                    act.wait_ge(o["full"], 16 * (W_SLOTS_GROUP + 4))
                    for k in range(starts[L][3], starts[L][3] + 4):
                        copy(w_hi[:, k % HIGH, :], raw[:, k % RING, :]).then_inc(o["split_hi"], 1)

            save_tile(0, 0)
            for L in range(DEPTH):
                (conv_mixer, retention_mixer, sgu_mixer)[L % 3](L)
                split_behind(starts[L][1] - 4)
                split_behind(starts[L][1] - 2)
                save_tile(3 * L + 1, 0)
                split_behind(starts[L][1] - 1)
                if L % 3 != 1:
                    copy(table[:, :], ident[:, 0:1], ACT.Sigmoid)
                save_embedding(L, 0)
                split_behind(starts[L][1])
                save_tile(3 * L + 1, 1)
                route(L)
                experts(L)
                for t in range(T):
                    save_tile(3 * L + 2, t)
                for t in range(T):
                    if t:
                        split_behind(starts[L][3] + 3)
                        if L + 1 < DEPTH:
                            save_tile(3 * L + 3, 0)
                    act.wait_ge(ple_arg, 2 * L + t + 1)
                    copy(ple[:, t, :], ple[:, t, :], ACT.Sigmoid).then_inc(ple_sig, 1)

        @block.vector
        def _(dve):
            steps = [0]

            def step(ins):
                steps[0] += 1
                ins.then_inc(dve_step, 1)

            def link(ins, beside=None):
                step(ins)
                done = steps[0]
                if beside is not None:
                    beside()
                dve.wait_ge(dve_step, done)

            tt, ts, stt = nc.vector.tensor_tensor, nc.vector.tensor_scalar, nc.vector.scalar_tensor_tensor
            split = [0]

            def rest(lo, whole, hi):
                return tt(lo, whole, hi.bitcast(F), ALU.subtract)

            def quad(bank):
                return psum[:, bank, :].rearrange("p (j n) -> p j n", j=4)

            def split_slot(n, later=0):
                dve.wait_ge(hi_ready, n + 1 + later)
                rest(w_lo[:, n % RING, :], raw[:, n % RING, :], w_hi[:, n % HIGH, :]).then_inc(lo_ready, 1)

            def split_behind(used):
                while split[0] < min(used + HIGH, starts[-1][3] + 4):
                    split_slot(split[0])
                    split[0] += 1

            def save_tile(k, t):
                for q in range(2):
                    dve.wait_ge(xt_hi, 4 * k + 2 * t + q + 1)
                    at = (slice(None), slice(4 * q, 4 * q + 4), bass.ts(t, P))
                    rest(xT[1][at], quad(4 + 2 * t + q), xT[0][at]).then_inc(xt_ready, 1)

            def residual(t, bank0):
                for c in range(2):
                    xs = x[:, t, c * NB:(c + 1) * NB]
                    step(stt(xs, xs, ALPHA, psum[:, bank0 + 2 * t + c, :], ALU.mult, ALU.add))

            def moments(parts, beside=None):
                m = len(parts)
                mv, var, sq, rstd = nmv[:, 0:m, :], nvar[:, 0:m], nsq[:, 0:m], nrstd[:, 0:m]
                jobs = iter(() if beside is None else [lambda i=i: beside(i) for i in range(2)])
                for i, v in enumerate(parts):
                    step(nc.vector.bn_aggr(nmv[:, i, :], v))
                dve.wait_ge(dve_step, steps[0])
                link(ts(var, mv[:, :, 1], LN_EPS, -0.5, ALU.add, ALU.mult), next(jobs, None))
                link(ts(rstd.bitcast(I32), var.bitcast(I32), -0.5,
                        float(0x5F3759DF - (1 << 22) - (1 << 30)), ALU.mult, ALU.add), next(jobs, None))
                for _ in range(3):
                    if m == 1:
                        link(stt(sq, rstd, var, rstd, ALU.mult, ALU.mult))
                    else:
                        link(tt(sq, rstd, rstd, ALU.mult))
                        link(tt(sq, sq, var, ALU.mult))
                    link(stt(rstd, sq, 1.5, rstd, ALU.add, ALU.mult))
                return [(nmv[:, i, 0:1], nrstd[:, i:i + 1]) for i in range(m)]

            def first_group(L):
                n = starts[L][0]
                split_behind(n)
                save_tile(3 * L, 1)
                dve.wait_ge(pt_hi, L + 1)
                rest(pT[1], psum[:, 2, :].rearrange("p (j n) -> p j n", j=2), pT[0]).then_inc(pt_ready, 1)
                split_behind(n + 4)

            def layer_norm(t, k, banks_read=None):
                ready = steps[0]
                for c in range(2):
                    dve.wait_ge(dve_step, ready - 1 + c)
                    step(nc.vector.bn_stats(stats[:, t, c, :], x[:, t, c * NB:(c + 1) * NB]))
                dve.wait_ge(dve_step, steps[0])
                if banks_read is not None:
                    dve.sem_inc(banks_read, 1)
                dve.wait_ge(lnp_loaded, 32 * (k + 1))

                def subtract_mean(i):
                    cols = slice(i * NB, (i + 1) * NB)
                    step(stt(x[:, t, cols], x[:, t, cols], nmv[:, 0, 0:1], ln_par[:, 0, cols],
                             ALU.subtract, ALU.mult))

                [(_, rstd)] = moments([stats[:, t, 0:2, :]], subtract_mean)
                dve.wait_ge(dve_step, steps[0])
                stt(x[:, t, :], x[:, t, :], rstd, ln_par[:, 1, :], ALU.mult, ALU.add
                    ).then_inc(x_tile_ready, 1)

            def conv_mixer(L):
                n = starts[L][0]
                nc.vector.memset(zT[:, :, 0:2], 0.0).then_inc(pad_ready[L], 1)
                first_group(L)
                split_behind(n + 5)
                for t in range(T):
                    dve.wait_ge(proj_ready[L], 6 + 2 * t)
                    tt(bch[:, t, D:2 * D], bch[:, t, D:2 * D], bch[:, t, 2 * D:3 * D], ALU.mult
                       ).then_inc(z_ready[L], 1)
                    split_behind(n + 7 + t)
                if L == 0:
                    dve.wait_ge(s_const, 16 * N_CONST)
                    dve.wait_ge(s_ident, 16)
                    tt(fold[:, :], ident[:, 0:NE], ident[:, NE:2 * NE], ALU.add)
                    ts(rw_pad[:, :, :], slot_no[:, 0:P].unsqueeze(1).broadcast_to([P, KD, P]), 0.0, None,
                       ALU.mult).then_inc(rw_zeroed, 1)
                base = steps[0]
                for w in (1, 2):
                    for j in range(KD):
                        if w == 1:
                            dve.wait_ge(tap_ready[L], j + 1)
                        else:
                            dve.wait_ge(dve_step, base + j + 1)
                        stt(conv[:, j, :], zT[:, j, w:w + SEQ], conv_w[:, L // 3, w, j:j + 1], conv[:, j, :],
                            ALU.mult, ALU.add).then_inc(dve_step, 1)
                    split_behind(n + 9)
                steps[0] += 2 * KD
                dve.wait_ge(dve_step, steps[0])
                for k in range(4):
                    t, q = divmod(k, 2)
                    at = (slice(None), slice(4 * q, 4 * q + 4), bass.ts(t, P))
                    dve.wait_ge(mt_in_psum[L], 4 + k + 1)
                    tt(bT[at], quad(4 + k), conv[at], ALU.mult).then_inc(conv_ready[L], 1)
                    if k % 2:
                        for q in range(2):
                            dve.wait_ge(conv_hi[L], 2 * t + q + 1)
                            at = (slice(None), slice(4 * q, 4 * q + 4), bass.ts(t, P))
                            rest(gT[1][at], bT[at], gT[0][at]).then_inc(gT_ready[L], 1)
                split_behind(n + 12)
                if L == 0:
                    dve.wait_ge(rw_hi_ready, 1)
                    rest(rw_pad[:, :, NE:2 * NE], rw[:, :, :], rw_pad[:, :, 0:NE]).then_inc(rw_ready, 1)

            def rotary(L, t, step):
                v = qk[:, t, :].rearrange("p (h a n) -> p h a n", h=2 * HEADS, a=2)
                t1, t2 = v[:, :, 0, :], v[:, :, 1, :]
                cos = rot[:, t, 0:1, :].broadcast_to([P, 2 * HEADS, DK // 2])
                sin = rot[:, t, 1:2, :].broadcast_to([P, 2 * HEADS, DK // 2])
                a, b, c = turned
                link((lambda: tt(a, t2, sin, ALU.mult), lambda: tt(b, t1, sin, ALU.mult),
                      lambda: tt(c, t1, cos, ALU.mult), lambda: tt(t1, c, a, ALU.subtract),
                      lambda: tt(c, t2, cos, ALU.mult), lambda: tt(t2, c, b, ALU.add))[step]())
                if step == 5:
                    dve.sem_inc(qk_ready, 1)

            def retention_mixer(L):
                n = starts[L][0]
                first_group(L)
                split_behind(n + 8)
                dve.wait_ge(b_loaded, 32)
                dve.wait_ge(proj_ready[L], 8)
                for i in range(12):
                    rotary(L, i // 6, i % 6)
                    if i >= 8:
                        split_behind(n + 1 + i)
                split_behind(n + 16)

                def silu_of(q, t):
                    for i in range(2):
                        k = 4 * (q - 4) + 2 * t + i
                        dve.wait_ge(proj_ready[L], 17 + k)
                        b = 2 * (q - 4) + i
                        gs = rg[:, t, b * NB:(b + 1) * NB]
                        tt(gs, gs, psum[:, 2 * t + i, :], ALU.mult).then_inc(g_ready, 1)

                def save_rest(k):
                    h, c = divmod(k, 2)
                    dve.wait_ge(oT_hi, k + 1)
                    at = (slice(None), slice(4 * h, 4 * h + 4), bass.ts(c, P))
                    rest(oT[1][at], quad(4 + k % 4), oT[0][at]).then_inc(oT_ready, 1)

                def normalize(first):
                    jobs = range(first, first + 4)
                    for k in jobs:
                        dve.wait_ge(o_in_psum, k + 1)
                        step(nc.vector.bn_stats(nstat[:, k, :], psum[:, 4 + k % 4, :]))
                    dve.wait_ge(dve_step, steps[0])
                    dve.wait_ge(g_ready, first + 4)
                    rows = moments([nstat[:, k, :] for k in jobs])
                    for k, (mean, rstd) in zip(jobs, rows):
                        h, c = divmod(k, 2)
                        gs = rg[:, c, h * DV:(h + 1) * DV]
                        step(stt(gs, psum[:, 4 + k % 4, :], mean, gs, ALU.subtract, ALU.mult))
                    for i, (k, (mean, rstd)) in enumerate(zip(jobs, rows)):
                        h, c = divmod(k, 2)
                        gs = rg[:, c, h * DV:(h + 1) * DV]
                        dve.wait_ge(dve_step, steps[0] - 3 + i)
                        ts(gs, gs, rstd, None, ALU.mult).then_inc(o_ready, 1)

                silu_of(4, 0)
                for h in range(HEADS):
                    dve.wait_ge(score_in_psum, h + 1)
                    bank = psum[:, 4 + h, :]
                    tt(sT[:, h, 0:2 * P], bank[:, 0:2 * P], decay[:, h, :], ALU.mult)
                    tt(sT[:, h, 2 * P:3 * P], bank[:, 2 * P:3 * P], decay[:, h, 0:P], ALU.mult
                       ).then_inc(sT_ready, 1)
                split_behind(n + 19)
                silu_of(4, 1)
                split_behind(n + 20)
                normalize(0)
                silu_of(5, 0)
                for k in range(4):
                    save_rest(k)
                split_behind(n + 23)
                silu_of(5, 1)
                split_behind(n + 24)
                normalize(4)
                split_behind(n + 26)
                for k in range(4, 8):
                    save_rest(k)
                split_behind(n + 28)

            def sgu_mixer(L):
                n = starts[L][0]
                dve.wait_ge(sw_loaded, 16)
                tt(sgu_w, sgu_w, causal[:, :].unsqueeze(1).broadcast_to([P, SGROUPS, P]), ALU.mult
                   ).then_inc(sw_masked, 1)
                first_group(L)
                for q in range(3):
                    for b, t in group_jobs(q):
                        dve.wait_ge(proj_ready[L], 4 * q + 2 * t + b % 2 + 1)
                        link(nc.vector.bn_stats(stats[:, t, b, :], sv[:, t, b * NB:(b + 1) * NB]))
                        if t and q:
                            split_behind(n + 4 * q + 2 * (b % 2 + 1))
                dve.wait_ge(c_loaded, 32)
                for t in range(T):
                    [(mean, rstd)] = moments([stats[:, t, :, :]])
                    for b in range(6):
                        cols = slice(b * NB, (b + 1) * NB)
                        link(stt(sv[:, t, cols], sv[:, t, cols], mean, c_ln[:, 0, cols], ALU.subtract, ALU.mult))
                        stt(sv[:, t, cols], sv[:, t, cols], rstd, c_ln[:, 1, cols], ALU.mult, ALU.add
                            ).then_inc(v_ready, 1)
                        if (t, b) in ((0, 4), (0, 5), (1, 3), (1, 4)):
                            split_behind(n + (9, 14)[t] + b)
                    split_behind(n + (16, 20)[t])
                split_behind(n + 20)

                def gate(m):
                    for k in range(4 * m, 4 * m + 4):
                        b, c = divmod(k, 2)
                        us = su[:, c, b * SVB:(b + 1) * SVB]
                        dve.wait_ge(vs_in_psum, k + 1)
                        stt(us, psum[:, 4 + k % 4, 0:SVB], sgu_b[:, b // 2:b // 2 + 1], us, ALU.add, ALU.mult
                            ).then_inc(uv_ready, 1)

                def save_uvT(m):
                    for k in range(4 * m, 4 * m + 4):
                        s, t = divmod(k, 2)
                        dve.wait_ge(uv_hi, k + 1)
                        at = (slice(None), slice(4 * s, 4 * s + 4), t)
                        rest(uvT[1][at], quad(4 + k % 4), uvT[0][at]).then_inc(mt_ready[L], 1)

                dve.wait_ge(v_ready, 12)
                dve.wait_ge(proj_ready[L], 20)
                gate(0)
                gate(1)
                split_behind(n + 22)
                save_uvT(0)
                split_behind(n + 24)
                dve.wait_ge(proj_ready[L], 24)
                for q in range(2):
                    gate(q + 2)
                    split_behind(n + 24 + 4 * q + 2)
                    save_uvT(q + 1)
                    split_behind(n + 24 + 4 * q + 4)

            def route(L):
                TG = T * NG
                lower = small[:, 0:16].rearrange("p (i j) -> p i j", i=4)
                group_base, group_number = small[:, 16:20], small[:, 20:24]
                dve.wait_ge(score_ready, L + 1)
                link(tt(sel[:, :, :], score[:, :, :], rb[:, :].unsqueeze(1).broadcast_to([P, T, NE]), ALU.add))

                def ahead(v, n, out):
                    other = v.unsqueeze(2).broadcast_to([P, n, 4, 4])
                    own = v.unsqueeze(3).broadcast_to([P, n, 4, 4])
                    low = lower.unsqueeze(1).broadcast_to([P, n, 4, 4])
                    link(tt(cmp2[:, 0:n], other, own, ALU.is_equal),
                         lambda: step(tt(cmp1[:, 0:n], other, own, ALU.is_gt)))
                    link(tt(cmp2[:, 0:n], cmp2[:, 0:n], low, ALU.mult))
                    link(tt(cmp1[:, 0:n], cmp1[:, 0:n], cmp2[:, 0:n], ALU.add))
                    link(nc.vector.tensor_reduce(out, cmp1[:, 0:n], X, ALU.add))

                s8 = sel[:, :, :].rearrange("p t (g e) -> p (t g) e", g=NG)
                best = cw[:, :, :, :].rearrange("p t g e -> p (t g) e")
                ahead(s8, TG, cnt[:, :])
                link(stt(best, cnt[:, :, :], 1.5, s8, ALU.is_lt, ALU.mult))
                link(nc.vector.tensor_reduce(gscore[:, :, :], cw[:, :, :, :], X, ALU.add))
                ahead(gscore[:, :, :], T, gcnt[:, :])
                ts(ghot[:, :, :], gcnt[:, :, :], 0.5, None, ALU.is_lt).then_inc(ghot_ready, 1)
                dve.wait_ge(ghot_ready, L + 1)
                link(tt(gpos[:, :, :], ghot[:, :, :], group_base.unsqueeze(1).broadcast_to([P, T, NG]), ALU.mult))
                link(nc.vector.tensor_reduce(gbase[:, :], gpos[:, :, :], X, ALU.add))
                link(ts(full[:, :], gbase[:, :], P - 0.5, None, ALU.add),
                     lambda: step(ts(shift[:, :], gbase[:, :], -1.0, float((NG - 1) * P), ALU.mult, ALU.add)))
                dve.wait_ge(rank_in_psum, 2 * L + 1)
                link(tt(gpos[:, :, :], ghot[:, :, :], psum[:, 5, 0:8].rearrange("p (t g) -> p t g", t=T), ALU.mult))
                link(nc.vector.tensor_reduce(key[:, :], gpos[:, :, :], X, ALU.add))
                for t in range(T):
                    at = slice(t, t + 1)
                    step(stt(over[:, at], key[:, at], full[:, at], shift[:, at], ALU.is_gt, ALU.mult))
                dve.wait_ge(dve_step, steps[0])
                for part in (slice(0, P), slice(P, NBLK * P)):
                    for t in range(T):
                        at = slice(t, t + 1)
                        ts(pick[:, t, part], slot_no[:, part], over[:, at], key[:, at], ALU.subtract,
                           ALU.is_equal).then_inc(pick_ready, 1)
                link(stt(best, cnt[:, :, :], 1.5, score[:, :, :].rearrange("p t (g e) -> p (t g) e", g=NG),
                         ALU.is_lt, ALU.mult))
                link(tt(cw[:, :, :, :], cw[:, :, :, :],
                        ghot[:, :, :].unsqueeze(3).broadcast_to([P, T, NG, 4]), ALU.mult))
                link(nc.vector.tensor_reduce(comb[:, :, :], cw[:, :, :, :].rearrange("p t g e -> p t e g"),
                                             X, ALU.add))
                link(nc.vector.tensor_reduce(den[:, :], comb[:, :, :], X, ALU.add))
                link(nc.vector.reciprocal(den[:, :], den[:, :]))
                tt(comb[:, :, :], comb[:, :, :], den[:, :].unsqueeze(2).broadcast_to([P, T, 4]), ALU.mult
                   ).then_inc(comb_ready, 1)
                dve.wait_ge(rank_in_psum, 2 * (L + 1))
                link(ts(big[:, :], psum[:, 7, 0:4], P + 0.5, None, ALU.is_gt))
                link(tt(big[:, :], big[:, :], group_number, ALU.mult))
                link(nc.vector.tensor_reduce(bigmax[:, :], big[:, :], X, ALU.max))
                nc.vector.tensor_copy(flag[:, :], bigmax[:, :]).then_inc(flag_ready, 1)
                split_behind(starts[L][1] - 1)

            def save_gather(first):
                for q in range(2):
                    dve.wait_ge(xg_hi, first + q)
                    at = (slice(None), slice(4 * q, 4 * q + 4))
                    rest(xg[1][at], quad(q), xg[0][at]).then_inc(xg_ready, 1)

            def experts(L):
                n0, s0 = EPG * NG * L, starts[L][2]
                save_gather(10 * L + 1)
                for k in range(3):
                    dve.wait_ge(place_in_psum, 3 * L + k + 1)
                    n = 2 if k < 2 else 1
                    nc.vector.tensor_copy(place[:, 2 * k:2 * k + n, :],
                                          psum[:, 4 + k, 0:n * SEQ].rearrange("p (b n) -> p b n", b=n)
                                          ).then_inc(y_banks_free, 1)
                split_behind(starts[L][2])
                dve.wait_ge(cg_ready, L + 1)
                with dve.Fori(0, NG) as g:
                    def hidden(e):
                        k = n0 + e + 1 + EPG * g
                        s = hid[:, e % 2, :]
                        dve.wait_ge(sig_ready, k)
                        tt(s, s, psum[:, e % 2 * 2, :], ALU.mult).then_inc(silu_ready, 1)
                        dve.wait_ge(silu_ready, k)
                        dve.wait_ge(weights_used, expert_slots(L, UP_AT[e]) + W_SLOTS_GROUP * g)
                        stt(s, psum[:, e % 2 * 2 + 1, :], cg[:, bass.ds(4 * g + e, 1)], s,
                            ALU.mult, ALU.mult).then_inc(h_ready, 1)

                    def save_hT(e):
                        dve.wait_ge(ht_hi, n0 + e + 1 + EPG * g)
                        rest(hT[1][:, e % 2, :, :], quad(4), hT[0][:, e % 2, :, :]).then_inc(ht_ready, 1)

                    for m in range(W_SLOTS_GROUP):
                        if m in (3, 7, 13, 19):
                            hidden((3, 7, 13, 19).index(m))
                        if m in (5, 11, 17, 20):
                            save_hT((5, 11, 17, 20).index(m))
                        if m == 23:
                            for c in range(2):
                                cols = slice(c * NB, (c + 1) * NB)
                                dve.wait_ge(y_hi, 2 * NG * L + c + 1 + 2 * g)
                                rest(y[1][:, g, cols], psum[:, 6 + c, :], y[0][:, g, cols]
                                     ).then_inc(y_banks_free, 1)
                        split_slot(s0 + m + HIGH, W_SLOTS_GROUP * g)
                        if m == 19:
                            save_gather(10 * L + 3 + 2 * g)
                split[0] = starts[L][3] + HIGH
                dve.wait_ge(flag_ready, L + 1)
                crowded = dve.value_load(flag[0:1, 0:1], min_val=0, max_val=NG)
                with dve.If(crowded > 0):
                    o = ov[L]
                    for e in range(EPG):
                        for k in range(W_SLOTS_EXPERT * e, W_SLOTS_EXPERT * (e + 1)):
                            dve.wait_ge(o["split_hi"], k + 1)
                            rest(w_lo[:, k % RING, :], raw[:, k % RING, :], w_hi[:, k % HIGH, :]
                                 ).then_inc(o["split_lo"], 1)
                        s = hid[:, e % 2, :]
                        dve.wait_ge(o["sig"], e + 1)
                        tt(s, s, psum[:, 0, :], ALU.mult).then_inc(o["silu"], 1)
                        dve.wait_ge(o["silu"], e + 1)
                        dve.wait_ge(o["used"], W_SLOTS_EXPERT * e + 4)
                        stt(s, psum[:, 1, :], cg[:, 4 * NG + e:4 * NG + e + 1], s,
                            ALU.mult, ALU.mult).then_inc(o["h"], 1)
                        dve.wait_ge(o["ht_hi"], e + 1)
                        rest(hT[1][:, e % 2, :, :], quad(4), hT[0][:, e % 2, :, :]).then_inc(o["ht"], 1)
                    for c in range(2):
                        cols = slice(c * NB, (c + 1) * NB)
                        dve.wait_ge(o["y_hi"], c + 1)
                        rest(y[1][:, NG, cols], psum[:, 6 + c, :], y[0][:, NG, cols]).then_inc(o["y_saved"], 1)
                    for i, k in enumerate(range(starts[L][3], starts[L][3] + 4)):
                        dve.wait_ge(o["split_hi"], W_SLOTS_GROUP + i + 1)
                        rest(w_lo[:, k % RING, :], raw[:, k % RING, :], w_hi[:, k % HIGH, :]
                             ).then_inc(o["split_lo"], 1)

            save_tile(0, 0)
            for L in range(DEPTH):
                (conv_mixer, retention_mixer, sgu_mixer)[L % 3](L)
                end = starts[L][1]
                split_behind(end - 4)
                wait_rows(dve, L, 0, mix_done, L + 1, end)
                residual(0, 0)
                layer_norm(0, 2 * L)
                split_behind(end - 3)
                save_tile(3 * L + 1, 0)
                wait_rows(dve, L, 1, mix_done, L + 1, end)
                residual(1, 0)
                layer_norm(1, 2 * L, mix_read)
                save_tile(3 * L + 1, 1)
                split_behind(end - 2)
                route(L)
                experts(L)
                dve.wait_ge(ffn_done, T * L + 1)
                residual(0, 0)
                layer_norm(0, 2 * L + 1)
                dve.wait_ge(ffn_done, T * L + 2)
                residual(1, 0)
                save_tile(3 * L + 2, 0)
                layer_norm(1, 2 * L + 1)
                save_tile(3 * L + 2, 1)
                n_gate = starts[L][3]
                dve.wait_ge(bg_loaded, 16 * (L + 1))
                for t in range(T):
                    if t and L + 1 < DEPTH:
                        save_tile(3 * L + 3, 0)
                    wait_rows(dve, L, t, ple_done, L + 1, n_gate + 4)
                    for c in range(2):
                        cols = slice(c * NB, (c + 1) * NB)
                        link(tt(ple[:, t, cols], psum[:, 2 * t + c, :], bgate[:, cols], ALU.add))
                    dve.sem_inc(ple_arg, 1)
                    if t:
                        split_behind(n_gate + 3)
                    dve.wait_ge(ple_sig, 2 * L + t + 1)
                    link(tt(ple[:, t, :], ple[:, t, :], emb[:, t, :], ALU.mult))
                    tt(x[:, t, :], x[:, t, :], ple[:, t, :], ALU.add).then_inc(x_tile_ready, 1)
                    if t == 0:
                        split_behind(n_gate + 2)
                split_behind(n_gate + 4)


def kernel(**inputs):
    import concourse.bacc as bacc
    from concourse.bass_utils import run_bass_kernel_spmd

    nc = bacc.Bacc("TRN2", target_bir_lowering=False, num_devices=1)
    arrays = {n: np.ascontiguousarray(a) for n, a in inputs.items()}
    arrays.update(shape_constants())
    aps, feed = {}, {}
    for name, a in arrays.items():
        feed[f"in_{name}"] = a
        aps[name] = nc.dram_tensor(f"in_{name}", a.shape, mybir.dt.from_np(a.dtype), kind="ExternalInput").ap()
    out = nc.dram_tensor("out", (1, SEQ, D), mybir.dt.float32, kind="ExternalOutput").ap()
    build(nc, aps, out)
    r = run_bass_kernel_spmd(nc, [feed], core_ids=[0])
    return r.results[0]["out"]
```
